# Optimizing a Trainium2 kernel written in Bass

```python
import jax, jax.numpy as jnp
from jax import lax
import numpy as np

D_MODEL = 1024
BATCH = 1
SEQ = 1024
DEPTH = 1

N_META = 16
WINDOW = 128
BLOCK = 128
PREFIX = BLOCK
PAD_FRONT = PREFIX - N_META
ATT_HEADS = 8
ATT_KV_HEADS = 2
ATT_HEAD_DIM = 64
ATT_GROUP = ATT_HEADS // ATT_KV_HEADS
ATT_Q = ATT_HEADS * ATT_HEAD_DIM
ATT_KV = ATT_KV_HEADS * ATT_HEAD_DIM
DN_HEADS = 4
DN_HEAD_DIM = 128
DN_W = DN_HEADS * DN_HEAD_DIM
DN_CHUNK = 64
CONV_WIDTH = 4
D_FF = -(-8 * D_MODEL // (3 * 256)) * 256
RMS_EPS = 1e-6
IN_SIZES = (ATT_Q, ATT_KV, ATT_KV, DN_W, DN_W, DN_W, DN_W, DN_HEADS, DN_HEADS, D_MODEL, D_MODEL)
IN_WIDTH = ATT_Q + 2 * ATT_KV + 4 * DN_W + 2 * DN_HEADS + 2 * D_MODEL

kernel_name = "hybrid_swa_sink_gated_deltanet_parallel"

def rmsnorm(x, w):
    xf = x.astype(jnp.float32)
    y = xf * lax.rsqrt(jnp.mean(xf * xf, axis=-1, keepdims=True) + RMS_EPS)
    return (y * w.astype(jnp.float32)).astype(x.dtype)

def l2norm(x):
    xf = x.astype(jnp.float32)
    return xf * lax.rsqrt(jnp.sum(xf * xf, axis=-1, keepdims=True) + RMS_EPS)

def sliding_window_attention(q, k, v, sinks):
    B, L = q.shape[:2]
    nb = L // BLOCK
    f32 = jnp.float32
    qb = q.astype(f32).reshape(B, nb, BLOCK, ATT_KV_HEADS, ATT_GROUP, ATT_HEAD_DIM) * (ATT_HEAD_DIM ** -0.5)

    def keys_for_blocks(t):
        t = t.astype(f32)
        tb = t.reshape(B, nb, BLOCK, ATT_KV_HEADS, ATT_HEAD_DIM)
        prev = jnp.concatenate([jnp.zeros_like(tb[:, :1]), tb[:, :-1]], axis=1)
        meta = jnp.broadcast_to(t[:, None, PAD_FRONT:PREFIX], (B, nb, N_META, ATT_KV_HEADS, ATT_HEAD_DIM))
        return jnp.concatenate([meta, prev, tb], axis=2)

    kk = keys_for_blocks(k)
    vv = keys_for_blocks(v)
    s = jnp.einsum('bnqhgd,bnkhd->bhgnqk', qb, kk)

    blk = jnp.arange(nb)[:, None]
    q_pos = blk * BLOCK + jnp.arange(BLOCK)[None, :]
    band_pos = (blk - 1) * BLOCK + jnp.arange(2 * BLOCK)[None, :]
    meta_pos = PAD_FRONT + jnp.arange(N_META)
    diff = q_pos[:, :, None] - band_pos[:, None, :]
    band_ok = (diff >= 0) & (diff < WINDOW) & (band_pos[:, None, :] >= PREFIX)
    meta_ok = jnp.broadcast_to(meta_pos[None, None, :] <= q_pos[:, :, None], (nb, BLOCK, N_META))
    mask = jnp.concatenate([meta_ok, band_ok], axis=-1)
    s = jnp.where(mask, s, -jnp.inf)

    sink = sinks.astype(f32).reshape(ATT_KV_HEADS, ATT_GROUP)[None, :, :, None, None, None]
    m = jnp.maximum(jnp.max(s, axis=-1, keepdims=True), sink)
    p = jnp.exp(s - m)
    probs = p / (jnp.sum(p, axis=-1, keepdims=True) + jnp.exp(sink - m))
    o = jnp.einsum('bhgnqk,bnkhd->bnqhgd', probs, vv)
    return o.reshape(B, L, ATT_Q).astype(q.dtype)

def causal_depthwise_conv(x, w):
    C = x.shape[-1]
    return lax.conv_general_dilated(
        x, w[:, None, :].astype(x.dtype), window_strides=(1,), padding=[(CONV_WIDTH - 1, 0)],
        dimension_numbers=('NWC', 'WIO', 'NWC'), feature_group_count=C)

def gated_delta_rule(q, k, v, g, beta):
    f32 = jnp.float32
    B, L, H, dk = q.shape
    dv = v.shape[-1]
    nc = L // DN_CHUNK
    C = DN_CHUNK

    def chunk(t):
        t = t.astype(f32).reshape((B, nc, C, H) + t.shape[3:])
        return jnp.moveaxis(t, 3, 1)

    q = chunk(q) * (dk ** -0.5)
    k = chunk(k)
    v = chunk(v)
    g = chunk(g)
    beta = chunk(beta)
    gcum = jnp.cumsum(g, axis=-1)
    tril = jnp.tril(jnp.ones((C, C), dtype=bool))
    strict = jnp.tril(jnp.ones((C, C), dtype=bool), -1)
    decay = jnp.exp(jnp.where(tril, gcum[..., :, None] - gcum[..., None, :], -jnp.inf))
    k_beta = k * beta[..., None]
    a = jnp.where(strict, jnp.einsum('bhncd,bhnsd->bhncs', k_beta, k) * decay, 0.0)
    lhs = a + jnp.eye(C, dtype=f32)
    w = lax.linalg.triangular_solve(lhs, k_beta * jnp.exp(gcum)[..., None],
                                    left_side=True, lower=True, unit_diagonal=True)
    u = lax.linalg.triangular_solve(lhs, v * beta[..., None],
                                    left_side=True, lower=True, unit_diagonal=True)
    attn = jnp.einsum('bhncd,bhnsd->bhncs', q, k) * decay
    q_dec = q * jnp.exp(gcum)[..., None]
    g_last = gcum[..., -1]
    k_dec = k * jnp.exp(g_last[..., None] - gcum)[..., None]

    def step(S, xs):
        q_i, k_i, u_i, w_i, attn_i, gl_i = xs
        v_new = u_i - jnp.einsum('bhcd,bhde->bhce', w_i, S)
        o_i = jnp.einsum('bhcd,bhde->bhce', q_i, S) + jnp.einsum('bhcs,bhse->bhce', attn_i, v_new)
        S = S * jnp.exp(gl_i)[..., None, None] + jnp.einsum('bhcd,bhce->bhde', k_i, v_new)
        return S, o_i

    xs = (jnp.moveaxis(q_dec, 2, 0), jnp.moveaxis(k_dec, 2, 0), jnp.moveaxis(u, 2, 0),
          jnp.moveaxis(w, 2, 0), jnp.moveaxis(attn, 2, 0), jnp.moveaxis(g_last, 2, 0))
    S0 = jnp.zeros((B, H, dk, dv), f32)
    _, o = lax.scan(step, S0, xs)
    return jnp.transpose(o, (1, 0, 3, 2, 4)).reshape(B, L, H, dv)

def hybrid_layer(x, valid, w_in, b_in, conv_w, a_log, dt_bias, dn_norm_w, att_sinks,
                 w_att_out, w_dn_out, w_out, norm_mix_pre, norm_mix_post,
                 norm_ffn_pre, norm_ffn_post, w_ffn_in, w_ffn_out):
    B, L, _ = x.shape
    f32 = jnp.float32
    h = rmsnorm(x, norm_mix_pre)
    proj = (h @ w_in + b_in) * valid
    splits = np.cumsum(IN_SIZES)[:-1].tolist()
    aq, ak, av, dq, dk, dv, dz, da, db, ga, gb = jnp.split(proj, splits, axis=-1)

    y_att = sliding_window_attention(aq.reshape(B, L, ATT_HEADS, ATT_HEAD_DIM),
                                     ak.reshape(B, L, ATT_KV_HEADS, ATT_HEAD_DIM),
                                     av.reshape(B, L, ATT_KV_HEADS, ATT_HEAD_DIM), att_sinks)

    qkv = jax.nn.silu(causal_depthwise_conv(jnp.concatenate([dq, dk, dv], axis=-1), conv_w))
    cq, ck, cv = jnp.split(qkv, 3, axis=-1)
    q = l2norm(cq.reshape(B, L, DN_HEADS, DN_HEAD_DIM))
    k = l2norm(ck.reshape(B, L, DN_HEADS, DN_HEAD_DIM))
    v = cv.reshape(B, L, DN_HEADS, DN_HEAD_DIM).astype(f32)
    g = -jnp.exp(a_log.astype(f32)) * jax.nn.softplus(da.astype(f32) + dt_bias.astype(f32))
    beta = jax.nn.sigmoid(db.astype(f32))
    o = gated_delta_rule(q, k, v, g, beta)
    o = rmsnorm(o, dn_norm_w) * jax.nn.silu(dz.reshape(B, L, DN_HEADS, DN_HEAD_DIM).astype(f32))
    y_dn = o.reshape(B, L, DN_W).astype(x.dtype)

    merged = jax.nn.sigmoid(ga) * (y_att @ w_att_out) + jax.nn.sigmoid(gb) * (y_dn @ w_dn_out)
    x = x + valid * rmsnorm(merged @ w_out, norm_mix_post)

    hf = rmsnorm(x, norm_ffn_pre)
    gate, up = jnp.split(hf @ w_ffn_in, 2, axis=-1)
    x = x + valid * rmsnorm((jax.nn.silu(gate) * up) @ w_ffn_out, norm_ffn_post)
    return x

def setup_inputs(seed: int = 0) -> dict:
    key = jax.random.key(seed)
    ks = jax.random.split(key, 20)
    f32 = jnp.float32
    nrm = lambda k, shape, scale: jax.random.normal(k, shape, f32) * scale
    gain = lambda k, shape: 1.0 + 0.02 * jax.random.normal(k, shape, f32)
    dt = jnp.exp(jax.random.uniform(ks[5], (DEPTH, DN_HEADS), f32, jnp.log(1e-3), jnp.log(1e-1)))
    return {
        "x": nrm(ks[0], (BATCH, SEQ, D_MODEL), 1.0),
        "meta_tokens": nrm(ks[1], (N_META, D_MODEL), 1.0),
        "w_in": nrm(ks[2], (DEPTH, D_MODEL, IN_WIDTH), D_MODEL ** -0.5),
        "b_in": nrm(ks[3], (DEPTH, IN_WIDTH), 0.02),
        "conv_w": nrm(ks[4], (DEPTH, CONV_WIDTH, 3 * DN_W), CONV_WIDTH ** -0.5),
        "a_log": jnp.log(jax.random.uniform(ks[6], (DEPTH, DN_HEADS), f32, 1.0, 16.0)),
        "dt_bias": dt + jnp.log(-jnp.expm1(-dt)),
        "dn_norm_w": gain(ks[7], (DEPTH, DN_HEAD_DIM)),
        "att_sinks": nrm(ks[8], (DEPTH, ATT_HEADS), 1.0),
        "w_att_out": nrm(ks[9], (DEPTH, ATT_Q, D_MODEL), ATT_Q ** -0.5),
        "w_dn_out": nrm(ks[10], (DEPTH, DN_W, D_MODEL), DN_W ** -0.5),
        "w_out": nrm(ks[11], (DEPTH, D_MODEL, D_MODEL), D_MODEL ** -0.5),
        "norm_mix_pre": gain(ks[12], (DEPTH, D_MODEL)),
        "norm_mix_post": gain(ks[13], (DEPTH, D_MODEL)),
        "norm_ffn_pre": gain(ks[14], (DEPTH, D_MODEL)),
        "norm_ffn_post": gain(ks[15], (DEPTH, D_MODEL)),
        "w_ffn_in": nrm(ks[16], (DEPTH, D_MODEL, 2 * D_FF), D_MODEL ** -0.5),
        "w_ffn_out": nrm(ks[17], (DEPTH, D_FF, D_MODEL), D_FF ** -0.5),
    }

def reference(x, meta_tokens, w_in, b_in, conv_w, a_log, dt_bias, dn_norm_w, att_sinks,
              w_att_out, w_dn_out, w_out, norm_mix_pre, norm_mix_post, norm_ffn_pre,
              norm_ffn_post, w_ffn_in, w_ffn_out):
    B = x.shape[0]
    pads = jnp.zeros((B, PAD_FRONT, D_MODEL), x.dtype)
    meta = jnp.broadcast_to(meta_tokens.astype(x.dtype)[None], (B, N_META, D_MODEL))
    h = jnp.concatenate([pads, meta, x], axis=1)
    L = h.shape[1]
    valid = (jnp.arange(L) >= PAD_FRONT).astype(x.dtype)[None, :, None]
    for l in range(DEPTH):
        h = hybrid_layer(h, valid, w_in[l], b_in[l], conv_w[l], a_log[l], dt_bias[l], dn_norm_w[l],
                         att_sinks[l], w_att_out[l], w_dn_out[l], w_out[l], norm_mix_pre[l],
                         norm_mix_post[l], norm_ffn_pre[l], norm_ffn_post[l], w_ffn_in[l], w_ffn_out[l])
    return h[:, PREFIX:]


_drawn_inputs = setup_inputs


def setup_inputs(seed=0):
    import zlib

    import numpy as np

    out = dict(_drawn_inputs(seed))
    spreads = {}
    factors = {'dn_norm_w': 3.496,
     'att_sinks': 8.0,
     'norm_mix_post': 3.344,
     'norm_ffn_pre': 3.471,
     'norm_ffn_post': 4.973}
    for name, (base, spread) in spreads.items():
        noise = np.random.default_rng([zlib.crc32(name.encode()), seed]).standard_normal(out[name].shape)
        drawn = base * np.exp(spread * noise) if base else spread * noise
        out[name] = __import__('jax').numpy.asarray(drawn.astype(out[name].dtype))
    for name, factor in factors.items():
        out[name] = (out[name] * factor).astype(out[name].dtype)
    return out
```

```python
import concourse.bass as bass
from concourse import mybir
import numpy as np

F32 = mybir.dt.float32
F32R = mybir.dt.float32r
ACT = mybir.ActivationFunctionType
ALU = mybir.AluOpType
AX = mybir.AxisListType

P = 128
D = 1024
KT = D // P
TOK = 1024
NT = TOK // P
META = 16
LW = META + TOK
HALF = 512
FF = 2816
EPS = 1e-6
NEG = -1.0e30
DH = 4
HD = 64
GRP = 4
Q0, K0, V0, DN0, DZ0, DAB0, G0 = 0, 512, 640, 768, 2304, 2816, 2824

N_KV, N_Q, N_DN, N_DZ, N_G, N_MERGE, N_OUT, N_FF = 0, 2, 6, 18, 22, 38, 46, 54
FF_GROUPS = [8, 8, 6]
R_BIAS, R_BG, R_PRE, R_POST, R_FPRE, R_FPOST, R_DNW, R_CONV = 0, 22, 38, 46, 54, 62, 70, 71
NROWS = R_CONV + 48

DELTA_OPS = [("ssq", 0), ("gam", 1), ("KK", 2), ("KQ", 0), ("vT", 1), ("kT", 2), ("DnT", 0), ("D2", 1), ("D2T", 2),
             ("D4", 0), ("D4T", 1), ("M2", 2), ("D8", 0), ("M3", 1), ("M4", 2), ("Ninv", 0), ("B", 1), ("BT", 2),
             ("B2", 0), ("B2T", 1), ("W2", 2), ("B4", 0), ("W3", 1), ("TT", 2), ("KS", 0), ("VN", 1), ("dS", 2),
             ("P1", 0), ("P2", 1), ("oT", 2)]
META_SKIP = {"KQ", "Ninv", "B", "BT", "B2", "B2T", "B4", "W2", "W3", "TT", "KS", "P1", "P2", "oT"}
ATT_OPS = ["S00", "S01", "O0", "S10", "S11", "O1"]


def lane_of(op):
    return dict(DELTA_OPS)[op]


def filled(op, c):
    lane = lane_of(op)
    everyone = [o for o, l in DELTA_OPS if l == lane]
    first = [o for o in everyone if o not in META_SKIP]
    if isinstance(c, int) and c == 0:
        return first.index(op) + 1
    return (c - 1) * len(everyone) + (len(first) + everyone.index(op) + 1)


def att_filled(op, c):
    return (c - 1) * len(ATT_OPS) + (ATT_OPS.index(op) + 2)


def build(nc, x, meta, w_in, b_in, conv_w, a_log, dt_bias, dn_norm_w, att_sinks, w_att, w_dn, w_out,
          n_pre, n_post, f_pre, f_post, w_fi, w_fo, out):
    qkv_d = nc.dram_tensor("qkv_scratch", [12, P, LW], F32, kind="Internal").ap()
    gate_d = nc.dram_tensor("gate_scratch", [16, P, TOK], F32, kind="Internal").ap()
    x2_d = nc.dram_tensor("x2_scratch", [8, P, TOK], F32, kind="Internal").ap()

    top = [(nc.sbuf_base + 31) // 32 * 32]

    def at(name, shape, dt, offset):
        t = nc.alloc_sbuf_tensor_at(name, shape, dt, offset=offset)
        return t

    def keep(name, shape, dt=F32):
        size = 4 * int(np.prod(shape[1:]))
        t = at(name, shape, dt, top[0])
        top[0] += (size + 31) // 32 * 32
        return t

    def region(start, size):
        cur = [start]

        def take(name, shape, dt=F32):
            n = 4 * int(np.prod(shape[1:]))
            t = at(name, shape, dt, cur[0])
            cur[0] += (n + 31) // 32 * 32
            assert cur[0] <= start + size, (name, cur[0] - start, size)
            return t
        return take

    raw = keep("w_raw", [P, 2, KT, P])
    whi = keep("w_hi", [P, 2, KT, P], F32R)
    wlo = keep("w_lo", [P, 2, KT, P], F32R)
    ident = keep("ident", [P, P])
    upper = keep("upper_ones", [P, P])
    ones = keep("ones", [P, P])
    mask_up = keep("mask_up", [P, P])
    mask_low = keep("mask_low", [P, P])
    blocks16 = keep("blocks16", [P, P])
    band = keep("band", [P, META + 2 * P])
    band_now = keep("band_now", [P, META + 2 * P])
    params = keep("params", [P, P])
    wd_raw = keep("wd_raw", [P, KT, 8])
    wd_hi = keep("wd_hi", [P, KT, 8], F32R)
    wd_lo = keep("wd_lo", [P, KT, 8], F32R)
    dab_b = keep("dab_bias", [P, 8])
    dtb = keep("dt_bias_bc", [P, 4])
    alog = keep("a_log_bc", [P, 4])
    sink = keep("sink_bc", [P, 8])
    half = keep("minus_half", [P, 1])
    cols = keep("cols", [P, NT + 1, 24])
    tiny = keep("tiny", [P, 96])
    small = keep("small", [P, 64])
    dabx = keep("dab", [P, NT + 1, 8])
    dabe = keep("dab_exp", [P, NT + 1, 8])
    R0 = top[0]
    R1 = R0 + 2 * KT * LW * 4
    R2 = R1 + 65536
    R3 = R2 + 32768
    end = nc.sbuf_usable_end
    assert end - R3 >= 12288, (end, R3, end - R3)

    take = region(R0, R1 - R0)
    h_hi = take("h_hi", [P, KT, LW], F32R)
    h_lo = take("h_lo", [P, KT, LW], F32R)
    take = region(R1, R2 - R1)
    aq = take("att_q", [P, GRP, TOK])
    ak = take("att_k", [P, P + TOK])
    av = take("att_v", [P, P + TOK])
    vtok = take("att_v_tokens", [P, NT + 1, P])
    gz = take("dn_gate", [P, DH, TOK])
    kwin = take("k_window", [P, META + 2 * P])
    qblk = take("q_block", [P, GRP, P])
    vwin = take("v_window", [P, 2, P])
    vmeta = take("v_meta", [META, P])
    prob = take("prob", [P, 2, 2, META + 2 * P])
    pt = take("prob_T", [P, 3, GRP * P])
    take = region(R2, R3 - R2)
    xin = take("x_in", [P, 2, D])
    xn = take("x_norm", [P, 2, D])
    xw = take("x_weighted", [P, 1, D])
    prow = take("param_rows", [P, P])
    take = region(R2, R3 - R2)
    rawc = take("conv_in", [P, 2, 3 + LW])
    cv = take("conv_sum", [P, 2, LW])
    cs = take("stored", [P, 2, LW])
    take = region(R0, R1 - R0)
    qkv = take("qkv", [P, 2, 12, P])
    sq = take("qk_squares", [P, 8, P])
    names = ["X1", "X2", "X3", "X4", "X5", "X6", "X7", "X8", "En", "Ninv", "TT", "t1", "DT", "DL", "attT", "vb",
             "kd", "Z", "vn", "o1", "op", "osq", "on", "S"]
    buf = {k: take("b_" + k, [P, DH, P]) for k in names}
    where = dict(Dn="X1", B="X1", DnT="X2", BT="X2", D2="X3", D8="X3", B2="X3", D2T="X4", B2T="X4", D4="X5",
                 B4="X5", D4T="X6", M1="X7", M3="X7", W1="X7", W3="X7", M2="X8", M4="X8", W2="X8")
    for k, v in where.items():
        buf[k] = buf[v]
    take = region(R2, R3 - R2)
    ya = take("y_att", [P, GRP, TOK])
    yd = take("y_dn", [P, DH, TOK])
    take = region(R0, R1 - R0)
    y_hi = take("y_hi", [P, KT, TOK], F32R)
    y_lo = take("y_lo", [P, KT, TOK], F32R)
    take = region(R1, R2 - R1)
    m_hi = take("m_hi", [P, KT, TOK], F32R)
    m_lo = take("m_lo", [P, KT, TOK], F32R)
    take = region(R2, R3 - R2)
    gin = take("gates_in", [P, 2, 2, TOK])
    mt = take("merge_parts", [P, 2, TOK])
    take = region(R2, R3 - R2)
    oT = take("o_T", [P, KT, TOK])
    take = region(R3, end - R3)
    sqt = take("square", [P, TOK])
    acc = take("square_sum", [P, TOK])
    rb = take("rms_bc", [P, TOK])
    take = region(R0, R1 - R0)
    xtok = take("x_tokens", [P, NT, D])
    take = region(R0, R1 - R0)
    f_hi = take("f_hi", [P, KT, TOK], F32R)
    f_lo = take("f_lo", [P, KT, TOK], F32R)
    take = region(R1, R2 - R1)
    u_hi = take("u_hi", [P, KT, TOK], F32R)
    u_lo = take("u_lo", [P, KT, TOK], F32R)
    take = region(R2, R3 - R2)
    facc = take("ffn_sum", [P, KT, TOK])
    take = region(R3, end - R3)
    sg = take("silu_gate", [P, TOK])
    up = take("hidden", [P, TOK])
    take = region(R0, R1 - R0)
    x2b = take("x2_back", [P, KT, TOK])
    otile = take("out_tile", [P, 4, D])

    ps = nc.alloc_psum_tensor("ps", [P, 8, HALF], F32)
    AS, APB = 0, 2

    def sem(name):
        return nc.alloc_semaphore(name)

    raw_in = [sem("raw_in0"), sem("raw_in1")]
    w_hi, w_lo = sem("w_hi"), sem("w_lo")
    mm_done = sem("mm_done")
    evac = [sem("evac0"), sem("evac1")]
    x_in = [sem("x_in0"), sem("x_in1")]
    x_sum, x_rs, x_nrm, x_tr, x_wt, x_hi, x_lo = (sem("x_sum"), sem("x_rs"), sem("x_nrm"), sem("x_tr"), sem("x_wt"),
                                                  sem("x_hi"), sem("x_lo"))
    par_in, par_tr, par_ok, wd_in, wd_h, wd_l = (sem("par_in"), sem("par_tr"), sem("par_ok"), sem("wd_in"),
                                                 sem("wd_h"), sem("wd_l"))
    consts, bc_in = sem("consts"), sem("bc_in")
    conv_in, conv_ok, silu_ok = sem("conv_in"), sem("conv_ok"), sem("silu_ok")
    dz_ok, gz_ok = sem("dz_ok"), sem("gz_ok")
    stored = [sem("stored0"), sem("stored1")]
    dab_mm, dab_add, dab_act, dab_g, cum_mm, cols_ok = (sem("dab_mm"), sem("dab_add"), sem("dab_act"), sem("dab_g"),
                                                        sem("cum_mm"), sem("cols_ok"))
    full = [sem("lane0_full"), sem("lane1_full"), sem("lane2_full")]
    free = [sem("lane0_read"), sem("lane1_read"), sem("lane2_read")]
    s_full, s_free, p_full, p_free = sem("score_full"), sem("score_read"), sem("probT_full"), sem("probT_read")
    qkv_in = [sem("qkv_in0"), sem("qkv_in1")]
    sq_ok, rr_ok, a1_ok, a2_ok, dt_ok, dl_ok, dlb_ok, de_ok, m1_ok, w1_ok = (
        sem("sq_ok"), sem("rr_ok"), sem("a1_ok"), sem("a2_ok"), sem("dt_ok"), sem("dl_ok"), sem("dlb_ok"),
        sem("de_ok"), sem("m1_ok"), sem("w1_ok"))
    o_ok, osq_ok, ored_ok, of_ok, on_ok = sem("o_ok"), sem("osq_ok"), sem("ored_ok"), sem("of_ok"), sem("on_ok")
    win_ok, sc_ok, nm_ok, ex_ok, rec_ok, pr_ok = (sem("win_ok"), sem("sc_ok"), sem("nm_ok"), sem("ex_ok"),
                                                  sem("rec_ok"), sem("pr_ok"))
    pcopy = sem("pcopy")
    y_h, y_l, gate_in = sem("y_h"), sem("y_l"), [sem("gate_in0"), sem("gate_in1")]
    mrg, m_h, m_l = sem("mrg"), sem("m_h"), sem("m_l")
    o_sq, o_acc, xt_in = sem("o_sq"), sem("o_acc"), sem("xt_in")
    n_mm, n_add, n_pow, n_dg, n_bc, n_rb = (sem("n_mm"), sem("n_add"), sem("n_pow"), sem("n_dg"), sem("n_bc"),
                                            sem("n_rb"))
    xt_ps, x2_ok, x2_st, fw, f_h, f_l = (sem("xt_ps"), sem("x2_ok"), sem("x2_st"), sem("fw"), sem("f_h"),
                                         sem("f_l"))
    sg_ok, up_ok, u_h, u_l = sem("sg_ok"), sem("up_ok"), sem("u_h"), sem("u_l")
    fa_ok, x2_back, x3_ok, ot_ps, ot_ok, out_st = (sem("fa_ok"), sem("x2_back"), sem("x3_ok"), sem("ot_ps"),
                                                   sem("ot_ok"), [sem("out_st0"), sem("out_st1")])

    TR = nc.tensor.transpose
    MM = nc.tensor.matmul

    def wait(eng, s, value):
        if isinstance(value, int) and value <= 0:
            return
        eng.wait_ge(s, value)

    def settle(eng):
        eng.wait_ge(consts, 1)

    def steps(eng, first, last, body, peel=0):
        for n in range(first, first + peel):
            body(n, n // 2, n % 2)
        s = first + peel
        if s == last:
            return
        assert (last - s) % 2 == 0
        if last - s == 2:
            for n in (s, s + 1):
                body(n, n // 2, n % 2)
            return
        with eng.Fori(0, (last - s) // 2) as i:
            for u in (0, 1):
                body(i * 2 + (s + u), i + (s + u) // 2, (s + u) % 2)

    def mixer_steps(eng, body):
        steps(eng, 1, NT + 1, body)

    def delta_bank(op):
        return ps[:, 5 + lane_of(op), :].rearrange("p (h c) -> p h c", h=DH)

    def banks(b, n=2):
        return ps[:, b:b + n, :].rearrange("p a b -> p (a b)")

    def split_hi(n1, m1, u1):
        wait(nc.scalar, raw_in[u1], (m1 + 1) * 48)
        wait(nc.scalar, mm_done, n1 - 1)
        nc.scalar.activation(whi[:, u1], raw[:, u1], ACT.Copy).then_inc(w_hi, 1)

    def split_lo(n1, m1, u1):
        wait(nc.vector, w_hi, n1 + 1)
        nc.vector.tensor_tensor(wlo[:, u1], raw[:, u1], whi[:, u1].bitcast(F32), ALU.subtract).then_inc(w_lo, 1)

    def after(n, m, u):
        return (n + 1, m + u, 1 - u)

    def dense(n, m, u, hi, lo, c0, nk=KT, meta_cols=False, ks=None, bank=0):
        if ks is None:
            wait(nc.tensor, w_lo, n + 1)
            wait(nc.tensor, evac[u], m)
            ks = list(range(nk))
        last = None
        groups = [(4 * u + bank + b, c0 + b * HALF, HALF) for b in range(2)]
        if meta_cols:
            groups.append((4 * u + 2, 0, META))
        for b, c, w in groups:
            for k in ks:
                for i, (a, mv) in enumerate(((whi, hi), (whi, lo), (wlo, hi))):
                    last = MM(ps[:, b, 0:w], a[:, u, k, :], mv[:, k, c:c + w],
                              start=(k == ks[0] and i == 0), stop=(k == ks[-1] and i == 2))
        return last

    block = nc.Block()
    block.__enter__()

    @block.sync
    def _(sp):
        sp.dma_start(xin[0:META, 0, :], meta).then_inc(x_in[0], 16)
        sp.dma_start(xin[:, 1, :], x[0:P, :]).then_inc(x_in[1], 16)
        bq = b_in[Q0:Q0 + 512].rearrange("(g j c) -> g j c", g=2, c=HD)
        sp.dma_start(prow[0:GRP, 0:HD], bq[0]).then_inc(par_in, 16)
        sp.dma_start(prow[0:GRP, HD:P], bq[1]).then_inc(par_in, 16)
        for dst, cnt, src in ((GRP, 18, b_in[K0:DAB0]), (R_BG, 16, b_in[G0:G0 + 2048]), (R_PRE, 8, n_pre),
                              (R_POST, 8, n_post), (R_FPRE, 8, f_pre), (R_FPOST, 8, f_post), (R_DNW, 1, dn_norm_w),
                              (R_CONV, 48, conv_w.rearrange("k c -> (k c)"))):
            sp.dma_start(prow[dst:dst + cnt, :], src.rearrange("(t p) -> t p", p=P)).then_inc(par_in, 16)

        def load(n, m, u, pieces):
            wait(sp, w_lo, n - 1)
            for dst, src in pieces:
                sp.dma_start(dst, src).then_inc(raw_in[u], 48 // len(pieces))

        def w_cols(w, c):
            return w[:, bass.ds(c, P)].rearrange("(k p) c -> p k c", p=P)

        def kv_w(n, m, u):
            load(n, m, u, [(raw[:, u], w_cols(w_in, (n - N_KV) * P + K0))])

        def q_w2(n, m, u):
            j = n - N_Q
            wait(sp, w_lo, n - 1)
            for g in range(2):
                sp.dma_start(raw[:, u, :, g * HD:(g + 1) * HD],
                             w_in[:, bass.ds(j * HD + g * GRP * HD, HD)].rearrange("(k p) c -> p k c", p=P)
                             ).then_inc(raw_in[u], 16 + 16 * g)

        def dn_w(n, m, u):
            load(n, m, u, [(raw[:, u], w_cols(w_in, (n - N_DN) * P + DN0))])

        def g_w(n, m, u):
            load(n, m, u, [(raw[:, u], w_cols(w_in, (n - N_G) * P + G0))])

        def merge_w(n, m, u):
            wait(sp, w_lo, n - 1)
            c = (n - N_MERGE) * P
            for g in range(2):
                src = w_att[g * GRP * HD:(g + 1) * GRP * HD, bass.ds(c, P)].rearrange("(j p) c -> p j c", p=HD)
                sp.dma_start(raw[g * HD:(g + 1) * HD, u, 0:4, :], src).then_inc(raw_in[u], 16)
            sp.dma_start(raw[:, u, 4:8, :], w_dn[:, bass.ds(c, P)].rearrange("(k p) c -> p k c", p=P)
                         ).then_inc(raw_in[u], 16)

        def out_w(n, m, u):
            load(n, m, u, [(raw[:, u], w_cols(w_out, (n - N_OUT) * P))])

        kv_w(0, 0, 0)
        kv_w(1, 0, 1)
        for dst, src in ((dab_b, b_in[DAB0:DAB0 + 8]), (dtb, dt_bias), (alog, a_log), (sink, att_sinks)):
            sp.dma_start(dst[:], src.rearrange("(a c) -> a c", a=1).to_broadcast([P, src.shape[0]])).then_inc(bc_in, 16)
        sp.dma_start(wd_raw[:], w_in[:, DAB0:DAB0 + 8].rearrange("(k p) c -> p k c", p=P)).then_inc(wd_in, 16)

        def x_load(t, m, u):
            wait(sp, x_nrm, t - 1)
            sp.dma_start(xin[:, u, :], x[bass.ds((t - 1) * P, P), :]).then_inc(x_in[u], 16)
        steps(sp, 2, NT + 1, x_load, peel=1)
        for n in range(N_Q, N_DN):
            q_w2(n, n // 2, n % 2)
        dn_w(N_DN, N_DN // 2, 0)
        dn_w(N_DN + 1, N_DN // 2, 1)

        def store_qkv(j, parity):
            sp.wait_ge(silu_ok, j + 1)
            sp.dma_start(qkv_d[bass.ds(j, 1)].rearrange("a p c -> p (a c)"), cs[:, parity, :]).then_inc(stored[parity], 16)

        def dn_step(n, m, u):
            dn_w(n, m, u)
            store_qkv(n - 2 - N_DN, u)
        steps(sp, N_DN + 2, N_DZ, dn_step)

        def dz_w(n, m, u):
            load(n, m, u, [(raw[:, u], w_cols(w_in, (n - N_DZ) * P + DZ0))])
            if n < N_DZ + 2:
                store_qkv(n - 2 - N_DN, u)
        for n in range(N_DZ, N_G):
            dz_w(n, n // 2, n % 2)
        g_w(N_G, N_G // 2, 0)
        g_w(N_G + 1, N_G // 2, 1)

        def g_step(n, m, u):
            if not (isinstance(n, int) and n >= N_MERGE):
                g_w(n, m, u)
            else:
                merge_w(n, m, u)
            sp.wait_ge(silu_ok, n - 2 - N_G + 13)
            sp.dma_start(gate_d[bass.ds(n - 2 - N_G, 1)].rearrange("a p c -> p (a c)"), cs[:, u, 0:TOK]
                         ).then_inc(stored[u], 16)
        steps(sp, N_G + 2, N_MERGE, g_step)
        g_step(N_MERGE, N_MERGE // 2, 0)
        g_step(N_MERGE + 1, N_MERGE // 2, 1)

        sp.wait_ge(mm_done, N_MERGE)
        for u in range(2):
            sp.wait_ge(stored[u], 16 * 14)
        sp.dma_start(qkv[:, 0, :, 0:META], qkv_d[:, :, 0:META].rearrange("t p c -> p t c")).then_inc(qkv_in[0], 16)

        def chunk_load(c, m, u):
            if isinstance(c, int) and c == 2:
                sp.wait_ge(full[lane_of("dS")], filled("dS", 0))
            elif not (isinstance(c, int) and c == 1):
                wait(sp, full[lane_of("P1")], filled("P1", c - 2))
            sp.dma_start(qkv[:, u], qkv_d[:, :, bass.ds((c - 1) * P + META, P)].rearrange("t p c -> p t c")
                         ).then_inc(qkv_in[u], 16)
        steps(sp, 1, NT + 1, chunk_load, peel=2)

        def gates_load(n, m, u):
            if isinstance(n, int) and n < N_MERGE + 2:
                sp.wait_ge(y_l, 2)
                sp.wait_ge(y_h, 2)
            else:
                sp.wait_ge(mrg, n - N_MERGE - 1)
            j = n - N_MERGE
            for g in range(2):
                sp.dma_start(gin[:, u, g, :], gate_d[bass.ds(j + 8 * g, 1)].rearrange("a p c -> p (a c)")
                             ).then_inc(gate_in[u], 16)
        gates_load(N_MERGE, N_MERGE // 2, 0)
        gates_load(N_MERGE + 1, N_MERGE // 2, 1)

        def merge_step(n, m, u):
            merge_w(n, m, u)
            gates_load(n, m, u)
        steps(sp, N_MERGE + 2, N_OUT, merge_step)
        out_w(N_OUT, N_OUT // 2, 0)
        out_w(N_OUT + 1, N_OUT // 2, 1)
        sp.wait_ge(mm_done, N_OUT)
        sp.dma_start(xtok[:], x.rearrange("(t p) d -> p t d", p=P)).then_inc(xt_in, 16)
        steps(sp, N_OUT + 2, N_FF, out_w)

        def ffn_weights(n0, s0, sz):
            def in_w(n, m, u):
                c = (m - n0 // 2 + s0) * P + u * FF
                load(n, m, u, [(raw[:, u], w_cols(w_fi, c))])

            def out_w2(n, m, u):
                load(n, m, u, [(raw[:, u, 0:sz, :],
                                w_fo[s0 * P:(s0 + sz) * P, bass.ds((n - n0 - 2 * sz) * P, P)]
                                .rearrange("(k p) c -> p k c", p=P))])
            return in_w, out_w2

        n0 = N_FF
        for gi, sz in enumerate(FF_GROUPS):
            in_w, out_w2 = ffn_weights(n0, sum(FF_GROUPS[:gi]), sz)
            if gi == 0:
                in_w(n0, n0 // 2, 0)
                in_w(n0 + 1, n0 // 2, 1)
                sp.wait_ge(x2_ok, KT)
                sp.dma_start(x2_d.rearrange("t p c -> p t c"), oT[:]).then_inc(x2_st, 16)
                steps(sp, n0 + 2, n0 + 2 * sz, in_w)
            else:
                steps(sp, n0, n0 + 2 * sz, in_w)
            steps(sp, n0 + 2 * sz, n0 + 2 * sz + KT, out_w2)
            n0 += 2 * sz + KT
        sp.wait_ge(x2_st, 16)
        sp.wait_ge(mm_done, n0 - KT)
        sp.dma_start(x2b[:], x2_d.rearrange("t p c -> p t c")).then_inc(x2_back, 16)

        def out_store(t, m, u):
            sp.wait_ge(ot_ok, t + 1)
            sp.dma_start(out[bass.ds(t * P, P), :], otile[:, u, :]).then_inc(out_st[u], 16)
        steps(sp, 0, NT, out_store)
        for u in range(2):
            sp.wait_ge(out_st[u], 16 * (NT // 2))

    @block.gpsimd
    def _(pool):
        g = nc.gpsimd
        g.memset(ones[:], 1.0)
        g.memset(half[:], -0.5)
        g.memset(small[:, 4:5], 1.0 / D)
        g.memset(band[:], 0.0)
        g.memset(mask_up[:], 0.0)
        g.memset(mask_low[:], 0.0)
        g.memset(ident[:], 0.0)
        g.memset(upper[:], 1.0)
        g.memset(blocks16[:], 1.0)
        g.memset(ak[:, 0:P - META], 0.0)
        g.memset(av[:, 0:P - META], 0.0)
        g.memset(vtok[:, 0, :], 0.0)
        g.drain()
        g.affine_select(out=ident[:], in_=ident[:], compare_op=ALU.not_equal, fill=1.0, base=0,
                        pattern=[[-1, P]], channel_multiplier=1).then_inc(consts, 1)
        g.affine_select(out=upper[:], in_=upper[:], compare_op=ALU.is_ge, fill=0.0, base=0,
                        pattern=[[1, P]], channel_multiplier=-1)
        g.affine_select(out=mask_up[:], in_=mask_up[:], compare_op=ALU.is_ge, fill=NEG, base=0,
                        pattern=[[1, P]], channel_multiplier=-1)
        g.affine_select(out=mask_low[:], in_=mask_low[:], compare_op=ALU.is_gt, fill=NEG, base=0,
                        pattern=[[-1, P]], channel_multiplier=1)
        b3 = blocks16[:].rearrange("p (b c) -> p b c", c=16)
        g.affine_select(out=b3, in_=b3, compare_op=ALU.is_ge, fill=0.0, base=0,
                        pattern=[[-16, 8], [0, 16]], channel_multiplier=1)
        g.drain()
        g.affine_select(out=b3, in_=b3, compare_op=ALU.is_ge, fill=0.0, base=15,
                        pattern=[[16, 8], [0, 16]], channel_multiplier=-1)
        g.affine_select(out=band[:, META:META + P], in_=band[:, META:META + P], compare_op=ALU.is_gt, fill=NEG,
                        base=0, pattern=[[1, P]], channel_multiplier=-1)
        g.affine_select(out=band[:, META + P:], in_=band[:, META + P:], compare_op=ALU.is_ge, fill=NEG,
                        base=0, pattern=[[-1, P]], channel_multiplier=1)
        g.drain()
        g.tensor_copy(band_now[:], band[:])
        g.drain()
        g.memset(band_now[:, META:META + P], NEG).then_inc(consts, 1)

        def x_rsqrt(t, w):
            settle(pool)
            pool.wait_ge(x_sum, t + 1)
            g.tensor_tensor(small[0:w, 2:3], small[0:w, 0:1], small[0:w, 4:5], ALU.mult)
            g.drain()
            g.tensor_scalar(small[0:w, 2:3], small[0:w, 2:3], EPS, None, ALU.add)
            g.drain()
            g.tensor_tensor(small[0:w, 3:4], small[0:w, 2:3], half[0:w, :], ALU.pow).then_inc(x_rs, 1)

        def x_low(t, w, c):
            pool.wait_ge(x_hi, t + 1)
            g.tensor_tensor(h_lo[:, :, bass.ds(c, w)], xw[:, 0, 0:KT * w].rearrange("p (k c) -> p k c", k=KT),
                            h_hi[:, :, bass.ds(c, w)].bitcast(F32), ALU.subtract).then_inc(x_lo, 1)
        x_rsqrt(0, META)
        x_low(0, META, 0)

        def x_step(t, m, u):
            x_rsqrt(t, P)
            x_low(t, P, (t - 1) * P + META)
        steps(pool, 1, NT + 1, x_step)
        pool.wait_ge(x_lo, NT + 1)
        pool.wait_ge(par_tr, 1)
        g.memset(rawc[:, :, 0:3], 0.0).then_inc(consts, 1)

        pool.wait_ge(dz_ok, DH)
        g.tensor_scalar(gz[:], gz[:], params[:, R_DNW:R_DNW + 1], None, ALU.mult).then_inc(gz_ok, 1)

        cc = [tiny[:, 0:24], tiny[:, 24:48]]
        E8, RR, BK, CA, CZ, S2, S2S, OF, OE = (small[:, 8:16], small[:, 16:24], small[:, 24:28], small[:, 28:32],
                                               small[:, 32:36], small[:, 36:40], small[:, 40:44], small[:, 44:48],
                                               small[:, 48:52])

        def pool_chunk(c, m, u, L=P):
            first = isinstance(c, int) and c == 0
            if first:
                pool.wait_ge(cols_ok, 3)
                g.tensor_copy(cc[u][0:L], cols[0:L, 0, :])
            else:
                g.tensor_copy(cc[u][:], cols[:, bass.ds(c, 1), :].rearrange("p a c -> p (a c)"))
            pool.wait_ge(qkv_in[u], (m + 1) * 16)
            g.tensor_tensor(sq[:, :, 0:L], qkv[:, u, 0:8, 0:L], qkv[:, u, 0:8, 0:L], ALU.mult).then_inc(sq_ok, 1)
            pool.wait_ge(free[lane_of("ssq")], filled("ssq", c))
            g.tensor_tensor(RR[0:L], E8[0:L], half[0:L, :].to_broadcast([L, 8]), ALU.pow)
            g.drain()
            g.tensor_tensor(BK[0:L], cc[u][0:L, 20:24], RR[0:L, 4:8], ALU.mult)
            g.tensor_scalar(S2[0:L], RR[0:L, 0:4], float(P) ** -0.5, None, ALU.mult)
            g.drain()
            g.tensor_tensor(CA[0:L], BK[0:L], RR[0:L, 4:8], ALU.mult)
            g.tensor_tensor(S2S[0:L], S2[0:L], S2[0:L], ALU.mult)
            g.drain()
            g.tensor_scalar(CA[0:L], CA[0:L], -1.0, None, ALU.mult)
            g.drain()
            g.tensor_tensor(CZ[0:L], CA[0:L], cc[u][0:L, 8:12], ALU.mult).then_inc(rr_ok, 1)
            g.drain()
            pool.wait_ge(dl_ok, c + 1)
            g.tensor_tensor(buf["DL"][0:L, :, 0:L], buf["DL"][0:L, :, 0:L],
                            CA[0:L].unsqueeze(2).to_broadcast([L, DH, L]), ALU.mult).then_inc(dlb_ok, 1)
            pool.wait_ge(free[lane_of("KK")], filled("KK", c))
            g.tensor_tensor(buf["Dn"][0:L, :, 0:L], buf["t1"][0:L, :, 0:L],
                            blocks16[0:L, 0:L].unsqueeze(1).to_broadcast([L, DH, L]), ALU.mult)
            g.drain()
            g.tensor_tensor(buf["En"][0:L, :, 0:L], buf["t1"][0:L, :, 0:L], buf["Dn"][0:L, :, 0:L],
                            ALU.subtract).then_inc(de_ok, 1)
            eye = ident[0:L, 0:L].unsqueeze(1).to_broadcast([L, DH, L])
            pool.wait_ge(free[lane_of("DnT")], filled("DnT", c))
            g.tensor_tensor(buf["M1"][0:L, :, 0:L], buf["DnT"][0:L, :, 0:L], eye, ALU.add).then_inc(m1_ok, 1)
            if first:
                return
            pool.wait_ge(free[lane_of("BT")], filled("BT", c))
            g.tensor_tensor(buf["W1"][:], buf["BT"][:], eye, ALU.add).then_inc(w1_ok, 1)
            pool.wait_ge(free[lane_of("P2")], filled("P2", c))
            g.tensor_tensor(buf["osq"][:], buf["op"][:], buf["op"][:], ALU.mult).then_inc(osq_ok, 1)
            pool.wait_ge(ored_ok, c)
            g.tensor_tensor(OE, OE, S2S, ALU.mult)
            g.drain()
            g.tensor_scalar(OE, OE, 1.0 / P, EPS, ALU.mult, ALU.add)
            g.drain()
            g.tensor_tensor(OE, OE, half[:].to_broadcast([P, 4]), ALU.pow)
            g.drain()
            g.tensor_tensor(OF, OE, S2, ALU.mult)
            g.drain()
            g.tensor_tensor(buf["on"][:], buf["op"][:], OF.unsqueeze(2).to_broadcast([P, DH, P]),
                            ALU.mult).then_inc(on_ok, 1)

        def windows(c):
            pool.wait_ge(s_full, att_filled("O1", c - 1))
            g.tensor_copy(kwin[:, META:], ak[:, bass.ds((c - 1) * P, 2 * P)])
            g.tensor_copy(vwin[:], vtok[:, bass.ds(c - 1, 2), :])
            g.tensor_copy(qblk[:], aq[:, :, bass.ds((c - 1) * P, P)]).then_inc(win_ok, 1)

        def probs(c, i):
            pool.wait_ge(rec_ok, (c - 1) * 4 + (i + 1))
            pb = prob[:, i % 2]
            g.tensor_tensor(pb, pb, small[:, 56 + 2 * (i % 2):58 + 2 * (i % 2)].unsqueeze(2)
                            .to_broadcast([P, 2, META + 2 * P]), ALU.mult).then_inc(pr_ok, 1)

        def mixer(c, m, u):
            windows(c)
            for i in range(4):
                probs(c, i)
            pool_chunk(c, m, u)
        pool_chunk(0, 0, 0, META)
        pool.wait_ge(s_free, 1)
        pool.wait_ge(p_free, 1)
        g.tensor_copy(kwin[:, 0:META], ak[:, P - META:P])
        mixer_steps(pool, mixer)

        def merge_add(n, m, u):
            pool.wait_ge(evac[u], m + 1)
            wait(pool, m_l, n - N_MERGE)
            g.tensor_tensor(mt[:, 0, :], mt[:, 0, :], mt[:, 1, :], ALU.add).then_inc(mrg, 1)
        steps(pool, N_MERGE, N_OUT, merge_add, peel=2)

        def sum_squares(base, count):
            for k in range(count):
                pool.wait_ge(o_sq, base + k + 1)
                if k == 0:
                    g.tensor_copy(acc[:], sqt[:]).then_inc(o_acc, 1)
                else:
                    g.drain()
                    g.tensor_tensor(acc[:], acc[:], sqt[:], ALU.add).then_inc(o_acc, 1)

        def rms_pow(r):
            pool.wait_ge(n_add, r)
            g.tensor_tensor(small[:, 0:8], small[:, 8:16], half[:].to_broadcast([P, 8]), ALU.pow).then_inc(n_pow, 1)
        sum_squares(0, KT)
        rms_pow(1)
        sum_squares(KT, KT)
        rms_pow(2)
        for k in range(KT):
            pool.wait_ge(f_h, k + 1)
            g.tensor_tensor(f_lo[:, k, :], [sg, up][k % 2][:], f_hi[:, k, :].bitcast(F32), ALU.subtract).then_inc(f_l, 1)
        n0 = N_FF
        done = 0
        for sz in FF_GROUPS:
            def hidden_lo(j, m, u, done=done, n0=n0):
                pool.wait_ge(u_h, j + (done + 1))
                g.tensor_tensor(u_lo[:, bass.ds(j, 1), :].rearrange("p a c -> p (a c)"), up[:],
                                u_hi[:, bass.ds(j, 1), :].rearrange("p a c -> p (a c)").bitcast(F32),
                                ALU.subtract).then_inc(u_l, 1)
            steps(pool, 0, sz, hidden_lo)
            done += sz
            n0 += 2 * sz + KT
        sum_squares(2 * KT, KT)
        rms_pow(3)

    @block.scalar
    def _(act):
        a = nc.scalar

        def x_tile(t, m, u, w=P, c=0):
            act.wait_ge(x_in[u], (m + 1) * 16)
            wait(act, x_nrm, t)
            a.activation(xw[0:w, 0, :], xin[0:w, u, :], ACT.Square, accum_out=small[0:w, 0:1]).then_inc(x_sum, 1)
            act.wait_ge(x_wt, t + 1)
            settle(act)
            a.activation(h_hi[:, :, bass.ds(c, w)], xw[:, 0, 0:KT * w].rearrange("p (k c) -> p k c", k=KT),
                         ACT.Copy).then_inc(x_hi, 1)
            act.wait_ge(x_lo, t + 1)

        x_tile(0, 0, 0, META, 0)
        steps(act, 1, NT + 1, lambda t, m, u: x_tile(t, m, u, P, (t - 1) * P + META))
        split_hi(0, 0, 0)
        act.wait_ge(wd_in, 16)
        a.activation(wd_hi[:], wd_raw[:], ACT.Copy).then_inc(wd_h, 1)

        def bias(base, j):
            return params[:, bass.ds(j + base, 1)]

        def kv_out(n, m, u):
            split_hi(*after(n, m, u))
            act.wait_ge(mm_done, n + 1)
            dst = (ak, av)[n]
            a.activation(dst[:, P:], banks(4 * u), ACT.Identity, bias=params[:, GRP + n:GRP + n + 1])
            a.activation(dst[:, P - META:P], ps[:, 4 * u + 2, 0:META], ACT.Identity,
                         bias=params[:, GRP + n:GRP + n + 1]).then_inc(evac[u], 1)
        kv_out(0, 0, 0)
        kv_out(1, 0, 1)

        def q_out(n, m, u):
            split_hi(*after(n, m, u))
            act.wait_ge(mm_done, n + 1)
            settle(act)
            a.activation(aq[:, bass.ds(n - N_Q, 1), :].rearrange("p a c -> p (a c)"), banks(4 * u), ACT.Identity,
                         bias=bias(0, n - N_Q)).then_inc(evac[u], 1)
        steps(act, N_Q, N_DN, q_out)

        def silu_conv(j, parity):
            act.wait_ge(conv_ok, j + 1)
            if not isinstance(j, int):
                act.wait_ge(stored[parity], (j_half(j)) * 16)
            elif j >= 2:
                act.wait_ge(stored[parity], (j // 2) * 16)
            a.activation(cs[:, parity, :], cv[:, parity, :], ACT.Silu).then_inc(silu_ok, 1)

        jh = {}

        def j_half(j):
            return jh["m"]

        def dn_out(n, m, u):
            split_hi(*after(n, m, u))
            j = n - N_DN
            if not (isinstance(n, int) and n == N_DN):
                jh["m"] = (m - N_DN // 2) + (0 if u == 1 else -1)
                silu_conv(j - 1, 1 - u)
            act.wait_ge(mm_done, n + 1)
            b = bias(R_BIAS, n - N_DN + 6)
            settle(act)
            a.activation(rawc[:, u, 3 + META:], banks(4 * u), ACT.Identity, bias=b)
            a.activation(rawc[:, u, 3:3 + META], ps[:, 4 * u + 2, 0:META], ACT.Identity, bias=b).then_inc(evac[u], 1)
        act.wait_ge(consts, 3)
        act.wait_ge(x_lo, NT + 1)
        steps(act, N_DN, N_DZ, dn_out, peel=4)

        def dz_out(n, m, u):
            split_hi(*after(n, m, u))
            if n == N_DZ:
                jh["m"] = 5
                silu_conv(11, 1)
            act.wait_ge(mm_done, n + 1)
            a.activation(gz[:, n - N_DZ, :], banks(4 * u), ACT.Silu, bias=bias(R_BIAS, n - N_DZ + 18)).then_inc(dz_ok, 1)
            a.drain().then_inc(evac[u], 1)
        for n in range(N_DZ, N_G):
            dz_out(n, n // 2, n % 2)

        def gate_out(n, m, u):
            split_hi(*after(n, m, u))
            act.wait_ge(mm_done, n + 1)
            act.wait_ge(stored[u], (m - N_G // 2 + 6) * 16)
            settle(act)
            a.activation(cs[:, u, 0:TOK], banks(4 * u), ACT.Sigmoid, bias=bias(R_BG, n - N_G)).then_inc(silu_ok, 1)
            a.drain().then_inc(evac[u], 1)
        steps(act, N_G, N_MERGE, gate_out)

        act.wait_ge(bc_in, 64)
        ea = tiny[:, 48:52]
        a.activation(ea, alog[:], ACT.Exp)
        act.wait_ge(dab_add, 1)
        dx = dabx[:]
        a.activation(dabe[:, :, 4:8], dx[:, :, 4:8], ACT.Exp, scale=-1.0)
        a.activation(dabe[:, :, 0:4], dx[:, :, 0:4], ACT.Abs)
        a.drain()
        a.activation(dabe[:, :, 0:4], dabe[:, :, 0:4], ACT.Exp, scale=-1.0)
        a.drain()
        a.activation(dabe[:, :, 0:4], dabe[:, :, 0:4], ACT.Ln, bias=1.0).then_inc(dab_act, 1)
        act.wait_ge(cols_ok, 1)
        a.activation(cols[:, :, 8:12], cols[:, :, 4:8], ACT.Exp)
        a.activation(cols[:, 1:, 12:16], cols[:, 1:, 12:16], ACT.Exp)
        a.activation(cols[0:META, 0, 12:16], cols[0:META, 0, 12:16], ACT.Exp)
        a.activation(cols[:, :, 16:20], cols[:, :, 16:20], ACT.Exp).then_inc(cols_ok, 2)

        def copy_of(op, c, L=P, dst=None):
            lane = lane_of(op)
            act.wait_ge(full[lane], filled(op, c))
            a.activation(buf[dst or op][0:L, :, 0:L], delta_bank(op)[0:L, :, 0:L], ACT.Copy).then_inc(free[lane], 1)

        def decays(c, L):
            act.wait_ge(a1_ok, c + 1)
            a.activation(buf["DT"][0:L, :, 0:L], buf["DT"][0:L, :, 0:L], ACT.Exp).then_inc(dt_ok, 1)
            act.wait_ge(a2_ok, c + 1)
            a.activation(buf["DL"][0:L, :, 0:L], buf["DL"][0:L, :, 0:L], ACT.Exp).then_inc(dl_ok, 1)

        def exps(c, i):
            act.wait_ge(nm_ok, (c - 1) * 4 + (i + 1))
            s = i % 2
            for h in range(2):
                a.activation(prob[:, s, h, :], prob[:, s, h, :], ACT.Exp, scale=HD ** -0.5,
                             bias=tiny[:, 56 + 4 * s + h:57 + 4 * s + h], accum_out=tiny[:, 64 + 4 * s + h:65 + 4 * s + h])
            a.activation(tiny[:, 66 + 4 * s:68 + 4 * s], tiny[:, 58 + 4 * s:60 + 4 * s], ACT.Exp).then_inc(ex_ok, 1)

        def probs_T(c, kv):
            act.wait_ge(p_full, (c - 1) * 2 + (kv + 2))
            a.activation(pt[0:META, 0, :], ps[0:META, APB, :], ACT.Copy)
            a.activation(pt[:, 1:3, :], ps[:, APB + 1:APB + 3, :], ACT.Copy).then_inc(p_free, 1)

        def att_out(c, kv):
            act.wait_ge(s_full, att_filled(f"O{kv}", c))
            settle(act)
            a.activation(ya[kv * HD:(kv + 1) * HD, :, bass.ds((c - 1) * P, P)],
                         ps[kv * HD:(kv + 1) * HD, AS, :].rearrange("p (j c) -> p j c", j=GRP),
                         ACT.Copy).then_inc(s_free, 1)

        decays(0, META)
        for op in ("DnT", "D2", "D2T", "D4", "D8"):
            copy_of(op, 0, META)
        act.wait_ge(full[1], filled("VN", 0))
        a.activation(buf["vn"][0:META], delta_bank("VN")[0:META], ACT.Copy).then_inc(free[1], 1)

        def mixer(c, m, u):
            exps(c, 0)
            exps(c, 1)
            probs_T(c, 0)
            att_out(c, 0)
            exps(c, 2)
            exps(c, 3)
            probs_T(c, 1)
            att_out(c, 1)
            decays(c, P)
            for op in ("DnT", "D2", "D2T", "D4", "D8", "Ninv", "B", "BT", "B2", "B4", "TT"):
                copy_of(op, c)
            act.wait_ge(full[1], filled("VN", c))
            a.activation(buf["vn"][:], delta_bank("VN"), ACT.Copy).then_inc(free[1], 1)
        mixer_steps(act, mixer)

        act.wait_ge(full[2], filled("oT", NT))
        act.wait_ge(s_free, att_filled("O1", NT))
        a.activation(y_hi[:, 0:4, :], ya[:], ACT.Copy).then_inc(y_h, 1)
        act.wait_ge(free[2], filled("oT", NT))
        a.activation(y_hi[:, 4:8, :], yd[:], ACT.Copy).then_inc(y_h, 1)

        def merge_hi(n, m, u):
            split_hi(*after(n, m, u))
            act.wait_ge(mrg, n - N_MERGE + 1)
            settle(act)
            a.activation(m_hi[:, bass.ds(n - N_MERGE, 1), :].rearrange("p a c -> p (a c)"), mt[:, 0, :],
                         ACT.Copy).then_inc(m_h, 1)
        steps(act, N_MERGE, N_OUT, merge_hi, peel=0)

        def square(src, idx):
            settle(act)
            wait(act, o_acc, idx)
            a.activation(sqt[:], src, ACT.Square).then_inc(o_sq, 1)

        def out_evac(n, m, u):
            split_hi(*after(n, m, u))
            act.wait_ge(mm_done, n + 1)
            if isinstance(n, int) and n == N_OUT:
                act.wait_ge(m_l, KT)
            settle(act)
            dst = oT[:, bass.ds(n - N_OUT, 1), :].rearrange("p a c -> p (a c)")
            a.activation(dst, banks(4 * u), ACT.Copy).then_inc(evac[u], 1)
            a.drain()
            square(dst, n - N_OUT)
        steps(act, N_OUT, N_FF, out_evac, peel=2)
        for k in range(KT):
            act.wait_ge(x2_ok, k + 1)
            square(oT[:, k, :], KT + k)
        for k in range(KT):
            act.wait_ge(fw, k + 1)
            a.activation(f_hi[:, k, :], [sg, up][k % 2][:], ACT.Copy).then_inc(f_h, 1)
        n0, done = N_FF, 0
        for gi, sz in enumerate(FF_GROUPS):
            def gate(n, m, u, n0=n0, done=done):
                split_hi(*after(n, m, u))
                if u == 0:
                    act.wait_ge(mm_done, n + 1)
                    act.wait_ge(f_l, KT)
                    wait(act, up_ok, m - n0 // 2 + done)
                    a.activation(sg[:], banks(0), ACT.Silu).then_inc(sg_ok, 1)
                    a.drain().then_inc(evac[0], 1)
                else:
                    j = m - n0 // 2
                    act.wait_ge(up_ok, j + (done + 1))
                    settle(act)
                    a.activation(u_hi[:, bass.ds(j, 1), :].rearrange("p a c -> p (a c)"), up[:],
                                 ACT.Copy).then_inc(u_h, 1)
            steps(act, n0, n0 + 2 * sz, gate, peel=2)
            n1 = n0 + 2 * sz

            def only_split(n, m, u):
                split_hi(*after(n, m, u))
            if gi < 2:
                steps(act, n1, n1 + KT, only_split)
            else:
                steps(act, n1, n1 + KT - 2, only_split)
                only_split(n1 + KT - 2, (n1 + KT - 2) // 2, 0)
            done += sz
            n0 = n1 + KT
        for k in range(KT):
            act.wait_ge(fa_ok, k + 1)
            square(facc[:, k, :], 2 * KT + k)
        def out_copy(t, m, u):
            act.wait_ge(ot_ps, t + 1)
            if not (isinstance(t, int) and t < 2):
                act.wait_ge(out_st[u], m * 16)
            a.activation(otile[:, u, :], banks(2 * u), ACT.Copy).then_inc(ot_ok, 1)
        steps(act, 0, NT, out_copy, peel=2)

    @block.vector
    def _(dve):
        v = nc.vector
        dve.wait_ge(par_tr, 1)
        v.tensor_copy(params[:, 0:NROWS], ps[:, 7, 0:NROWS]).then_inc(par_ok, 1)
        v.drain()

        def x_tile(t, m, u, w=P):
            dve.wait_ge(x_rs, t + 1)
            wait(dve, x_tr, t - 1)
            v.tensor_scalar(xn[0:w, u, :], xin[0:w, u, :], small[0:w, 3:4], None, ALU.mult).then_inc(x_nrm, 1)
            dve.wait_ge(x_tr, t + 1)
            v.tensor_tensor(xw[:, 0, 0:KT * w].rearrange("p (k c) -> p k c", k=KT),
                            banks(4 + 0)[:, 0:KT * w].rearrange("p (k c) -> p k c", k=KT),
                            params[:, R_PRE:R_PRE + KT].unsqueeze(2).to_broadcast([P, KT, w]),
                            ALU.mult).then_inc(x_wt, 1)
        x_tile(0, 0, 0, META)
        x_tile(1, 0, 1)
        steps(dve, 2, NT, lambda t, m, u: x_tile(t, m, u))
        x_tile(NT, NT // 2, 0)
        split_lo(0, 0, 0)
        dve.wait_ge(wd_h, 1)
        v.tensor_tensor(wd_lo[:], wd_raw[:], wd_hi[:].bitcast(F32), ALU.subtract).then_inc(wd_l, 1)
        split_lo(1, 0, 1)
        steps(dve, 2, N_DN, lambda n, m, u: split_lo(n, m, u))
        split_lo(N_DN, N_DN // 2, 0)

        def conv(n, m, u):
            split_lo(*after(n, m, u))
            j = n - N_DN
            dve.wait_ge(evac[u], m + 1)
            if not (isinstance(n, int) and n < N_DN + 2):
                dve.wait_ge(silu_ok, j - 1)
            v.tensor_scalar(cv[:, u, :], rawc[:, u, 0:LW], params[:, bass.ds(j + R_CONV, 1)], None, ALU.mult)
            for k in range(1, 4):
                v.drain()
                last = v.scalar_tensor_tensor(cv[:, u, :], rawc[:, u, k:k + LW],
                                              params[:, bass.ds(j + (R_CONV + 12 * k), 1)], cv[:, u, :],
                                              ALU.mult, ALU.add)
            last.then_inc(conv_ok, 1)
        steps(dve, N_DN, N_DZ, conv, peel=2)
        dve.wait_ge(dab_mm, 1)
        dve.wait_ge(bc_in, 64)
        v.tensor_tensor(dab_b[:, 0:4], dab_b[:, 0:4], dtb[:], ALU.add)
        v.drain()
        v.tensor_tensor(dabx[:], ps[:, 3, 0:8 * (NT + 1)].rearrange("p (t c) -> p t c", c=8),
                        dab_b[:].unsqueeze(1).to_broadcast([P, NT + 1, 8]), ALU.add).then_inc(dab_add, 1)
        steps(dve, N_DZ, N_MERGE, lambda n, m, u: split_lo(*after(n, m, u)))

        dve.wait_ge(dab_act, 1)
        v.tensor_scalar(dabx[:, :, 0:4], dabx[:, :, 0:4], 0.0, None, ALU.max)
        v.tensor_scalar(dabe[:, :, 4:8], dabe[:, :, 4:8], 1.0, None, ALU.add)
        v.drain()
        v.tensor_tensor(dabx[:, :, 0:4], dabx[:, :, 0:4], dabe[:, :, 0:4], ALU.add)
        v.reciprocal(cols[:, :, 20:24], dabe[:, :, 4:8])
        v.tensor_scalar(tiny[:, 52:56], tiny[:, 48:52], -1.0, None, ALU.mult)
        v.drain()
        v.tensor_tensor(cols[:, :, 0:4], dabx[:, :, 0:4], tiny[:, 52:56].unsqueeze(1).to_broadcast([P, NT + 1, 4]),
                        ALU.mult).then_inc(dab_g, 1)
        dve.wait_ge(cum_mm, 1)
        c36 = [ps[:, 3, 128 * i:128 * i + 36].rearrange("p (t c) -> p t c", c=4) for i in range(2)]
        v.tensor_copy(cols[:, :, 4:8], c36[0])
        v.tensor_copy(cols[:, :, 16:20], c36[1])
        v.drain()
        v.tensor_tensor(cols[:, :, 12:16], cols[:, :, 16:20], cols[:, :, 4:8], ALU.subtract).then_inc(cols_ok, 1)

        dve.wait_ge(s_full, 1)
        v.tensor_copy(vtok[:, 1:, :], banks(AS).rearrange("p (t c) -> p t c", c=P)).then_inc(s_free, 1)
        dve.wait_ge(p_full, 1)
        v.tensor_copy(vmeta[:], ps[0:META, APB, 0:P]).then_inc(p_free, 1)

        E8, BK, CZ, OE = small[:, 8:16], small[:, 24:28], small[:, 32:36], small[:, 48:52]

        def pre(c, u, L):
            cc = tiny[:, 24 * u:24 * u + 24]
            dve.wait_ge(full[0], filled("ssq", c))
            if not (isinstance(c, int) and c == 0):
                dve.wait_ge(rr_ok, c)
            v.tensor_scalar(E8[0:L], ps[0:L, 5, 0:8], EPS, None, ALU.add).then_inc(free[0], 1)
            dve.wait_ge(full[1], filled("gam", c))
            bl = delta_bank("gam")[0:L, :, 0:L]
            g_col = cc[0:L, 4:8].unsqueeze(2).to_broadcast([L, DH, L])
            v.tensor_tensor(buf["t1"][0:L, :, 0:L], bl, g_col, ALU.subtract).then_inc(free[1], 1)
            v.drain()
            v.tensor_tensor(buf["DT"][0:L, :, 0:L], buf["t1"][0:L, :, 0:L],
                            mask_up[0:L, 0:L].unsqueeze(1).to_broadcast([L, DH, L]), ALU.add).then_inc(a1_ok, 1)
            v.scalar_tensor_tensor(buf["DL"][0:L, :, 0:L], buf["t1"][0:L, :, 0:L], -1.0,
                                   mask_low[0:L, 0:L].unsqueeze(1).to_broadcast([L, DH, L]),
                                   ALU.mult, ALU.add).then_inc(a2_ok, 1)
            v.drain()
            dve.wait_ge(full[2], filled("KK", c))
            dve.wait_ge(dlb_ok, c + 1)
            v.tensor_tensor(buf["t1"][0:L, :, 0:L], delta_bank("KK")[0:L, :, 0:L], buf["DL"][0:L, :, 0:L],
                            ALU.mult).then_inc(free[2], 1)
            if not (isinstance(c, int) and c == 0):
                dve.wait_ge(full[0], filled("KQ", c))
                dve.wait_ge(dt_ok, c + 1)
                v.tensor_tensor(buf["attT"][:], delta_bank("KQ"), buf["DT"][:], ALU.mult).then_inc(free[0], 1)
            dve.wait_ge(rr_ok, c + 1)
            dve.wait_ge(full[1], filled("vT", c))
            v.tensor_tensor(buf["vb"][0:L], delta_bank("vT")[0:L], BK[0:L].unsqueeze(2).to_broadcast([L, DH, P]),
                            ALU.mult).then_inc(free[1], 1)
            dve.wait_ge(full[2], filled("kT", c))
            v.tensor_tensor(buf["kd"][0:L], delta_bank("kT")[0:L],
                            cc[0:L, 12:16].unsqueeze(2).to_broadcast([L, DH, P]), ALU.mult).then_inc(free[2], 1)

        def copy_of(op, c, L=P):
            lane = lane_of(op)
            dve.wait_ge(full[lane], filled(op, c))
            v.tensor_copy(buf[op][0:L, :, 0:L], delta_bank(op)[0:L, :, 0:L]).then_inc(free[lane], 1)

        def add_of(op, prev, c, L=P):
            lane = lane_of(op)
            dve.wait_ge(full[lane], filled(op, c))
            v.tensor_tensor(buf[op][0:L, :, 0:L], delta_bank(op)[0:L, :, 0:L], buf[prev][0:L, :, 0:L],
                            ALU.add).then_inc(free[lane], 1)
            v.drain()

        def invert(c, L):
            copy_of("D4T", c, L)
            dve.wait_ge(m1_ok, c + 1)
            add_of("M2", "M1", c, L)
            add_of("M3", "M2", c, L)
            add_of("M4", "M3", c, L)

        pre(0, 0, META)
        invert(0, META)
        dve.wait_ge(full[2], filled("dS", 0))
        v.tensor_copy(buf["S"][:], delta_bank("dS")).then_inc(free[2], 1)
        v.drain()

        def scores(c, i):
            s = i % 2
            dve.wait_ge(s_full, att_filled(["S00", "S01", "S10", "S11"][i], c))
            dve.wait_ge(p_full, (c - 1) * 2 + (1 if i < 2 else 2))
            pb = prob[:, s]
            v.tensor_tensor(pb, ps[:, AS:AS + 2, 0:META + 2 * P],
                            band_now[:].unsqueeze(1).to_broadcast([P, 2, META + 2 * P]), ALU.add).then_inc(s_free, 1)
            v.drain()
            v.tensor_reduce(tiny[:, 72 + 2 * s:74 + 2 * s], pb, axis=AX.X, op=ALU.max)
            v.drain()
            kh = 4 * (i // 2) + 2 * (i % 2)
            t0 = tiny[:, 72 + 2 * s:74 + 2 * s]
            v.scalar_tensor_tensor(t0, t0, HD ** -0.5, sink[:, kh:kh + 2], ALU.mult, ALU.max)
            v.drain()
            v.tensor_scalar(tiny[:, 56 + 4 * s:58 + 4 * s], t0, -1.0, None, ALU.mult)
            v.tensor_tensor(tiny[:, 58 + 4 * s:60 + 4 * s], sink[:, kh:kh + 2], t0, ALU.subtract).then_inc(nm_ok, 1)

        def denominators(c, i):
            s = i % 2
            dve.wait_ge(ex_ok, (c - 1) * 4 + (i + 1))
            v.tensor_tensor(tiny[:, 76 + 2 * s:78 + 2 * s], tiny[:, 64 + 4 * s:66 + 4 * s],
                            tiny[:, 66 + 4 * s:68 + 4 * s], ALU.add)
            v.drain()
            v.reciprocal(small[:, 56 + 2 * s:58 + 2 * s], tiny[:, 76 + 2 * s:78 + 2 * s]).then_inc(rec_ok, 1)

        def mixer(c, m, u):
            cc = tiny[:, 24 * u:24 * u + 24]
            scores(c, 0)
            scores(c, 1)
            denominators(c, 0)
            denominators(c, 1)
            scores(c, 2)
            scores(c, 3)
            denominators(c, 2)
            denominators(c, 3)
            v.drain()
            v.tensor_copy(band_now[:], band[:])
            pre(c, u, P)
            invert(c, P)
            copy_of("B2T", c)
            dve.wait_ge(w1_ok, c)
            add_of("W2", "W1", c)
            add_of("W3", "W2", c)
            dve.wait_ge(full[0], filled("KS", c))
            for h in range(DH):
                last = v.scalar_tensor_tensor(buf["Z"][:, h, :], delta_bank("KS")[:, h, :], CZ[:, h:h + 1],
                                              buf["vb"][:, h, :], ALU.mult, ALU.add)
            last.then_inc(free[0], 1)
            dve.wait_ge(full[2], filled("dS", c))
            dve.wait_ge(full[0], filled("P1", c))
            for h in range(DH):
                last = v.scalar_tensor_tensor(buf["S"][:, h, :], buf["S"][:, h, :], cc[:, 16 + h:17 + h],
                                              delta_bank("dS")[:, h, :], ALU.mult, ALU.add)
            last.then_inc(free[2], 1)
            v.tensor_tensor(buf["o1"][:], delta_bank("P1"), cc[:, 8:12].unsqueeze(2).to_broadcast([P, DH, P]),
                            ALU.mult).then_inc(free[0], 1)
            v.drain()
            dve.wait_ge(full[1], filled("P2", c))
            v.tensor_tensor(buf["op"][:], delta_bank("P2"), buf["o1"][:], ALU.add).then_inc(free[1], 1)
            dve.wait_ge(osq_ok, c)
            v.tensor_reduce(OE, buf["osq"][:], axis=AX.X, op=ALU.add).then_inc(ored_ok, 1)
            dve.wait_ge(gz_ok, 1)
            dve.wait_ge(full[2], filled("oT", c))
            v.tensor_tensor(yd[:, :, bass.ds((c - 1) * P, P)], delta_bank("oT"), gz[:, :, bass.ds((c - 1) * P, P)],
                            ALU.mult).then_inc(free[2], 1)
        mixer_steps(dve, mixer)

        for i, src in enumerate((ya, yd)):
            dve.wait_ge(y_h, i + 1)
            v.tensor_tensor(y_lo[:, 4 * i:4 * i + 4, :], src[:], y_hi[:, 4 * i:4 * i + 4, :].bitcast(F32),
                            ALU.subtract).then_inc(y_l, 1)

        def merge_mul(n, m, u):
            split_lo(*after(n, m, u))
            v.drain()
            dve.wait_ge(mm_done, n + 1)
            dve.wait_ge(gate_in[u], (m - N_MERGE // 2 + 1) * 32)
            v.tensor_tensor(mt[:, 0, :], banks(4 * u), gin[:, u, 0, :], ALU.mult)
            v.tensor_tensor(mt[:, 1, :], banks(4 * u + 2), gin[:, u, 1, :], ALU.mult).then_inc(evac[u], 1)
            dve.wait_ge(m_h, n - N_MERGE + 1)
            v.tensor_tensor(m_lo[:, bass.ds(n - N_MERGE, 1), :].rearrange("p a c -> p (a c)"), mt[:, 0, :],
                            m_hi[:, bass.ds(n - N_MERGE, 1), :].rearrange("p a c -> p (a c)").bitcast(F32),
                            ALU.subtract).then_inc(m_l, 1)
        steps(dve, N_MERGE, N_OUT, merge_mul)
        steps(dve, N_OUT, N_FF, lambda n, m, u: split_lo(*after(n, m, u)))

        def rms(r):
            dve.wait_ge(n_mm, r)
            v.tensor_scalar(small[:, 8:16], ps[:, 7, 0:8], 1.0 / D, EPS, ALU.mult, ALU.add).then_inc(n_add, 1)
            dve.wait_ge(n_pow, r)
            v.tensor_tensor(sqt[:].rearrange("p (t c) -> p t c", c=P), ident[:].unsqueeze(1).to_broadcast([P, NT, P]),
                            small[:, 0:8].unsqueeze(2).to_broadcast([P, NT, P]), ALU.mult).then_inc(n_dg, 1)
            dve.wait_ge(n_bc, r)
            v.tensor_copy(rb[:], banks(5)).then_inc(n_rb, 1)
            v.drain()
        rms(1)
        for k in range(KT):
            v.scalar_tensor_tensor(oT[:, k, :], oT[:, k, :], params[:, R_POST + k:R_POST + k + 1], rb[:],
                                   ALU.mult, ALU.mult)
            dve.wait_ge(xt_ps, k + 1)
            v.drain()
            v.tensor_tensor(oT[:, k, :], oT[:, k, :], banks(2 * (k % 2)), ALU.add).then_inc(x2_ok, 1)
        rms(2)
        for k in range(KT):
            if k >= 2:
                dve.wait_ge(f_l, k - 1)
            v.scalar_tensor_tensor([sg, up][k % 2][:], oT[:, k, :], params[:, R_FPRE + k:R_FPRE + k + 1], rb[:],
                                   ALU.mult, ALU.mult).then_inc(fw, 1)
        n0, done = N_FF, 0
        for gi, sz in enumerate(FF_GROUPS):
            def prod(n, m, u, n0=n0, done=done):
                split_lo(*after(n, m, u))
                if u == 1:
                    j = m - n0 // 2
                    dve.wait_ge(mm_done, n + 1)
                    dve.wait_ge(sg_ok, j + (done + 1))
                    wait(dve, u_l, j + done)
                    v.tensor_tensor(up[:], banks(4), sg[:], ALU.mult).then_inc(up_ok, 1)
                    v.drain().then_inc(evac[1], 1)
            steps(dve, n0, n0 + 2 * sz, prod, peel=2)
            n1 = n0 + 2 * sz

            def down(n, m, u, n1=n1, gi=gi, split=True):
                if split:
                    split_lo(*after(n, m, u))
                dve.wait_ge(mm_done, n + 1)
                dst = facc[:, bass.ds(n - n1, 1), :].rearrange("p a c -> p (a c)")
                if gi == 0:
                    if isinstance(n, int) and n == n1:
                        dve.wait_ge(x2_st, 16)
                    last = v.tensor_copy(dst, banks(4 * u))
                else:
                    last = v.tensor_tensor(dst, dst, banks(4 * u), ALU.add)
                last.then_inc(evac[u], 1)
                if gi == 2:
                    v.drain().then_inc(fa_ok, 1)
            if gi == 0:
                steps(dve, n1, n1 + KT, down, peel=2)
            elif gi == 1:
                v.drain()
                steps(dve, n1, n1 + KT, down)
            else:
                v.drain()
                steps(dve, n1, n1 + KT - 2, down)
                down(n1 + KT - 2, (n1 + KT - 2) // 2, 0)
                down(n1 + KT - 1, (n1 + KT - 1) // 2, 1, split=False)
            done += sz
            n0 = n1 + KT
        rms(3)
        dve.wait_ge(x2_back, 16)
        for k in range(KT):
            v.scalar_tensor_tensor(facc[:, k, :], facc[:, k, :], params[:, R_FPOST + k:R_FPOST + k + 1], rb[:],
                                   ALU.mult, ALU.mult)
            v.drain()
            v.tensor_tensor(facc[:, k, :], facc[:, k, :], x2b[:, k, :], ALU.add).then_inc(x3_ok, 1)

    @block.tensor
    def _(pe):
        pe.wait_ge(consts, 1)
        pe.wait_ge(par_in, 160)
        TR(ps[:, 7, 0:NROWS], prow[0:NROWS, :], ident[0:NROWS, 0:NROWS]).then_inc(par_tr, 1)

        def x_tile(t, m, u, w=P):
            pe.wait_ge(x_nrm, t + 1)
            wait(pe, x_wt, t)
            if isinstance(t, int) and t == 0:
                pe.wait_ge(par_ok, 1)
            for k in range(KT):
                last = TR(banks(4)[:, k * w:(k + 1) * w], xn[0:w, u, k * P:(k + 1) * P], ident[0:w, 0:w])
            last.then_inc(x_tr, 1)
        x_tile(0, 0, 0, META)
        steps(pe, 1, NT + 1, x_tile)
        pe.wait_ge(x_lo, NT + 1)
        for n in range(2):
            dense(n, 0, n, h_hi, h_lo, META, meta_cols=True).then_inc(mm_done, 1)
        steps(pe, N_Q, N_DN, lambda n, m, u: dense(n, m, u, h_hi, h_lo, META).then_inc(mm_done, 1))
        steps(pe, N_DN, N_DZ, lambda n, m, u: dense(n, m, u, h_hi, h_lo, META, meta_cols=True).then_inc(mm_done, 1))
        pe.wait_ge(wd_l, 1)
        for t in range(NT + 1):
            c = max(0, META + (t - 1) * P)
            for k in range(KT):
                for i, (h, w) in enumerate(((h_hi, wd_hi), (h_hi, wd_lo), (h_lo, wd_hi))):
                    last = MM(ps[:, 3, 8 * t:8 * t + 8], h[:, k, c:c + P], w[:, k, :],
                              start=(k == 0 and i == 0), stop=(k == KT - 1 and i == 2))
        last.then_inc(dab_mm, 1)
        steps(pe, N_DZ, N_MERGE, lambda n, m, u: dense(n, m, u, h_hi, h_lo, META).then_inc(mm_done, 1))

        for u in range(2):
            pe.wait_ge(evac[u], N_MERGE // 2)
        pe.wait_ge(consts, 2)
        pe.wait_ge(dab_g, 1)
        g_all = cols[:, :, 0:4]
        MM(ps[:, 3, 0:36].rearrange('p (t c) -> p t c', c=4), upper[:], g_all, start=True, stop=True)
        MM(ps[:, 3, 128 + 4:128 + 36].rearrange('p (t c) -> p t c', c=4), ones[:], cols[:, 1:, 0:4], start=True, stop=True)
        MM(ps[:, 3, 128:128 + 4], ones[0:META, :], cols[0:META, 0, 0:4], start=True, stop=True).then_inc(cum_mm, 1)
        for t in range(NT):
            last = TR(banks(AS)[:, t * P:(t + 1) * P], av[:, P + t * P:2 * P + t * P], ident[:])
        last.then_inc(s_full, 1)
        TR(ps[0:META, APB, 0:P], av[:, P - META:P], ident[:]).then_inc(p_full, 1)

        def fill(op, c, L, make, *waits):
            lane = lane_of(op)
            pe.wait_ge(free[lane], filled(op, c) - 1) if not (isinstance(c, int) and filled(op, c) == 1) else None
            for s, value in waits:
                pe.wait_ge(s, value)
            for h in range(DH):
                last = make(h)
            last.then_inc(full[lane], 1)

        def ready(op, c):
            return free[lane_of(op)], filled(op, c)

        def delta_pre(c, u, L):
            q = lambda t: qkv[:, u, t, 0:L]
            X = lambda k, h: buf[k][0:L, h, 0:L]
            bank = lambda op, h: delta_bank(op)[0:L, h, 0:L]

            def prod(op, lhsT, rhs, *waits):
                fill(op, c, L, lambda h: MM(bank(op, h), X(lhsT, h), X(rhs, h), start=True, stop=True), *waits)
            lane = lane_of("ssq")
            if not (isinstance(c, int) and c == 0):
                pe.wait_ge(free[lane], filled("ssq", c) - 1)
            pe.wait_ge(sq_ok, c + 1)
            for t in range(8):
                last = MM(ps[0:L, 5, t:t + 1], sq[:, t, 0:L], ones[:, 0:1], start=True, stop=True)
            last.then_inc(full[lane], 1)
            cc = tiny[:, 24 * u:24 * u + 24]
            fill("gam", c, L, lambda h: MM(bank("gam", h), cc[0:L, h:h + 1].to_broadcast([L, L]), upper[0:L, 0:L],
                                           start=True, stop=True))
            fill("KK", c, L, lambda h: MM(bank("KK", h), q(4 + h), q(4 + h), start=True, stop=True))
            if not (isinstance(c, int) and c == 0):
                fill("KQ", c, L, lambda h: MM(bank("KQ", h), q(4 + h), q(h), start=True, stop=True))
            fill("vT", c, L, lambda h: TR(delta_bank("vT")[0:L, h, :], q(8 + h), ident[:]))
            fill("kT", c, L, lambda h: TR(delta_bank("kT")[0:L, h, :], q(4 + h), ident[:]))
            fill("DnT", c, L, lambda h: TR(bank("DnT", h), X("Dn", h), ident[0:L, 0:L]), (de_ok, c + 1))
            prod("D2", "DnT", "Dn", ready("DnT", c))
            prod("D2T", "Dn", "DnT")
            prod("D4", "D2T", "D2", ready("D2", c), ready("D2T", c))
            prod("D4T", "D2", "D2T")
            prod("M2", "D2", "M1", (m1_ok, c + 1))
            prod("D8", "D4T", "D4", ready("D4", c), ready("D4T", c))
            prod("M3", "D4", "M2", ready("M2", c))
            prod("M4", "D8", "M3", ready("D8", c), ready("M3", c))

        def delta_solve(c, u):
            X = lambda k, h: buf[k][:, h, :]

            def prod(op, lhsT, rhs, *waits):
                fill(op, c, P, lambda h: MM(delta_bank(op)[:, h, :], X(lhsT, h), X(rhs, h), start=True, stop=True),
                     *waits)
            fill("Ninv", c, P, lambda h: TR(delta_bank("Ninv")[:, h, :], X("M4", h), ident[:]), ready("M4", c))
            prod("B", "M4", "En")
            prod("BT", "En", "M4")
            prod("B2", "BT", "B", ready("B", c), ready("BT", c))
            prod("B2T", "B", "BT")
            prod("W2", "B2", "W1", ready("B2", c), (w1_ok, c))
            prod("B4", "B2T", "B2", ready("B2T", c))
            prod("W3", "B4", "W2", ready("B4", c), ready("W2", c))
            prod("TT", "Ninv", "W3", ready("Ninv", c), ready("W3", c))

        def delta_scan(c, u):
            X = lambda k, h: buf[k][:, h, :]
            q = lambda t: qkv[:, u, t, :]

            def prod(op, lhsT, rhs, *waits):
                fill(op, c, P, lambda h: MM(delta_bank(op)[:, h, :], lhsT(h), rhs(h), start=True, stop=True), *waits)
            S = lambda h: X("S", h)
            prod("KS", lambda h: q(4 + h), S)
            prod("VN", lambda h: X("TT", h), lambda h: X("Z", h), ready("TT", c), ready("KS", c))
            prod("dS", lambda h: X("kd", h), lambda h: X("vn", h), ready("VN", c))
            prod("P1", lambda h: q(h), S)
            prod("P2", lambda h: X("attT", h), lambda h: X("vn", h))
            fill("oT", c, P, lambda h: TR(delta_bank("oT")[:, h, :], X("on", h), ident[:]), (on_ok, c))

        def score(c, i):
            op = ["S00", "S01", "S10", "S11"][i]
            kv, j0 = i // 2, 2 * (i % 2)
            pe.wait_ge(s_free, att_filled(op, c) - 1)
            if i == 0:
                pe.wait_ge(win_ok, c)
            r = slice(kv * HD, (kv + 1) * HD)
            for j in range(2):
                last = MM(ps[:, AS + j, 0:META + 2 * P], qblk[r, j0 + j, :], kwin[r, :], start=True, stop=True)
            last.then_inc(s_full, 1)

        def prob_T(c, i):
            kv, j0 = i // 2, 2 * (i % 2)
            if i % 2 == 0:
                pe.wait_ge(p_free, (c - 1) * 2 + (kv + 1))
            pe.wait_ge(pr_ok, (c - 1) * 4 + (i + 1))
            for j in range(2):
                o = slice((j0 + j) * P, (j0 + j + 1) * P)
                TR(ps[0:META, APB, o], prob[:, i % 2, j, 0:META], ident[:])
                for b in range(2):
                    last = TR(ps[:, APB + 1 + b, o], prob[:, i % 2, j, META + b * P:META + (b + 1) * P], ident[:])
            if i % 2:
                last.then_inc(p_full, 1)

        def att_out(c, kv):
            op = f"O{kv}"
            pe.wait_ge(s_free, att_filled(op, c) - 1)
            pe.wait_ge(p_free, (c - 1) * 2 + (kv + 2))
            r = slice(kv * HD, (kv + 1) * HD)
            MM(ps[r, AS, :], vmeta[:, r], pt[0:META, 0, :], start=True, stop=False)
            MM(ps[r, AS, :], vwin[:, 0, r], pt[:, 1, :], start=False, stop=False)
            MM(ps[r, AS, :], vwin[:, 1, r], pt[:, 2, :], start=False, stop=True).then_inc(s_full, 1)

        delta_pre(0, 0, META)
        fill("VN", 0, META, lambda h: MM(delta_bank("VN")[0:META, h, :], buf["M4"][0:META, h, 0:META],
                                         buf["vb"][0:META, h, :], start=True, stop=True), ready("M4", 0))
        fill("dS", 0, META, lambda h: MM(delta_bank("dS")[:, h, :], buf["kd"][0:META, h, :],
                                         buf["vn"][0:META, h, :], start=True, stop=True), ready("VN", 0))

        def mixer(c, m, u):
            score(c, 0)
            score(c, 1)
            prob_T(c, 0)
            prob_T(c, 1)
            att_out(c, 0)
            score(c, 2)
            score(c, 3)
            prob_T(c, 2)
            prob_T(c, 3)
            att_out(c, 1)
            delta_pre(c, u, P)
            delta_solve(c, u)
            delta_scan(c, u)
        mixer_steps(pe, mixer)

        pe.wait_ge(y_l, 2)

        def merge(n, m, u):
            wait(pe, w_lo, n + 1)
            wait(pe, evac[u], m)
            dense(n, m, u, y_hi, y_lo, 0, ks=range(0, 4), bank=0)
            dense(n, m, u, y_hi, y_lo, 0, ks=range(4, 8), bank=2).then_inc(mm_done, 1)
        steps(pe, N_MERGE, N_OUT, merge)
        pe.wait_ge(m_l, KT)
        steps(pe, N_OUT, N_FF, lambda n, m, u: dense(n, m, u, m_hi, m_lo, 0).then_inc(mm_done, 1))

        def rms(r, slot_tiles):
            for u in range(2):
                pe.wait_ge(evac[u], slot_tiles)
            pe.wait_ge(o_acc, r * KT)
            for t in range(NT):
                last = MM(ps[:, 7, t:t + 1], acc[:, t * P:(t + 1) * P], ones[:, 0:1], start=True, stop=True)
            last.then_inc(n_mm, 1)
            pe.wait_ge(n_dg, r)
            for b in range(2):
                last = MM(ps[:, 5 + b, :], ones[:], sqt[:, b * HALF:(b + 1) * HALF], start=True, stop=True)
            last.then_inc(n_bc, 1)
        rms(1, N_FF // 2)
        pe.wait_ge(xt_in, 16)
        for k in range(KT):
            if k >= 2:
                pe.wait_ge(x2_ok, k - 1)
            for t in range(NT):
                last = TR(banks(2 * (k % 2))[:, t * P:(t + 1) * P], xtok[:, t, k * P:(k + 1) * P], ident[:])
            last.then_inc(xt_ps, 1)
        rms(2, N_FF // 2)
        pe.wait_ge(f_l, KT)
        pe.wait_ge(x2_ok, KT)
        pe.wait_ge(n_rb, 2)
        n0, done = N_FF, 0
        for gi, sz in enumerate(FF_GROUPS):
            steps(pe, n0, n0 + 2 * sz, lambda n, m, u: dense(n, m, u, f_hi, f_lo, 0).then_inc(mm_done, 1))
            done += sz
            pe.wait_ge(u_l, done)
            n1 = n0 + 2 * sz
            steps(pe, n1, n1 + KT, lambda n, m, u: dense(n, m, u, u_hi, u_lo, 0, nk=sz).then_inc(mm_done, 1))
            n0 = n1 + KT
        rms(3, n0 // 2)
        pe.wait_ge(n_rb, 3)
        pe.wait_ge(x3_ok, KT)

        def out_T(t, m, u):
            if not (isinstance(t, int) and t < 2):
                pe.wait_ge(ot_ok, t - 1)
            for k in range(KT):
                last = TR(banks(2 * u)[:, k * P:(k + 1) * P], facc[:, k, t * P:(t + 1) * P], ident[:])
            last.then_inc(ot_ps, 1)
        for t in range(NT):
            out_T(t, t // 2, t % 2)

    block.__exit__(None, None, None)


_INS = ["x", "meta_tokens", "w_in", "b_in", "conv_w", "a_log", "dt_bias", "dn_norm_w", "att_sinks", "w_att_out",
        "w_dn_out", "w_out", "norm_mix_pre", "norm_mix_post", "norm_ffn_pre", "norm_ffn_post", "w_ffn_in", "w_ffn_out"]


def kernel(**inputs):
    import numpy as _np
    import concourse.bacc as _bacc
    from concourse import mybir as _mybir
    from concourse.bass_utils import run_bass_kernel_spmd as _run

    nc = _bacc.Bacc("TRN2", target_bir_lowering=False, num_devices=1)
    arrays, args = {}, []
    for name in _INS:
        a = _np.ascontiguousarray(inputs[name])
        if name != "meta_tokens":
            a = a[0]
        arrays[f"in_{name}"] = a
        args.append(nc.dram_tensor(f"in_{name}", a.shape, _mybir.dt.from_np(a.dtype), kind="ExternalInput").ap())
    result = nc.dram_tensor("out_0", (1, TOK, D), _mybir.dt.float32, kind="ExternalOutput").ap()
    build(nc, *args, result[0])
    r = _run(nc, [arrays], core_ids=[0])
    return r.results[0]["out_0"]
```

```python
import concourse.bass as bass
from concourse import mybir
import numpy as np

F32 = mybir.dt.float32
F32R = mybir.dt.float32r
ACT = mybir.ActivationFunctionType
ALU = mybir.AluOpType
AX = mybir.AxisListType

P = 128
D = 1024
KT = D // P
TOK = 1024
NT = TOK // P
META = 16
LW = META + TOK
HALF = 512
FF = 2816
EPS = 1e-6
NEG = -1.0e30
DH = 4
HD = 64
GRP = 4
Q0, K0, V0, DN0, DZ0, DAB0, G0 = 0, 512, 640, 768, 2304, 2816, 2824

N_KV, N_Q, N_DN, N_DZ, N_G, N_MERGE, N_OUT, N_FF = 0, 2, 6, 18, 22, 38, 46, 54
FF_GROUPS = [8, 8, 6]
R_BIAS, R_BG, R_PRE, R_POST, R_FPRE, R_FPOST, R_DNW, R_CONV = 0, 22, 38, 46, 54, 62, 70, 71
NROWS = R_CONV + 48

DELTA_OPS = [("KS", 0), ("P1", 1), ("DnT", 2), ("D2", 0), ("D2T", 1), ("VN", 2), ("D4", 0), ("D4T", 1), ("M2", 2),
             ("dS", 0), ("D8", 1), ("P2", 2), ("M3", 0), ("M4", 1), ("B", 2), ("BT", 0), ("ssq", 1), ("gam", 2),
             ("oT", 0), ("B2", 1), ("B2T", 2), ("Ninv", 0), ("KK", 1), ("W2", 0), ("B4", 2), ("KQ", 0), ("W3", 2),
             ("vT", 0), ("TT", 2), ("kT", 0)]
SCAN = ["KS", "VN", "P1", "dS", "P2", "oT"]
FRONT = ["ssq", "gam", "KK", "KQ", "vT", "kT"]
META_OPS = ["ssq", "gam", "KK", "vT", "kT", "DnT", "D2", "D2T", "D4", "D4T", "M2", "D8", "M3", "M4", "VN", "dS"]
ATT_OPS = ["S00", "S01", "O0", "S10", "S11", "O1"]


def lane_of(op):
    return dict(DELTA_OPS)[op]


def ops_in(step, lane):
    every = [o for o, l in DELTA_OPS if l == lane]
    front = [o for o in every if o in FRONT]
    scan = [o for o in every if o in SCAN]
    if step == 0:
        return [(o, 0) for o in META_OPS if lane_of(o) == lane] + [(o, 1) for o in front]
    if step == NT + 1:
        return [(o, NT) for o in scan]
    part = [o for o in every if (step > 1 or o not in scan) and (step < NT or o not in front)]
    return [(o, step + (o in front) - (o in scan)) for o in part]


def filled(op, c):
    lane = lane_of(op)
    if isinstance(c, int):
        order = [o for step in range(NT + 2) for o in ops_in(step, lane)]
        return order.index((op, c)) + 1
    step = c + (op in SCAN) - (op in FRONT)
    every = [o for o, l in DELTA_OPS if l == lane]
    done = len(ops_in(0, lane)) + len(ops_in(1, lane))
    return (step - 2) * len(every) + (done + every.index(op) + 1)


def att_filled(op, c):
    return (c - 1) * len(ATT_OPS) + (ATT_OPS.index(op) + 2)


def build(nc, x, meta, w_in, b_in, conv_w, a_log, dt_bias, dn_norm_w, att_sinks, w_att, w_dn, w_out,
          n_pre, n_post, f_pre, f_post, w_fi, w_fo, out):
    qkv_d = nc.dram_tensor("qkv_scratch", [12, P, LW], F32, kind="Internal").ap()
    gate_d = nc.dram_tensor("gate_scratch", [16, P, TOK], F32, kind="Internal").ap()
    x2_d = nc.dram_tensor("x2_scratch", [8, P, TOK], F32, kind="Internal").ap()

    top = [(nc.sbuf_base + 31) // 32 * 32]

    def at(name, shape, dt, offset):
        t = nc.alloc_sbuf_tensor_at(name, shape, dt, offset=offset)
        return t

    def keep(name, shape, dt=F32):
        size = 4 * int(np.prod(shape[1:]))
        t = at(name, shape, dt, top[0])
        top[0] += (size + 31) // 32 * 32
        return t

    def region(start, size):
        cur = [start]

        def take(name, shape, dt=F32):
            n = 4 * int(np.prod(shape[1:]))
            t = at(name, shape, dt, cur[0])
            cur[0] += (n + 31) // 32 * 32
            assert cur[0] <= start + size, (name, cur[0] - start, size)
            return t
        return take

    raw = keep("w_raw", [P, 2, KT, P])
    whi = keep("w_hi", [P, 2, KT, P], F32R)
    wlo = keep("w_lo", [P, 2, KT, P], F32R)
    ident = keep("ident", [P, P])
    upper = keep("upper_ones", [P, P])
    ones = keep("ones", [P, P])
    mask_up = keep("mask_up", [P, P])
    mask_low = keep("mask_low", [P, P])
    blocks16 = keep("blocks16", [P, P])
    band = keep("band", [P, META + 2 * P])
    band_now = keep("band_now", [P, META + 2 * P])
    params = keep("params", [P, P])
    wd_raw = keep("wd_raw", [P, KT, 8])
    wd_hi = keep("wd_hi", [P, KT, 8], F32R)
    wd_lo = keep("wd_lo", [P, KT, 8], F32R)
    dab_b = keep("dab_bias", [P, 8])
    dtb = keep("dt_bias_bc", [P, 4])
    alog = keep("a_log_bc", [P, 4])
    sink = keep("sink_bc", [P, 8])
    half = keep("minus_half", [P, 1])
    cols = keep("cols", [P, NT + 1, 24])
    tiny = keep("tiny", [P, 96])
    small = keep("small", [P, 96])
    dabx = keep("dab", [P, NT + 1, 8])
    dabe = keep("dab_exp", [P, NT + 1, 8])
    R0 = top[0]
    R1 = R0 + 2 * KT * LW * 4
    R2 = R1 + 65536
    R3 = R2 + 32768
    end = nc.sbuf_usable_end
    assert end - R3 >= 12288, (end, R3, end - R3)

    take = region(R0, R1 - R0)
    h_hi = take("h_hi", [P, KT, LW], F32R)
    h_lo = take("h_lo", [P, KT, LW], F32R)
    take = region(R1, R2 - R1)
    aq = take("att_q", [P, GRP, TOK])
    ak = take("att_k", [P, P + TOK])
    av = take("att_v", [P, P + TOK])
    vtok = take("att_v_tokens", [P, NT + 1, P])
    gz = take("dn_gate", [P, DH, TOK])
    kwin = take("k_window", [P, 2, META + 2 * P])
    qblk = take("q_block", [P, 2, GRP, P])
    vwin = [take("v_window0", [P, 2, P])]
    vmeta = take("v_meta", [META, P])
    prob = take("prob", [P, 2, 2, META + 2 * P])
    pt = take("prob_T", [P, 3, GRP * P])
    take = region(R2, R3 - R2)
    xin = take("x_in", [P, 2, D])
    xn = take("x_norm", [P, 2, D])
    xw = take("x_weighted", [P, 1, D])
    prow = take("param_rows", [P, P])
    take = region(R2, R3 - R2)
    rawc = take("conv_in", [P, 2, 3 + LW])
    cv = take("conv_sum", [P, 2, LW])
    cs = take("stored", [P, 2, LW])
    take = region(R0, R1 - R0)
    qkv = take("qkv", [P, 2, 12, P])
    sq = take("qk_squares", [P, 8, P])
    names = ["X1", "X2", "X3", "X4", "X5", "X6", "X7", "X8", "En", "Ninv", "TT0", "t1", "DT", "DL", "attT0",
             "vb0", "kd0", "Z", "vn", "o1", "op", "osq", "on", "S"]
    buf = {k: take("b_" + k, [P, DH, P]) for k in names}
    vwin.append(take("v_window1", [P, 2, P]))
    where = dict(Dn="X1", B="X1", DnT="X2", BT="X2", D2="X3", D8="X3", B2="X3", D2T="X4", B2T="X4", D4="X5",
                 B4="X5", D4T="X6", M1="X7", M3="X7", W1="X7", W3="X7", M2="X8", M4="X8", W2="X8")
    for k, v in where.items():
        buf[k] = buf[v]
    take = region(R3, end - R3)
    buf.update({k: take("b_" + k, [P, DH, P]) for k in ("TT1", "attT1", "vb1", "kd1")})
    take = region(R2, R3 - R2)
    ya = take("y_att", [P, GRP, TOK])
    yd = take("y_dn", [P, DH, TOK])
    take = region(R0, R1 - R0)
    y_hi = take("y_hi", [P, KT, TOK], F32R)
    y_lo = take("y_lo", [P, KT, TOK], F32R)
    take = region(R1, R2 - R1)
    m_hi = take("m_hi", [P, KT, TOK], F32R)
    m_lo = take("m_lo", [P, KT, TOK], F32R)
    take = region(R2, R3 - R2)
    gin = take("gates_in", [P, 2, 2, TOK])
    mt = take("merge_parts", [P, 2, TOK])
    take = region(R2, R3 - R2)
    oT = take("o_T", [P, KT, TOK])
    take = region(R3, end - R3)
    sqt = take("square", [P, TOK])
    acc = take("square_sum", [P, TOK])
    rb = take("rms_bc", [P, TOK])
    take = region(R0, R1 - R0)
    xtok = take("x_tokens", [P, NT, D])
    take = region(R0, R1 - R0)
    f_hi = take("f_hi", [P, KT, TOK], F32R)
    f_lo = take("f_lo", [P, KT, TOK], F32R)
    take = region(R1, R2 - R1)
    u_hi = take("u_hi", [P, KT, TOK], F32R)
    u_lo = take("u_lo", [P, KT, TOK], F32R)
    take = region(R2, R3 - R2)
    facc = take("ffn_sum", [P, KT, TOK])
    take = region(R3, end - R3)
    sg = take("silu_gate", [P, TOK])
    up = take("hidden", [P, TOK])
    take = region(R0, R1 - R0)
    x2b = take("x2_back", [P, KT, TOK])
    otile = take("out_tile", [P, 4, D])

    ps = nc.alloc_psum_tensor("ps", [P, 8, HALF], F32)
    AS, APB = 0, 2

    def sem(name):
        return nc.alloc_semaphore(name)

    raw_in = [sem("raw_in0"), sem("raw_in1")]
    w_hi, w_lo = sem("w_hi"), sem("w_lo")
    mm_done = sem("mm_done")
    evac = [sem("evac0"), sem("evac1")]
    x_in = [sem("x_in0"), sem("x_in1")]
    x_sum, x_rs, x_nrm, x_tr, x_wt, x_hi, x_lo = (sem("x_sum"), sem("x_rs"), sem("x_nrm"), sem("x_tr"), sem("x_wt"),
                                                  sem("x_hi"), sem("x_lo"))
    par_in, par_tr, par_ok, wd_in, wd_h, wd_l = (sem("par_in"), sem("par_tr"), sem("par_ok"), sem("wd_in"),
                                                 sem("wd_h"), sem("wd_l"))
    consts, bc_in = sem("consts"), sem("bc_in")
    conv_in, conv_ok, silu_ok = sem("conv_in"), sem("conv_ok"), sem("silu_ok")
    dz_ok, gz_ok = sem("dz_ok"), sem("gz_ok")
    stored = [sem("stored0"), sem("stored1")]
    dab_mm, dab_add, dab_act, dab_g, cum_mm, cols_ok = (sem("dab_mm"), sem("dab_add"), sem("dab_act"), sem("dab_g"),
                                                        sem("cum_mm"), sem("cols_ok"))
    full = [sem("lane0_full"), sem("lane1_full"), sem("lane2_full")]
    free = [sem("lane0_read"), sem("lane1_read"), sem("lane2_read")]
    s_full, s_free, p_full, p_free = sem("score_full"), sem("score_read"), sem("probT_full"), sem("probT_read")
    qkv_in = [sem("qkv_in0"), sem("qkv_in1")]
    sq_ok, rr_ok, a1_ok, a2_ok, dt_ok, dl_ok, dlb_ok, de_ok, m1_ok, w1_ok, dn_ok = (
        sem("sq_ok"), sem("rr_ok"), sem("a1_ok"), sem("a2_ok"), sem("dt_ok"), sem("dl_ok"), sem("dlb_ok"),
        sem("de_ok"), sem("m1_ok"), sem("w1_ok"), sem("dn_ok"))
    o_ok, osq_ok, ored_ok, of_ok, on_ok = sem("o_ok"), sem("osq_ok"), sem("ored_ok"), sem("of_ok"), sem("on_ok")
    win_ok, sc_ok, nm_ok, ex_ok, rec_ok, pr_ok = (sem("win_ok"), sem("sc_ok"), sem("nm_ok"), sem("ex_ok"),
                                                  sem("rec_ok"), sem("pr_ok"))
    pcopy = sem("pcopy")
    y_h, y_l, gate_in = sem("y_h"), sem("y_l"), [sem("gate_in0"), sem("gate_in1")]
    mrg, m_h, m_l = sem("mrg"), sem("m_h"), sem("m_l")
    o_sq, o_acc, xt_in = sem("o_sq"), sem("o_acc"), sem("xt_in")
    n_mm, n_add, n_pow, n_dg, n_bc, n_rb = (sem("n_mm"), sem("n_add"), sem("n_pow"), sem("n_dg"), sem("n_bc"),
                                            sem("n_rb"))
    xt_ps, x2_ok, x2_st, fw, f_h, f_l = (sem("xt_ps"), sem("x2_ok"), sem("x2_st"), sem("fw"), sem("f_h"),
                                         sem("f_l"))
    sg_ok, up_ok, u_h, u_l = sem("sg_ok"), sem("up_ok"), sem("u_h"), sem("u_l")
    fa_ok, x2_back, x3_ok, ot_ps, ot_ok, out_st = (sem("fa_ok"), sem("x2_back"), sem("x3_ok"), sem("ot_ps"),
                                                   sem("ot_ok"), [sem("out_st0"), sem("out_st1")])

    TR = nc.tensor.transpose
    MM = nc.tensor.matmul

    def wait(eng, s, value):
        if isinstance(value, int) and value <= 0:
            return
        eng.wait_ge(s, value)

    def settle(eng):
        eng.wait_ge(consts, 1)

    def steps(eng, first, last, body, peel=0):
        for n in range(first, first + peel):
            body(n, n // 2, n % 2)
        s = first + peel
        if s == last:
            return
        assert (last - s) % 2 == 0
        if last - s == 2:
            for n in (s, s + 1):
                body(n, n // 2, n % 2)
            return
        with eng.Fori(0, (last - s) // 2) as i:
            for u in (0, 1):
                body(i * 2 + (s + u), i + (s + u) // 2, (s + u) % 2)

    def mixer_steps(eng, step, scan):
        step(1, 0, 1, False, True)
        steps(eng, 2, NT, lambda c, m, u: step(c, m, u, True, True))
        step(NT, NT // 2, NT % 2, True, False)
        scan(NT, NT % 2)

    def delta_bank(op):
        return ps[:, 5 + lane_of(op), :].rearrange("p (h c) -> p h c", h=DH)

    def banks(b, n=2):
        return ps[:, b:b + n, :].rearrange("p a b -> p (a b)")

    def split_hi(n1, m1, u1):
        wait(nc.scalar, raw_in[u1], (m1 + 1) * 48)
        wait(nc.scalar, mm_done, n1 - 1)
        nc.scalar.activation(whi[:, u1], raw[:, u1], ACT.Copy).then_inc(w_hi, 1)

    def split_lo(n1, m1, u1):
        wait(nc.vector, w_hi, n1 + 1)
        nc.vector.tensor_tensor(wlo[:, u1], raw[:, u1], whi[:, u1].bitcast(F32), ALU.subtract).then_inc(w_lo, 1)

    def after(n, m, u):
        return (n + 1, m + u, 1 - u)

    def dense(n, m, u, hi, lo, c0, nk=KT, meta_cols=False, ks=None, bank=0):
        if ks is None:
            wait(nc.tensor, w_lo, n + 1)
            wait(nc.tensor, evac[u], m)
            ks = list(range(nk))
        last = None
        groups = [(4 * u + bank + b, c0 + b * HALF, HALF) for b in range(2)]
        if meta_cols:
            groups.append((4 * u + 2, 0, META))
        for b, c, w in groups:
            for k in ks:
                for i, (a, mv) in enumerate(((whi, hi), (whi, lo), (wlo, hi))):
                    last = MM(ps[:, b, 0:w], a[:, u, k, :], mv[:, k, c:c + w],
                              start=(k == ks[0] and i == 0), stop=(k == ks[-1] and i == 2))
        return last

    block = nc.Block()
    block.__enter__()

    @block.sync
    def _(sp):
        sp.dma_start(xin[0:META, 0, :], meta).then_inc(x_in[0], 16)
        sp.dma_start(xin[:, 1, :], x[0:P, :]).then_inc(x_in[1], 16)
        bq = b_in[Q0:Q0 + 512].rearrange("(g j c) -> g j c", g=2, c=HD)
        sp.dma_start(prow[0:GRP, 0:HD], bq[0]).then_inc(par_in, 16)
        sp.dma_start(prow[0:GRP, HD:P], bq[1]).then_inc(par_in, 16)
        for dst, cnt, src in ((GRP, 18, b_in[K0:DAB0]), (R_BG, 16, b_in[G0:G0 + 2048]), (R_PRE, 8, n_pre),
                              (R_POST, 8, n_post), (R_FPRE, 8, f_pre), (R_FPOST, 8, f_post), (R_DNW, 1, dn_norm_w),
                              (R_CONV, 48, conv_w.rearrange("k c -> (k c)"))):
            sp.dma_start(prow[dst:dst + cnt, :], src.rearrange("(t p) -> t p", p=P)).then_inc(par_in, 16)

        def load(n, m, u, pieces):
            wait(sp, w_lo, n - 1)
            for dst, src in pieces:
                sp.dma_start(dst, src).then_inc(raw_in[u], 48 // len(pieces))

        def w_cols(w, c):
            return w[:, bass.ds(c, P)].rearrange("(k p) c -> p k c", p=P)

        def kv_w(n, m, u):
            load(n, m, u, [(raw[:, u], w_cols(w_in, (n - N_KV) * P + K0))])

        def q_w2(n, m, u):
            j = n - N_Q
            wait(sp, w_lo, n - 1)
            for g in range(2):
                sp.dma_start(raw[:, u, :, g * HD:(g + 1) * HD],
                             w_in[:, bass.ds(j * HD + g * GRP * HD, HD)].rearrange("(k p) c -> p k c", p=P)
                             ).then_inc(raw_in[u], 16 + 16 * g)

        def dn_w(n, m, u):
            load(n, m, u, [(raw[:, u], w_cols(w_in, (n - N_DN) * P + DN0))])

        def g_w(n, m, u):
            load(n, m, u, [(raw[:, u], w_cols(w_in, (n - N_G) * P + G0))])

        def merge_w(n, m, u):
            wait(sp, w_lo, n - 1)
            c = (n - N_MERGE) * P
            for g in range(2):
                src = w_att[g * GRP * HD:(g + 1) * GRP * HD, bass.ds(c, P)].rearrange("(j p) c -> p j c", p=HD)
                sp.dma_start(raw[g * HD:(g + 1) * HD, u, 0:4, :], src).then_inc(raw_in[u], 16)
            sp.dma_start(raw[:, u, 4:8, :], w_dn[:, bass.ds(c, P)].rearrange("(k p) c -> p k c", p=P)
                         ).then_inc(raw_in[u], 16)

        def out_w(n, m, u):
            load(n, m, u, [(raw[:, u], w_cols(w_out, (n - N_OUT) * P))])

        kv_w(0, 0, 0)
        kv_w(1, 0, 1)
        for dst, src in ((dab_b, b_in[DAB0:DAB0 + 8]), (dtb, dt_bias), (alog, a_log), (sink, att_sinks)):
            sp.dma_start(dst[:], src.rearrange("(a c) -> a c", a=1).to_broadcast([P, src.shape[0]])).then_inc(bc_in, 16)
        sp.dma_start(wd_raw[:], w_in[:, DAB0:DAB0 + 8].rearrange("(k p) c -> p k c", p=P)).then_inc(wd_in, 16)

        def x_load(t, m, u):
            wait(sp, x_nrm, t - 1)
            sp.dma_start(xin[:, u, :], x[bass.ds((t - 1) * P, P), :]).then_inc(x_in[u], 16)
        steps(sp, 2, NT + 1, x_load, peel=1)
        for n in range(N_Q, N_DN):
            q_w2(n, n // 2, n % 2)
        dn_w(N_DN, N_DN // 2, 0)
        dn_w(N_DN + 1, N_DN // 2, 1)

        def store_qkv(j, parity):
            sp.wait_ge(silu_ok, j + 1)
            sp.dma_start(qkv_d[bass.ds(j, 1)].rearrange("a p c -> p (a c)"), cs[:, parity, :]).then_inc(stored[parity], 16)

        def dn_step(n, m, u):
            dn_w(n, m, u)
            store_qkv(n - 2 - N_DN, u)
        steps(sp, N_DN + 2, N_DZ, dn_step)

        def dz_w(n, m, u):
            load(n, m, u, [(raw[:, u], w_cols(w_in, (n - N_DZ) * P + DZ0))])
            if n < N_DZ + 2:
                store_qkv(n - 2 - N_DN, u)
        for n in range(N_DZ, N_G):
            dz_w(n, n // 2, n % 2)
        g_w(N_G, N_G // 2, 0)
        g_w(N_G + 1, N_G // 2, 1)

        def g_step(n, m, u):
            if not (isinstance(n, int) and n >= N_MERGE):
                g_w(n, m, u)
            else:
                merge_w(n, m, u)
            sp.wait_ge(silu_ok, n - 2 - N_G + 13)
            sp.dma_start(gate_d[bass.ds(n - 2 - N_G, 1)].rearrange("a p c -> p (a c)"), cs[:, u, 0:TOK]
                         ).then_inc(stored[u], 16)
        steps(sp, N_G + 2, N_MERGE, g_step)
        g_step(N_MERGE, N_MERGE // 2, 0)
        g_step(N_MERGE + 1, N_MERGE // 2, 1)

        sp.wait_ge(mm_done, N_MERGE)
        for u in range(2):
            sp.wait_ge(stored[u], 16 * 14)
        sp.dma_start(qkv[:, 0, :, 0:META], qkv_d[:, :, 0:META].rearrange("t p c -> p t c")).then_inc(qkv_in[0], 16)

        def chunk_load(c, m, u):
            if isinstance(c, int) and c == 2:
                sp.wait_ge(full[lane_of("dS")], filled("dS", 0))
            elif not (isinstance(c, int) and c == 1):
                wait(sp, full[lane_of("P1")], filled("P1", c - 2))
            sp.dma_start(qkv[:, u], qkv_d[:, :, bass.ds((c - 1) * P + META, P)].rearrange("t p c -> p t c")
                         ).then_inc(qkv_in[u], 16)
        steps(sp, 1, NT + 1, chunk_load, peel=2)

        def gates_load(n, m, u):
            if isinstance(n, int) and n < N_MERGE + 2:
                sp.wait_ge(y_l, 2)
                sp.wait_ge(y_h, 2)
            else:
                sp.wait_ge(mrg, n - N_MERGE - 1)
            j = n - N_MERGE
            for g in range(2):
                sp.dma_start(gin[:, u, g, :], gate_d[bass.ds(j + 8 * g, 1)].rearrange("a p c -> p (a c)")
                             ).then_inc(gate_in[u], 16)
        gates_load(N_MERGE, N_MERGE // 2, 0)
        gates_load(N_MERGE + 1, N_MERGE // 2, 1)

        def merge_step(n, m, u):
            merge_w(n, m, u)
            gates_load(n, m, u)
        steps(sp, N_MERGE + 2, N_OUT, merge_step)
        out_w(N_OUT, N_OUT // 2, 0)
        out_w(N_OUT + 1, N_OUT // 2, 1)
        sp.wait_ge(mm_done, N_OUT)
        sp.dma_start(xtok[:], x.rearrange("(t p) d -> p t d", p=P)).then_inc(xt_in, 16)
        steps(sp, N_OUT + 2, N_FF, out_w)

        def ffn_weights(n0, s0, sz):
            def in_w(n, m, u):
                c = (m - n0 // 2 + s0) * P + u * FF
                load(n, m, u, [(raw[:, u], w_cols(w_fi, c))])

            def out_w2(n, m, u):
                load(n, m, u, [(raw[:, u, 0:sz, :],
                                w_fo[s0 * P:(s0 + sz) * P, bass.ds((n - n0 - 2 * sz) * P, P)]
                                .rearrange("(k p) c -> p k c", p=P))])
            return in_w, out_w2

        n0 = N_FF
        for gi, sz in enumerate(FF_GROUPS):
            in_w, out_w2 = ffn_weights(n0, sum(FF_GROUPS[:gi]), sz)
            if gi == 0:
                in_w(n0, n0 // 2, 0)
                in_w(n0 + 1, n0 // 2, 1)
                sp.wait_ge(x2_ok, KT)
                sp.dma_start(x2_d.rearrange("t p c -> p t c"), oT[:]).then_inc(x2_st, 16)
                steps(sp, n0 + 2, n0 + 2 * sz, in_w)
            else:
                steps(sp, n0, n0 + 2 * sz, in_w)
            steps(sp, n0 + 2 * sz, n0 + 2 * sz + KT, out_w2)
            n0 += 2 * sz + KT
        sp.wait_ge(x2_st, 16)
        sp.wait_ge(mm_done, n0 - KT)
        sp.dma_start(x2b[:], x2_d.rearrange("t p c -> p t c")).then_inc(x2_back, 16)

        def out_store(t, m, u):
            sp.wait_ge(ot_ok, t + 1)
            sp.dma_start(out[bass.ds(t * P, P), :], otile[:, u, :]).then_inc(out_st[u], 16)
        steps(sp, 0, NT, out_store)
        for u in range(2):
            sp.wait_ge(out_st[u], 16 * (NT // 2))

    @block.gpsimd
    def _(pool):
        g = nc.gpsimd
        g.memset(ones[:], 1.0)
        g.memset(half[:], -0.5)
        g.memset(small[:, 4:5], 1.0 / D)
        g.memset(band[:], 0.0)
        g.memset(mask_up[:], 0.0)
        g.memset(mask_low[:], 0.0)
        g.memset(ident[:], 0.0)
        g.memset(upper[:], 1.0)
        g.memset(blocks16[:], 1.0)
        g.memset(ak[:, 0:P - META], 0.0)
        g.memset(av[:, 0:P - META], 0.0)
        g.memset(vtok[:, 0, :], 0.0)
        g.drain()
        g.affine_select(out=ident[:], in_=ident[:], compare_op=ALU.not_equal, fill=1.0, base=0,
                        pattern=[[-1, P]], channel_multiplier=1).then_inc(consts, 1)
        g.affine_select(out=upper[:], in_=upper[:], compare_op=ALU.is_ge, fill=0.0, base=0,
                        pattern=[[1, P]], channel_multiplier=-1)
        g.affine_select(out=mask_up[:], in_=mask_up[:], compare_op=ALU.is_ge, fill=NEG, base=0,
                        pattern=[[1, P]], channel_multiplier=-1)
        g.affine_select(out=mask_low[:], in_=mask_low[:], compare_op=ALU.is_gt, fill=NEG, base=0,
                        pattern=[[-1, P]], channel_multiplier=1)
        b3 = blocks16[:].rearrange("p (b c) -> p b c", c=16)
        g.affine_select(out=b3, in_=b3, compare_op=ALU.is_ge, fill=0.0, base=0,
                        pattern=[[-16, 8], [0, 16]], channel_multiplier=1)
        g.drain()
        g.affine_select(out=b3, in_=b3, compare_op=ALU.is_ge, fill=0.0, base=15,
                        pattern=[[16, 8], [0, 16]], channel_multiplier=-1)
        g.affine_select(out=band[:, META:META + P], in_=band[:, META:META + P], compare_op=ALU.is_gt, fill=NEG,
                        base=0, pattern=[[1, P]], channel_multiplier=-1)
        g.affine_select(out=band[:, META + P:], in_=band[:, META + P:], compare_op=ALU.is_ge, fill=NEG,
                        base=0, pattern=[[-1, P]], channel_multiplier=1)
        g.drain()
        g.tensor_copy(band_now[:], band[:])
        g.drain()
        g.memset(band_now[:, META:META + P], NEG).then_inc(consts, 1)

        def x_rsqrt(t, w):
            settle(pool)
            pool.wait_ge(x_sum, t + 1)
            g.tensor_tensor(small[0:w, 2:3], small[0:w, 0:1], small[0:w, 4:5], ALU.mult)
            g.drain()
            g.tensor_scalar(small[0:w, 2:3], small[0:w, 2:3], EPS, None, ALU.add)
            g.drain()
            g.tensor_tensor(small[0:w, 3:4], small[0:w, 2:3], half[0:w, :], ALU.pow).then_inc(x_rs, 1)

        def x_low(t, w, c):
            pool.wait_ge(x_hi, t + 1)
            g.tensor_tensor(h_lo[:, :, bass.ds(c, w)], xw[:, 0, 0:KT * w].rearrange("p (k c) -> p k c", k=KT),
                            h_hi[:, :, bass.ds(c, w)].bitcast(F32), ALU.subtract).then_inc(x_lo, 1)
        x_rsqrt(0, META)
        x_low(0, META, 0)

        def x_step(t, m, u):
            x_rsqrt(t, P)
            x_low(t, P, (t - 1) * P + META)
        steps(pool, 1, NT + 1, x_step)
        pool.wait_ge(x_lo, NT + 1)
        pool.wait_ge(par_tr, 1)
        g.memset(rawc[:, :, 0:3], 0.0).then_inc(consts, 1)

        pool.wait_ge(dz_ok, DH)
        g.tensor_scalar(gz[:], gz[:], params[:, R_DNW:R_DNW + 1], None, ALU.mult).then_inc(gz_ok, 1)

        cc = [tiny[:, 0:24], tiny[:, 24:48]]
        E8, RR, BK, CA, OF, OE = (small[:, 8:16], small[:, 16:24], small[:, 24:28], small[:, 28:32],
                                  small[:, 44:48], small[:, 48:52])
        CZ, S2, S2S = ([small[:, o + 16 * s:o + 4 + 16 * s] for s in range(2)] for o in (60, 64, 68))

        def squares(c, m, u, L=P):
            if isinstance(c, int) and c == 0:
                pool.wait_ge(cols_ok, 3)
                g.tensor_copy(cc[u][0:L], cols[0:L, 0, :])
            else:
                g.tensor_copy(cc[u][:], cols[:, bass.ds(c, 1), :].rearrange("p a c -> p (a c)"))
            pool.wait_ge(qkv_in[u], (m + 1) * 16)
            g.tensor_tensor(sq[:, :, 0:L], qkv[:, u, 0:8, 0:L], qkv[:, u, 0:8, 0:L], ALU.mult).then_inc(sq_ok, 1)

        def scales(c, u, L=P):
            pool.wait_ge(free[lane_of("ssq")], filled("ssq", c))
            g.tensor_tensor(RR[0:L], E8[0:L], half[0:L, :].to_broadcast([L, 8]), ALU.pow)
            g.drain()
            g.tensor_tensor(BK[0:L], cc[u][0:L, 20:24], RR[0:L, 4:8], ALU.mult)
            g.tensor_scalar(S2[u][0:L], RR[0:L, 0:4], float(P) ** -0.5, None, ALU.mult)
            g.drain()
            g.tensor_tensor(CA[0:L], BK[0:L], RR[0:L, 4:8], ALU.mult)
            g.tensor_tensor(S2S[u][0:L], S2[u][0:L], S2[u][0:L], ALU.mult)
            g.drain()
            g.tensor_scalar(CA[0:L], CA[0:L], -1.0, None, ALU.mult)
            g.drain()
            g.tensor_tensor(CZ[u][0:L], CA[0:L], cc[u][0:L, 8:12], ALU.mult).then_inc(rr_ok, 1)

        def scaled_decay(c, L=P):
            pool.wait_ge(dl_ok, c + 1)
            g.tensor_tensor(buf["DL"][0:L, :, 0:L], buf["DL"][0:L, :, 0:L],
                            CA[0:L].unsqueeze(2).to_broadcast([L, DH, L]), ALU.mult).then_inc(dlb_ok, 1)

        def lower(c, L=P, last=None):
            if last is not None:
                pool.wait_ge(free[lane_of("B2T")], filled("B2T", last))
            pool.wait_ge(free[lane_of("KK")], filled("KK", c))
            g.tensor_tensor(buf["Dn"][0:L, :, 0:L], buf["t1"][0:L, :, 0:L],
                            blocks16[0:L, 0:L].unsqueeze(1).to_broadcast([L, DH, L]), ALU.mult).then_inc(dn_ok, 1)
            g.drain()
            g.tensor_tensor(buf["En"][0:L, :, 0:L], buf["t1"][0:L, :, 0:L], buf["Dn"][0:L, :, 0:L],
                            ALU.subtract).then_inc(de_ok, 1)

        def plus_one(dst, src, c, signal, L=P):
            pool.wait_ge(free[lane_of(src)], filled(src, c))
            g.tensor_tensor(buf[dst][0:L, :, 0:L], buf[src][0:L, :, 0:L],
                            ident[0:L, 0:L].unsqueeze(1).to_broadcast([L, DH, L]), ALU.add).then_inc(signal, 1)

        def out_squares(c):
            pool.wait_ge(free[lane_of("P2")], filled("P2", c))
            g.tensor_tensor(buf["osq"][:], buf["op"][:], buf["op"][:], ALU.mult).then_inc(osq_ok, 1)

        def out_norm(c, u):
            pool.wait_ge(ored_ok, c)
            g.tensor_tensor(OE, OE, S2S[u], ALU.mult)
            g.drain()
            g.tensor_scalar(OE, OE, 1.0 / P, EPS, ALU.mult, ALU.add)
            g.drain()
            g.tensor_tensor(OE, OE, half[:].to_broadcast([P, 4]), ALU.pow)
            g.drain()
            g.tensor_tensor(OF, OE, S2[u], ALU.mult)
            g.drain()
            g.tensor_tensor(buf["on"][:], buf["op"][:], OF.unsqueeze(2).to_broadcast([P, DH, P]),
                            ALU.mult).then_inc(on_ok, 1)

        def windows(c, u, first=False):
            if not first:
                pool.wait_ge(s_full, att_filled("O1", c - 2))
            g.tensor_copy(kwin[:, u, META:], ak[:, bass.ds((c - 1) * P, 2 * P)])
            g.tensor_copy(vwin[u][:], vtok[:, bass.ds(c - 1, 2), :])
            g.tensor_copy(qblk[:, u], aq[:, :, bass.ds((c - 1) * P, P)]).then_inc(win_ok, 1)

        def probs(c, i):
            pool.wait_ge(rec_ok, (c - 1) * 4 + (i + 1))
            pb = prob[:, i % 2]
            g.tensor_tensor(pb, pb, small[:, 56 + 2 * (i % 2):58 + 2 * (i % 2)].unsqueeze(2)
                            .to_broadcast([P, 2, META + 2 * P]), ALU.mult).then_inc(pr_ok, 1)

        def mixer(c, m, u, scan, front):
            plus_one("M1", "DnT", c, m1_ok)
            if front:
                windows(c + 1, 1 - u)
            if scan:
                out_squares(c - 1)
            probs(c, 0)
            if scan:
                out_norm(c - 1, 1 - u)
            if front:
                squares(c + 1, m + u, 1 - u)
            probs(c, 1)
            if front:
                scales(c + 1, 1 - u)
            plus_one("W1", "BT", c, w1_ok)
            if front:
                scaled_decay(c + 1)
            probs(c, 2)
            if front:
                lower(c + 1, P, c)
            probs(c, 3)

        def last_scan(c, u):
            out_squares(c)
            out_norm(c, u)
        for c, L in ((0, META), (1, P)):
            squares(c, 0, c, L)
            scales(c, c, L)
            scaled_decay(c, L)
            if c == 1:
                pool.wait_ge(free[lane_of("M4")], filled("M4", 0))
            lower(c, L)
            if c == 0:
                plus_one("M1", "DnT", 0, m1_ok, META)
        pool.wait_ge(s_free, 1)
        pool.wait_ge(p_free, 1)
        for u in range(2):
            g.tensor_copy(kwin[:, u, 0:META], ak[:, P - META:P])
        windows(1, 1, True)
        mixer_steps(pool, mixer, last_scan)

        def merge_add(n, m, u):
            pool.wait_ge(evac[u], m + 1)
            wait(pool, m_l, n - N_MERGE)
            g.tensor_tensor(mt[:, 0, :], mt[:, 0, :], mt[:, 1, :], ALU.add).then_inc(mrg, 1)
        steps(pool, N_MERGE, N_OUT, merge_add, peel=2)

        def sum_squares(base, count):
            for k in range(count):
                pool.wait_ge(o_sq, base + k + 1)
                if k == 0:
                    g.tensor_copy(acc[:], sqt[:]).then_inc(o_acc, 1)
                else:
                    g.drain()
                    g.tensor_tensor(acc[:], acc[:], sqt[:], ALU.add).then_inc(o_acc, 1)

        def rms_pow(r):
            pool.wait_ge(n_add, r)
            g.tensor_tensor(small[:, 0:8], small[:, 8:16], half[:].to_broadcast([P, 8]), ALU.pow).then_inc(n_pow, 1)
        sum_squares(0, KT)
        rms_pow(1)
        sum_squares(KT, KT)
        rms_pow(2)
        for k in range(KT):
            pool.wait_ge(f_h, k + 1)
            g.tensor_tensor(f_lo[:, k, :], [sg, up][k % 2][:], f_hi[:, k, :].bitcast(F32), ALU.subtract).then_inc(f_l, 1)
        n0 = N_FF
        done = 0
        for sz in FF_GROUPS:
            def hidden_lo(j, m, u, done=done, n0=n0):
                pool.wait_ge(u_h, j + (done + 1))
                g.tensor_tensor(u_lo[:, bass.ds(j, 1), :].rearrange("p a c -> p (a c)"), up[:],
                                u_hi[:, bass.ds(j, 1), :].rearrange("p a c -> p (a c)").bitcast(F32),
                                ALU.subtract).then_inc(u_l, 1)
            steps(pool, 0, sz, hidden_lo)
            done += sz
            n0 += 2 * sz + KT
        sum_squares(2 * KT, KT)
        rms_pow(3)

    @block.scalar
    def _(act):
        a = nc.scalar

        def x_tile(t, m, u, w=P, c=0):
            act.wait_ge(x_in[u], (m + 1) * 16)
            wait(act, x_nrm, t)
            a.activation(xw[0:w, 0, :], xin[0:w, u, :], ACT.Square, accum_out=small[0:w, 0:1]).then_inc(x_sum, 1)
            act.wait_ge(x_wt, t + 1)
            settle(act)
            a.activation(h_hi[:, :, bass.ds(c, w)], xw[:, 0, 0:KT * w].rearrange("p (k c) -> p k c", k=KT),
                         ACT.Copy).then_inc(x_hi, 1)
            act.wait_ge(x_lo, t + 1)

        x_tile(0, 0, 0, META, 0)
        steps(act, 1, NT + 1, lambda t, m, u: x_tile(t, m, u, P, (t - 1) * P + META))
        split_hi(0, 0, 0)
        act.wait_ge(wd_in, 16)
        a.activation(wd_hi[:], wd_raw[:], ACT.Copy).then_inc(wd_h, 1)

        def bias(base, j):
            return params[:, bass.ds(j + base, 1)]

        def kv_out(n, m, u):
            split_hi(*after(n, m, u))
            act.wait_ge(mm_done, n + 1)
            dst = (ak, av)[n]
            a.activation(dst[:, P:], banks(4 * u), ACT.Identity, bias=params[:, GRP + n:GRP + n + 1])
            a.activation(dst[:, P - META:P], ps[:, 4 * u + 2, 0:META], ACT.Identity,
                         bias=params[:, GRP + n:GRP + n + 1]).then_inc(evac[u], 1)
        kv_out(0, 0, 0)
        kv_out(1, 0, 1)

        def q_out(n, m, u):
            split_hi(*after(n, m, u))
            act.wait_ge(mm_done, n + 1)
            settle(act)
            a.activation(aq[:, bass.ds(n - N_Q, 1), :].rearrange("p a c -> p (a c)"), banks(4 * u), ACT.Identity,
                         bias=bias(0, n - N_Q)).then_inc(evac[u], 1)
        steps(act, N_Q, N_DN, q_out)

        def silu_conv(j, parity):
            act.wait_ge(conv_ok, j + 1)
            if not isinstance(j, int):
                act.wait_ge(stored[parity], (j_half(j)) * 16)
            elif j >= 2:
                act.wait_ge(stored[parity], (j // 2) * 16)
            a.activation(cs[:, parity, :], cv[:, parity, :], ACT.Silu).then_inc(silu_ok, 1)

        jh = {}

        def j_half(j):
            return jh["m"]

        def dn_out(n, m, u):
            split_hi(*after(n, m, u))
            j = n - N_DN
            if not (isinstance(n, int) and n == N_DN):
                jh["m"] = (m - N_DN // 2) + (0 if u == 1 else -1)
                silu_conv(j - 1, 1 - u)
            act.wait_ge(mm_done, n + 1)
            b = bias(R_BIAS, n - N_DN + 6)
            settle(act)
            a.activation(rawc[:, u, 3 + META:], banks(4 * u), ACT.Identity, bias=b)
            a.activation(rawc[:, u, 3:3 + META], ps[:, 4 * u + 2, 0:META], ACT.Identity, bias=b).then_inc(evac[u], 1)
        act.wait_ge(consts, 3)
        act.wait_ge(x_lo, NT + 1)
        steps(act, N_DN, N_DZ, dn_out, peel=4)

        def dz_out(n, m, u):
            split_hi(*after(n, m, u))
            if n == N_DZ:
                jh["m"] = 5
                silu_conv(11, 1)
            act.wait_ge(mm_done, n + 1)
            a.activation(gz[:, n - N_DZ, :], banks(4 * u), ACT.Silu, bias=bias(R_BIAS, n - N_DZ + 18)).then_inc(dz_ok, 1)
            a.drain().then_inc(evac[u], 1)
        for n in range(N_DZ, N_G):
            dz_out(n, n // 2, n % 2)

        def gate_out(n, m, u):
            split_hi(*after(n, m, u))
            act.wait_ge(mm_done, n + 1)
            act.wait_ge(stored[u], (m - N_G // 2 + 6) * 16)
            settle(act)
            a.activation(cs[:, u, 0:TOK], banks(4 * u), ACT.Sigmoid, bias=bias(R_BG, n - N_G)).then_inc(silu_ok, 1)
            a.drain().then_inc(evac[u], 1)
        steps(act, N_G, N_MERGE, gate_out)

        act.wait_ge(bc_in, 64)
        ea = tiny[:, 48:52]
        a.activation(ea, alog[:], ACT.Exp)
        act.wait_ge(dab_add, 1)
        dx = dabx[:]
        a.activation(dabe[:, :, 4:8], dx[:, :, 4:8], ACT.Exp, scale=-1.0)
        a.activation(dabe[:, :, 0:4], dx[:, :, 0:4], ACT.Abs)
        a.drain()
        a.activation(dabe[:, :, 0:4], dabe[:, :, 0:4], ACT.Exp, scale=-1.0)
        a.drain()
        a.activation(dabe[:, :, 0:4], dabe[:, :, 0:4], ACT.Ln, bias=1.0).then_inc(dab_act, 1)
        act.wait_ge(cols_ok, 1)
        a.activation(cols[:, :, 8:12], cols[:, :, 4:8], ACT.Exp)
        a.activation(cols[:, 1:, 12:16], cols[:, 1:, 12:16], ACT.Exp)
        a.activation(cols[0:META, 0, 12:16], cols[0:META, 0, 12:16], ACT.Exp)
        a.activation(cols[:, :, 16:20], cols[:, :, 16:20], ACT.Exp).then_inc(cols_ok, 2)

        def copy_of(op, c, L=P, dst=None):
            lane = lane_of(op)
            act.wait_ge(full[lane], filled(op, c))
            a.activation(buf[dst or op][0:L, :, 0:L], delta_bank(op)[0:L, :, 0:L], ACT.Copy).then_inc(free[lane], 1)

        def decays(c, L):
            act.wait_ge(a2_ok, c + 1)
            a.activation(buf["DL"][0:L, :, 0:L], buf["DL"][0:L, :, 0:L], ACT.Exp).then_inc(dl_ok, 1)
            act.wait_ge(a1_ok, c + 1)
            a.activation(buf["DT"][0:L, :, 0:L], buf["DT"][0:L, :, 0:L], ACT.Exp).then_inc(dt_ok, 1)

        def exps(c, i):
            act.wait_ge(nm_ok, (c - 1) * 4 + (i + 1))
            s = i % 2
            for h in range(2):
                a.activation(prob[:, s, h, :], prob[:, s, h, :], ACT.Exp, scale=HD ** -0.5,
                             bias=tiny[:, 56 + 4 * s + h:57 + 4 * s + h], accum_out=tiny[:, 64 + 4 * s + h:65 + 4 * s + h])
            a.activation(tiny[:, 66 + 4 * s:68 + 4 * s], tiny[:, 58 + 4 * s:60 + 4 * s], ACT.Exp).then_inc(ex_ok, 1)

        def probs_T(c, kv):
            act.wait_ge(p_full, (c - 1) * 2 + (kv + 2))
            a.activation(pt[0:META, 0, :], ps[0:META, APB, :], ACT.Copy)
            a.activation(pt[:, 1:3, :], ps[:, APB + 1:APB + 3, :], ACT.Copy).then_inc(p_free, 1)

        def att_out(c, kv):
            act.wait_ge(s_full, att_filled(f"O{kv}", c))
            settle(act)
            a.activation(ya[kv * HD:(kv + 1) * HD, :, bass.ds((c - 1) * P, P)],
                         ps[kv * HD:(kv + 1) * HD, AS, :].rearrange("p (j c) -> p j c", j=GRP),
                         ACT.Copy).then_inc(s_free, 1)

        decays(0, META)
        for op in ("DnT", "D2", "D2T", "D4", "D8"):
            copy_of(op, 0, META)
        act.wait_ge(full[lane_of("VN")], filled("VN", 0))
        a.activation(buf["vn"][0:META], delta_bank("VN")[0:META], ACT.Copy).then_inc(free[lane_of("VN")], 1)

        decays(1, P)

        def mixer(c, m, u, scan, front):
            for op in ("DnT", "D2", "D2T"):
                copy_of(op, c)
            if scan:
                copy_of("VN", c - 1, dst="vn")
            exps(c, 0)
            copy_of("D4", c)
            copy_of("D8", c)
            exps(c, 1)
            copy_of("B", c)
            copy_of("BT", c)
            if front:
                decays(c + 1, P)
            copy_of("B2", c)
            probs_T(c, 0)
            copy_of("Ninv", c)
            att_out(c, 0)
            copy_of("B4", c)
            exps(c, 2)
            exps(c, 3)
            copy_of("TT", c, dst=f"TT{u}")
            probs_T(c, 1)
            att_out(c, 1)
        mixer_steps(act, mixer, lambda c, u: copy_of("VN", c, dst="vn"))

        act.wait_ge(full[lane_of("oT")], filled("oT", NT))
        act.wait_ge(s_free, att_filled("O1", NT))
        a.activation(y_hi[:, 0:4, :], ya[:], ACT.Copy).then_inc(y_h, 1)
        act.wait_ge(free[lane_of("oT")], filled("oT", NT))
        a.activation(y_hi[:, 4:8, :], yd[:], ACT.Copy).then_inc(y_h, 1)

        def merge_hi(n, m, u):
            split_hi(*after(n, m, u))
            act.wait_ge(mrg, n - N_MERGE + 1)
            settle(act)
            a.activation(m_hi[:, bass.ds(n - N_MERGE, 1), :].rearrange("p a c -> p (a c)"), mt[:, 0, :],
                         ACT.Copy).then_inc(m_h, 1)
        steps(act, N_MERGE, N_OUT, merge_hi, peel=0)

        def square(src, idx):
            settle(act)
            wait(act, o_acc, idx)
            a.activation(sqt[:], src, ACT.Square).then_inc(o_sq, 1)

        def out_evac(n, m, u):
            split_hi(*after(n, m, u))
            act.wait_ge(mm_done, n + 1)
            if isinstance(n, int) and n == N_OUT:
                act.wait_ge(m_l, KT)
            settle(act)
            dst = oT[:, bass.ds(n - N_OUT, 1), :].rearrange("p a c -> p (a c)")
            a.activation(dst, banks(4 * u), ACT.Copy).then_inc(evac[u], 1)
            a.drain()
            square(dst, n - N_OUT)
        steps(act, N_OUT, N_FF, out_evac, peel=2)
        for k in range(KT):
            act.wait_ge(x2_ok, k + 1)
            square(oT[:, k, :], KT + k)
        for k in range(KT):
            act.wait_ge(fw, k + 1)
            a.activation(f_hi[:, k, :], [sg, up][k % 2][:], ACT.Copy).then_inc(f_h, 1)
        n0, done = N_FF, 0
        for gi, sz in enumerate(FF_GROUPS):
            def gate(n, m, u, n0=n0, done=done):
                split_hi(*after(n, m, u))
                if u == 0:
                    act.wait_ge(mm_done, n + 1)
                    act.wait_ge(f_l, KT)
                    wait(act, up_ok, m - n0 // 2 + done)
                    a.activation(sg[:], banks(0), ACT.Silu).then_inc(sg_ok, 1)
                    a.drain().then_inc(evac[0], 1)
                else:
                    j = m - n0 // 2
                    act.wait_ge(up_ok, j + (done + 1))
                    settle(act)
                    a.activation(u_hi[:, bass.ds(j, 1), :].rearrange("p a c -> p (a c)"), up[:],
                                 ACT.Copy).then_inc(u_h, 1)
            steps(act, n0, n0 + 2 * sz, gate, peel=2)
            n1 = n0 + 2 * sz

            def only_split(n, m, u):
                split_hi(*after(n, m, u))
            if gi < 2:
                steps(act, n1, n1 + KT, only_split)
            else:
                steps(act, n1, n1 + KT - 2, only_split)
                only_split(n1 + KT - 2, (n1 + KT - 2) // 2, 0)
            done += sz
            n0 = n1 + KT
        for k in range(KT):
            act.wait_ge(fa_ok, k + 1)
            square(facc[:, k, :], 2 * KT + k)
        def out_copy(t, m, u):
            act.wait_ge(ot_ps, t + 1)
            if not (isinstance(t, int) and t < 2):
                act.wait_ge(out_st[u], m * 16)
            a.activation(otile[:, u, :], banks(2 * u), ACT.Copy).then_inc(ot_ok, 1)
        steps(act, 0, NT, out_copy, peel=2)

    @block.vector
    def _(dve):
        v = nc.vector
        dve.wait_ge(par_tr, 1)
        v.tensor_copy(params[:, 0:NROWS], ps[:, 7, 0:NROWS]).then_inc(par_ok, 1)
        v.drain()

        def x_tile(t, m, u, w=P):
            dve.wait_ge(x_rs, t + 1)
            wait(dve, x_tr, t - 1)
            v.tensor_scalar(xn[0:w, u, :], xin[0:w, u, :], small[0:w, 3:4], None, ALU.mult).then_inc(x_nrm, 1)
            dve.wait_ge(x_tr, t + 1)
            v.tensor_tensor(xw[:, 0, 0:KT * w].rearrange("p (k c) -> p k c", k=KT),
                            banks(4 + 0)[:, 0:KT * w].rearrange("p (k c) -> p k c", k=KT),
                            params[:, R_PRE:R_PRE + KT].unsqueeze(2).to_broadcast([P, KT, w]),
                            ALU.mult).then_inc(x_wt, 1)
        x_tile(0, 0, 0, META)
        x_tile(1, 0, 1)
        steps(dve, 2, NT, lambda t, m, u: x_tile(t, m, u))
        x_tile(NT, NT // 2, 0)
        split_lo(0, 0, 0)
        dve.wait_ge(wd_h, 1)
        v.tensor_tensor(wd_lo[:], wd_raw[:], wd_hi[:].bitcast(F32), ALU.subtract).then_inc(wd_l, 1)
        split_lo(1, 0, 1)
        steps(dve, 2, N_DN, lambda n, m, u: split_lo(n, m, u))
        split_lo(N_DN, N_DN // 2, 0)

        def conv(n, m, u):
            split_lo(*after(n, m, u))
            j = n - N_DN
            dve.wait_ge(evac[u], m + 1)
            if not (isinstance(n, int) and n < N_DN + 2):
                dve.wait_ge(silu_ok, j - 1)
            v.tensor_scalar(cv[:, u, :], rawc[:, u, 0:LW], params[:, bass.ds(j + R_CONV, 1)], None, ALU.mult)
            for k in range(1, 4):
                v.drain()
                last = v.scalar_tensor_tensor(cv[:, u, :], rawc[:, u, k:k + LW],
                                              params[:, bass.ds(j + (R_CONV + 12 * k), 1)], cv[:, u, :],
                                              ALU.mult, ALU.add)
            last.then_inc(conv_ok, 1)
        steps(dve, N_DN, N_DZ, conv, peel=2)
        dve.wait_ge(dab_mm, 1)
        dve.wait_ge(bc_in, 64)
        v.tensor_tensor(dab_b[:, 0:4], dab_b[:, 0:4], dtb[:], ALU.add)
        v.drain()
        v.tensor_tensor(dabx[:], ps[:, 3, 0:8 * (NT + 1)].rearrange("p (t c) -> p t c", c=8),
                        dab_b[:].unsqueeze(1).to_broadcast([P, NT + 1, 8]), ALU.add).then_inc(dab_add, 1)
        steps(dve, N_DZ, N_MERGE, lambda n, m, u: split_lo(*after(n, m, u)))

        dve.wait_ge(dab_act, 1)
        v.tensor_scalar(dabx[:, :, 0:4], dabx[:, :, 0:4], 0.0, None, ALU.max)
        v.tensor_scalar(dabe[:, :, 4:8], dabe[:, :, 4:8], 1.0, None, ALU.add)
        v.drain()
        v.tensor_tensor(dabx[:, :, 0:4], dabx[:, :, 0:4], dabe[:, :, 0:4], ALU.add)
        v.reciprocal(cols[:, :, 20:24], dabe[:, :, 4:8])
        v.tensor_scalar(tiny[:, 52:56], tiny[:, 48:52], -1.0, None, ALU.mult)
        v.drain()
        v.tensor_tensor(cols[:, :, 0:4], dabx[:, :, 0:4], tiny[:, 52:56].unsqueeze(1).to_broadcast([P, NT + 1, 4]),
                        ALU.mult).then_inc(dab_g, 1)
        dve.wait_ge(cum_mm, 1)
        c36 = [ps[:, 3, 128 * i:128 * i + 36].rearrange("p (t c) -> p t c", c=4) for i in range(2)]
        v.tensor_copy(cols[:, :, 4:8], c36[0])
        v.tensor_copy(cols[:, :, 16:20], c36[1])
        v.drain()
        v.tensor_tensor(cols[:, :, 12:16], cols[:, :, 16:20], cols[:, :, 4:8], ALU.subtract).then_inc(cols_ok, 1)

        dve.wait_ge(s_full, 1)
        v.tensor_copy(vtok[:, 1:, :], banks(AS).rearrange("p (t c) -> p t c", c=P)).then_inc(s_free, 1)
        dve.wait_ge(p_full, 1)
        v.tensor_copy(vmeta[:], ps[0:META, APB, 0:P]).then_inc(p_free, 1)

        E8, BK, OE = small[:, 8:16], small[:, 24:28], small[:, 48:52]
        CZ = [small[:, 60 + 16 * s:64 + 16 * s] for s in range(2)]
        cc = [tiny[:, 0:24], tiny[:, 24:48]]

        def evac_of(op, c, make):
            lane = lane_of(op)
            dve.wait_ge(full[lane], filled(op, c))
            last = make(delta_bank(op))
            last.then_inc(free[lane], 1)

        def norms(c, L=P):
            if not (isinstance(c, int) and c == 0):
                dve.wait_ge(rr_ok, c)
            evac_of("ssq", c, lambda b: v.tensor_scalar(E8[0:L], b[0:L, 0, 0:8], EPS, None, ALU.add))

        def exponents(c, u, L=P):
            g_col = cc[u][0:L, 4:8].unsqueeze(2).to_broadcast([L, DH, L])
            evac_of("gam", c, lambda b: v.tensor_tensor(buf["t1"][0:L, :, 0:L], b[0:L, :, 0:L], g_col, ALU.subtract))
            v.drain()
            v.scalar_tensor_tensor(buf["DL"][0:L, :, 0:L], buf["t1"][0:L, :, 0:L], -1.0,
                                   mask_low[0:L, 0:L].unsqueeze(1).to_broadcast([L, DH, L]),
                                   ALU.mult, ALU.add).then_inc(a2_ok, 1)
            v.tensor_tensor(buf["DT"][0:L, :, 0:L], buf["t1"][0:L, :, 0:L],
                            mask_up[0:L, 0:L].unsqueeze(1).to_broadcast([L, DH, L]), ALU.add).then_inc(a1_ok, 1)
            v.drain()

        def minus_a(c, L=P):
            dve.wait_ge(dlb_ok, c + 1)
            evac_of("KK", c, lambda b: v.tensor_tensor(buf["t1"][0:L, :, 0:L], b[0:L, :, 0:L],
                                                       buf["DL"][0:L, :, 0:L], ALU.mult))

        def att_T(c, u):
            dve.wait_ge(dt_ok, c + 1)
            evac_of("KQ", c, lambda b: v.tensor_tensor(buf[f"attT{u}"][:], b, buf["DT"][:], ALU.mult))

        def values(c, u, L=P):
            dve.wait_ge(rr_ok, c + 1)
            evac_of("vT", c, lambda b: v.tensor_tensor(
                buf[f"vb{u}"][0:L], b[0:L], BK[0:L].unsqueeze(2).to_broadcast([L, DH, P]), ALU.mult))

        def keys(c, u, L=P):
            evac_of("kT", c, lambda b: v.tensor_tensor(
                buf[f"kd{u}"][0:L], b[0:L], cc[u][0:L, 12:16].unsqueeze(2).to_broadcast([L, DH, P]), ALU.mult))

        def copy_of(op, c, L=P):
            evac_of(op, c, lambda b: v.tensor_copy(buf[op][0:L, :, 0:L], b[0:L, :, 0:L]))

        def add_of(op, prev, c, L=P):
            evac_of(op, c, lambda b: v.tensor_tensor(buf[op][0:L, :, 0:L], b[0:L, :, 0:L], buf[prev][0:L, :, 0:L],
                                                     ALU.add))
            v.drain()

        norms(0, META)
        exponents(0, 0, META)
        minus_a(0, META)
        values(0, 0, META)
        keys(0, 0, META)
        copy_of("D4T", 0, META)
        dve.wait_ge(m1_ok, 1)
        add_of("M2", "M1", 0, META)
        add_of("M3", "M2", 0, META)
        add_of("M4", "M3", 0, META)
        evac_of("dS", 0, lambda b: v.tensor_copy(buf["S"][:], b))
        v.drain()
        norms(1)
        exponents(1, 1)
        minus_a(1)
        att_T(1, 1)
        values(1, 1)
        keys(1, 1)

        def z_rows(c, u):
            lane = lane_of("KS")
            v.drain()
            dve.wait_ge(full[lane], filled("KS", c))
            for h in range(DH):
                last = v.scalar_tensor_tensor(buf["Z"][:, h, :], delta_bank("KS")[:, h, :], CZ[u][:, h:h + 1],
                                              buf[f"vb{u}"][:, h, :], ALU.mult, ALU.add)
            last.then_inc(free[lane], 1)

        def state_out(c, u):
            evac_of("P1", c, lambda b: v.tensor_tensor(
                buf["o1"][:], b, cc[u][:, 8:12].unsqueeze(2).to_broadcast([P, DH, P]), ALU.mult))

        def state(c, u):
            lane = lane_of("dS")
            dve.wait_ge(full[lane], filled("dS", c))
            for h in range(DH):
                last = v.scalar_tensor_tensor(buf["S"][:, h, :], buf["S"][:, h, :], cc[u][:, 16 + h:17 + h],
                                              delta_bank("dS")[:, h, :], ALU.mult, ALU.add)
            last.then_inc(free[lane], 1)
            v.drain()

        def out_sum(c):
            evac_of("P2", c, lambda b: v.tensor_tensor(buf["op"][:], b, buf["o1"][:], ALU.add))

        def out_reduce(c):
            dve.wait_ge(osq_ok, c)
            v.tensor_reduce(OE, buf["osq"][:], axis=AX.X, op=ALU.add).then_inc(ored_ok, 1)

        def gated(c):
            evac_of("oT", c, lambda b: v.tensor_tensor(yd[:, :, bass.ds((c - 1) * P, P)], b,
                                                       gz[:, :, bass.ds((c - 1) * P, P)], ALU.mult))

        def scores(c, i):
            s = i % 2
            dve.wait_ge(s_full, att_filled(["S00", "S01", "S10", "S11"][i], c))
            dve.wait_ge(p_full, (c - 1) * 2 + (1 if i < 2 else 2))
            pb = prob[:, s]
            mask = band_now if isinstance(c, int) and c == 1 else band
            v.tensor_tensor(pb, ps[:, AS:AS + 2, 0:META + 2 * P],
                            mask[:].unsqueeze(1).to_broadcast([P, 2, META + 2 * P]), ALU.add).then_inc(s_free, 1)
            v.drain()
            v.tensor_reduce(tiny[:, 72 + 2 * s:74 + 2 * s], pb, axis=AX.X, op=ALU.max)
            v.drain()
            kh = 4 * (i // 2) + 2 * (i % 2)
            t0 = tiny[:, 72 + 2 * s:74 + 2 * s]
            v.scalar_tensor_tensor(t0, t0, HD ** -0.5, sink[:, kh:kh + 2], ALU.mult, ALU.max)
            v.drain()
            v.tensor_scalar(tiny[:, 56 + 4 * s:58 + 4 * s], t0, -1.0, None, ALU.mult)
            v.tensor_tensor(tiny[:, 58 + 4 * s:60 + 4 * s], sink[:, kh:kh + 2], t0, ALU.subtract).then_inc(nm_ok, 1)

        def denominators(c, i):
            s = i % 2
            dve.wait_ge(ex_ok, (c - 1) * 4 + (i + 1))
            v.tensor_tensor(tiny[:, 76 + 2 * s:78 + 2 * s], tiny[:, 64 + 4 * s:66 + 4 * s],
                            tiny[:, 66 + 4 * s:68 + 4 * s], ALU.add)
            v.drain()
            v.reciprocal(small[:, 56 + 2 * s:58 + 2 * s], tiny[:, 76 + 2 * s:78 + 2 * s]).then_inc(rec_ok, 1)

        def mixer(c, m, u, scan, front):
            w = 1 - u
            if scan:
                z_rows(c - 1, w)
                state_out(c - 1, w)
            scores(c, 0)
            copy_of("D4T", c)
            denominators(c, 0)
            dve.wait_ge(m1_ok, c + 1)
            add_of("M2", "M1", c)
            if scan:
                state(c - 1, w)
                out_sum(c - 1)
            add_of("M3", "M2", c)
            scores(c, 1)
            add_of("M4", "M3", c)
            if scan:
                out_reduce(c - 1)
            denominators(c, 1)
            if front:
                norms(c + 1)
                exponents(c + 1, w)
            if scan:
                gated(c - 1)
            copy_of("B2T", c)
            dve.wait_ge(w1_ok, c)
            add_of("W2", "W1", c)
            scores(c, 2)
            if front:
                minus_a(c + 1)
                att_T(c + 1, w)
            add_of("W3", "W2", c)
            scores(c, 3)
            if front:
                values(c + 1, w)
            denominators(c, 2)
            if front:
                keys(c + 1, w)
            denominators(c, 3)

        def last_scan(c, u):
            z_rows(c, u)
            state_out(c, u)
            state(c, u)
            out_sum(c)
            out_reduce(c)
            gated(c)
        dve.wait_ge(gz_ok, 1)
        mixer_steps(dve, mixer, last_scan)

        for i, src in enumerate((ya, yd)):
            dve.wait_ge(y_h, i + 1)
            v.tensor_tensor(y_lo[:, 4 * i:4 * i + 4, :], src[:], y_hi[:, 4 * i:4 * i + 4, :].bitcast(F32),
                            ALU.subtract).then_inc(y_l, 1)

        def merge_mul(n, m, u):
            split_lo(*after(n, m, u))
            v.drain()
            dve.wait_ge(mm_done, n + 1)
            dve.wait_ge(gate_in[u], (m - N_MERGE // 2 + 1) * 32)
            v.tensor_tensor(mt[:, 0, :], banks(4 * u), gin[:, u, 0, :], ALU.mult)
            v.tensor_tensor(mt[:, 1, :], banks(4 * u + 2), gin[:, u, 1, :], ALU.mult).then_inc(evac[u], 1)
            dve.wait_ge(m_h, n - N_MERGE + 1)
            v.tensor_tensor(m_lo[:, bass.ds(n - N_MERGE, 1), :].rearrange("p a c -> p (a c)"), mt[:, 0, :],
                            m_hi[:, bass.ds(n - N_MERGE, 1), :].rearrange("p a c -> p (a c)").bitcast(F32),
                            ALU.subtract).then_inc(m_l, 1)
        steps(dve, N_MERGE, N_OUT, merge_mul)
        steps(dve, N_OUT, N_FF, lambda n, m, u: split_lo(*after(n, m, u)))

        def rms(r):
            dve.wait_ge(n_mm, r)
            v.tensor_scalar(small[:, 8:16], ps[:, 7, 0:8], 1.0 / D, EPS, ALU.mult, ALU.add).then_inc(n_add, 1)
            dve.wait_ge(n_pow, r)
            v.tensor_tensor(sqt[:].rearrange("p (t c) -> p t c", c=P), ident[:].unsqueeze(1).to_broadcast([P, NT, P]),
                            small[:, 0:8].unsqueeze(2).to_broadcast([P, NT, P]), ALU.mult).then_inc(n_dg, 1)
            dve.wait_ge(n_bc, r)
            v.tensor_copy(rb[:], banks(5)).then_inc(n_rb, 1)
            v.drain()
        rms(1)
        for k in range(KT):
            v.scalar_tensor_tensor(oT[:, k, :], oT[:, k, :], params[:, R_POST + k:R_POST + k + 1], rb[:],
                                   ALU.mult, ALU.mult)
            dve.wait_ge(xt_ps, k + 1)
            v.drain()
            v.tensor_tensor(oT[:, k, :], oT[:, k, :], banks(2 * (k % 2)), ALU.add).then_inc(x2_ok, 1)
        rms(2)
        for k in range(KT):
            if k >= 2:
                dve.wait_ge(f_l, k - 1)
            v.scalar_tensor_tensor([sg, up][k % 2][:], oT[:, k, :], params[:, R_FPRE + k:R_FPRE + k + 1], rb[:],
                                   ALU.mult, ALU.mult).then_inc(fw, 1)
        n0, done = N_FF, 0
        for gi, sz in enumerate(FF_GROUPS):
            def prod(n, m, u, n0=n0, done=done):
                split_lo(*after(n, m, u))
                if u == 1:
                    j = m - n0 // 2
                    dve.wait_ge(mm_done, n + 1)
                    dve.wait_ge(sg_ok, j + (done + 1))
                    wait(dve, u_l, j + done)
                    v.tensor_tensor(up[:], banks(4), sg[:], ALU.mult).then_inc(up_ok, 1)
                    v.drain().then_inc(evac[1], 1)
            steps(dve, n0, n0 + 2 * sz, prod, peel=2)
            n1 = n0 + 2 * sz

            def down(n, m, u, n1=n1, gi=gi, split=True):
                if split:
                    split_lo(*after(n, m, u))
                dve.wait_ge(mm_done, n + 1)
                dst = facc[:, bass.ds(n - n1, 1), :].rearrange("p a c -> p (a c)")
                if gi == 0:
                    if isinstance(n, int) and n == n1:
                        dve.wait_ge(x2_st, 16)
                    last = v.tensor_copy(dst, banks(4 * u))
                else:
                    last = v.tensor_tensor(dst, dst, banks(4 * u), ALU.add)
                last.then_inc(evac[u], 1)
                if gi == 2:
                    v.drain().then_inc(fa_ok, 1)
            if gi == 0:
                steps(dve, n1, n1 + KT, down, peel=2)
            elif gi == 1:
                v.drain()
                steps(dve, n1, n1 + KT, down)
            else:
                v.drain()
                steps(dve, n1, n1 + KT - 2, down)
                down(n1 + KT - 2, (n1 + KT - 2) // 2, 0)
                down(n1 + KT - 1, (n1 + KT - 1) // 2, 1, split=False)
            done += sz
            n0 = n1 + KT
        rms(3)
        dve.wait_ge(x2_back, 16)
        for k in range(KT):
            v.scalar_tensor_tensor(facc[:, k, :], facc[:, k, :], params[:, R_FPOST + k:R_FPOST + k + 1], rb[:],
                                   ALU.mult, ALU.mult)
            v.drain()
            v.tensor_tensor(facc[:, k, :], facc[:, k, :], x2b[:, k, :], ALU.add).then_inc(x3_ok, 1)

    @block.tensor
    def _(pe):
        pe.wait_ge(consts, 1)
        pe.wait_ge(par_in, 160)
        TR(ps[:, 7, 0:NROWS], prow[0:NROWS, :], ident[0:NROWS, 0:NROWS]).then_inc(par_tr, 1)

        def x_tile(t, m, u, w=P):
            pe.wait_ge(x_nrm, t + 1)
            wait(pe, x_wt, t)
            if isinstance(t, int) and t == 0:
                pe.wait_ge(par_ok, 1)
            for k in range(KT):
                last = TR(banks(4)[:, k * w:(k + 1) * w], xn[0:w, u, k * P:(k + 1) * P], ident[0:w, 0:w])
            last.then_inc(x_tr, 1)
        x_tile(0, 0, 0, META)
        steps(pe, 1, NT + 1, x_tile)
        pe.wait_ge(x_lo, NT + 1)
        for n in range(2):
            dense(n, 0, n, h_hi, h_lo, META, meta_cols=True).then_inc(mm_done, 1)
        steps(pe, N_Q, N_DN, lambda n, m, u: dense(n, m, u, h_hi, h_lo, META).then_inc(mm_done, 1))
        steps(pe, N_DN, N_DZ, lambda n, m, u: dense(n, m, u, h_hi, h_lo, META, meta_cols=True).then_inc(mm_done, 1))
        pe.wait_ge(wd_l, 1)
        for t in range(NT + 1):
            c = max(0, META + (t - 1) * P)
            for k in range(KT):
                for i, (h, w) in enumerate(((h_hi, wd_hi), (h_hi, wd_lo), (h_lo, wd_hi))):
                    last = MM(ps[:, 3, 8 * t:8 * t + 8], h[:, k, c:c + P], w[:, k, :],
                              start=(k == 0 and i == 0), stop=(k == KT - 1 and i == 2))
        last.then_inc(dab_mm, 1)
        steps(pe, N_DZ, N_MERGE, lambda n, m, u: dense(n, m, u, h_hi, h_lo, META).then_inc(mm_done, 1))

        for u in range(2):
            pe.wait_ge(evac[u], N_MERGE // 2)
        pe.wait_ge(consts, 2)
        pe.wait_ge(dab_g, 1)
        g_all = cols[:, :, 0:4]
        MM(ps[:, 3, 0:36].rearrange('p (t c) -> p t c', c=4), upper[:], g_all, start=True, stop=True)
        MM(ps[:, 3, 128 + 4:128 + 36].rearrange('p (t c) -> p t c', c=4), ones[:], cols[:, 1:, 0:4], start=True, stop=True)
        MM(ps[:, 3, 128:128 + 4], ones[0:META, :], cols[0:META, 0, 0:4], start=True, stop=True).then_inc(cum_mm, 1)
        for t in range(NT):
            last = TR(banks(AS)[:, t * P:(t + 1) * P], av[:, P + t * P:2 * P + t * P], ident[:])
        last.then_inc(s_full, 1)
        TR(ps[0:META, APB, 0:P], av[:, P - META:P], ident[:]).then_inc(p_full, 1)

        def fill(op, c, L, make, *waits):
            lane = lane_of(op)
            pe.wait_ge(free[lane], filled(op, c) - 1) if not (isinstance(c, int) and filled(op, c) == 1) else None
            for s, value in waits:
                pe.wait_ge(s, value)
            for h in range(DH):
                last = make(h)
            last.then_inc(full[lane], 1)

        def ready(op, c):
            return free[lane_of(op)], filled(op, c)

        def own(op, c, u, L=P, *waits):
            q = lambda t: qkv[:, u, t, 0:L]
            X = lambda k, h: buf[k][0:L, h, 0:L]
            bank = lambda h: delta_bank(op)[0:L, h, 0:L]
            eye = ident[0:L, 0:L]
            cc = tiny[:, 24 * u:24 * u + 24]
            pair = dict(D2=("DnT", "Dn"), D2T=("Dn", "DnT"), D4=("D2T", "D2"), D4T=("D2", "D2T"), M2=("D2", "M1"),
                        D8=("D4T", "D4"), M3=("D4", "M2"), M4=("D8", "M3"), B=("M4", "En"), BT=("En", "M4"),
                        B2=("BT", "B"), B2T=("B", "BT"), W2=("B2", "W1"), B4=("B2T", "B2"), W3=("B4", "W2"),
                        TT=("Ninv", "W3"))
            make = {"gam": lambda h: MM(bank(h), cc[0:L, h:h + 1].to_broadcast([L, L]), upper[0:L, 0:L],
                                        start=True, stop=True),
                    "KK": lambda h: MM(bank(h), q(4 + h), q(4 + h), start=True, stop=True),
                    "KQ": lambda h: MM(bank(h), q(4 + h), q(h), start=True, stop=True),
                    "vT": lambda h: TR(delta_bank("vT")[0:L, h, :], q(8 + h), ident[:]),
                    "kT": lambda h: TR(delta_bank("kT")[0:L, h, :], q(4 + h), ident[:]),
                    "DnT": lambda h: TR(bank(h), X("Dn", h), eye),
                    "Ninv": lambda h: TR(bank(h), X("M4", h), eye)}
            if op in pair:
                lhsT, rhs = pair[op]
                fill(op, c, L, lambda h: MM(bank(h), X(lhsT, h), X(rhs, h), start=True, stop=True), *waits)
            else:
                fill(op, c, L, make[op], *waits)

        def norms(c, L=P):
            lane = lane_of("ssq")
            if not (isinstance(c, int) and c == 0):
                pe.wait_ge(free[lane], filled("ssq", c) - 1)
            pe.wait_ge(sq_ok, c + 1)
            for t in range(8):
                last = MM(delta_bank("ssq")[0:L, 0, t:t + 1], sq[:, t, 0:L], ones[:, 0:1], start=True, stop=True)
            last.then_inc(full[lane], 1)

        def scan_of(op, c, u, *waits):
            q = lambda t: qkv[:, u, t, :]
            X = lambda k, h: buf[k][:, h, :]
            pair = dict(KS=lambda h: (q(4 + h), X("S", h)), VN=lambda h: (X(f"TT{u}", h), X("Z", h)),
                        dS=lambda h: (X(f"kd{u}", h), X("vn", h)), P1=lambda h: (q(h), X("S", h)),
                        P2=lambda h: (X(f"attT{u}", h), X("vn", h)))
            if op == "oT":
                fill(op, c, P, lambda h: TR(delta_bank(op)[:, h, :], X("on", h), ident[:]), *waits)
            else:
                fill(op, c, P, lambda h: MM(delta_bank(op)[:, h, :], *pair[op](h), start=True, stop=True), *waits)

        def score(c, i, u):
            op = ["S00", "S01", "S10", "S11"][i]
            kv, j0 = i // 2, 2 * (i % 2)
            pe.wait_ge(s_free, att_filled(op, c) - 1)
            if i == 0:
                pe.wait_ge(win_ok, c)
            r = slice(kv * HD, (kv + 1) * HD)
            for j in range(2):
                last = MM(ps[:, AS + j, 0:META + 2 * P], qblk[r, u, j0 + j, :], kwin[r, u, :], start=True, stop=True)
            last.then_inc(s_full, 1)

        def prob_T(c, i):
            kv, j0 = i // 2, 2 * (i % 2)
            if i % 2 == 0:
                pe.wait_ge(p_free, (c - 1) * 2 + (kv + 1))
            pe.wait_ge(pr_ok, (c - 1) * 4 + (i + 1))
            for j in range(2):
                o = slice((j0 + j) * P, (j0 + j + 1) * P)
                TR(ps[0:META, APB, o], prob[:, i % 2, j, 0:META], ident[:])
                for b in range(2):
                    last = TR(ps[:, APB + 1 + b, o], prob[:, i % 2, j, META + b * P:META + (b + 1) * P], ident[:])
            if i % 2:
                last.then_inc(p_full, 1)

        def att_out(c, kv, u):
            op = f"O{kv}"
            pe.wait_ge(s_free, att_filled(op, c) - 1)
            pe.wait_ge(p_free, (c - 1) * 2 + (kv + 2))
            r = slice(kv * HD, (kv + 1) * HD)
            MM(ps[r, AS, :], vmeta[:, r], pt[0:META, 0, :], start=True, stop=False)
            MM(ps[r, AS, :], vwin[u][:, 0, r], pt[:, 1, :], start=False, stop=False)
            MM(ps[r, AS, :], vwin[u][:, 1, r], pt[:, 2, :], start=False, stop=True).then_inc(s_full, 1)

        norms(0, META)
        for op in ("gam", "KK", "vT", "kT"):
            own(op, 0, 0, META)
        own("DnT", 0, 0, META, (dn_ok, 1))
        own("D2", 0, 0, META, ready("DnT", 0))
        own("D2T", 0, 0, META)
        own("D4", 0, 0, META, ready("D2", 0), ready("D2T", 0))
        own("D4T", 0, 0, META)
        own("M2", 0, 0, META, (m1_ok, 1))
        own("D8", 0, 0, META, ready("D4", 0), ready("D4T", 0))
        own("M3", 0, 0, META, ready("M2", 0))
        own("M4", 0, 0, META, ready("D8", 0), ready("M3", 0))
        fill("VN", 0, META, lambda h: MM(delta_bank("VN")[0:META, h, :], buf["M4"][0:META, h, 0:META],
                                         buf["vb0"][0:META, h, :], start=True, stop=True), ready("M4", 0))
        fill("dS", 0, META, lambda h: MM(delta_bank("dS")[:, h, :], buf["kd0"][0:META, h, :],
                                         buf["vn"][0:META, h, :], start=True, stop=True), ready("VN", 0))
        norms(1)
        for op in ("gam", "KK", "KQ", "vT", "kT"):
            own(op, 1, 1)

        def mixer(c, m, u, scan, front):
            w = 1 - u
            if scan:
                scan_of("KS", c - 1, w, ready("TT", c - 1))
                scan_of("P1", c - 1, w)
            own("DnT", c, u, P, (dn_ok, c + 1))
            score(c, 0, u)
            own("D2", c, u, P, ready("DnT", c))
            own("D2T", c, u)
            if scan:
                scan_of("VN", c - 1, w, ready("KS", c - 1))
            own("D4", c, u, P, ready("D2", c), ready("D2T", c))
            own("D4T", c, u)
            own("M2", c, u, P, (m1_ok, c + 1))
            if scan:
                scan_of("dS", c - 1, w, ready("VN", c - 1))
            own("D8", c, u, P, ready("D4", c), ready("D4T", c))
            if scan:
                scan_of("P2", c - 1, w)
            own("M3", c, u, P, ready("M2", c))
            score(c, 1, u)
            own("M4", c, u, P, ready("D8", c), ready("M3", c))
            prob_T(c, 0)
            own("B", c, u, P, ready("M4", c), (de_ok, c + 1))
            own("BT", c, u)
            if front:
                norms(c + 1)
                own("gam", c + 1, w)
            prob_T(c, 1)
            if scan:
                scan_of("oT", c - 1, w, (on_ok, c - 1))
            own("B2", c, u, P, ready("B", c), ready("BT", c))
            own("B2T", c, u)
            own("Ninv", c, u)
            att_out(c, 0, u)
            if front:
                own("KK", c + 1, w)
            own("W2", c, u, P, ready("B2", c), (w1_ok, c))
            score(c, 2, u)
            own("B4", c, u, P, ready("B2T", c))
            if front:
                own("KQ", c + 1, w)
            own("W3", c, u, P, ready("B4", c), ready("W2", c))
            score(c, 3, u)
            if front:
                own("vT", c + 1, w)
            own("TT", c, u, P, ready("Ninv", c), ready("W3", c))
            prob_T(c, 2)
            if front:
                own("kT", c + 1, w)
            prob_T(c, 3)
            att_out(c, 1, u)

        def last_scan(c, u):
            scan_of("KS", c, u, ready("TT", c))
            scan_of("P1", c, u)
            scan_of("VN", c, u, ready("KS", c))
            scan_of("dS", c, u, ready("VN", c))
            scan_of("P2", c, u)
            scan_of("oT", c, u, (on_ok, c))
        mixer_steps(pe, mixer, last_scan)

        pe.wait_ge(y_l, 2)

        def merge(n, m, u):
            wait(pe, w_lo, n + 1)
            wait(pe, evac[u], m)
            dense(n, m, u, y_hi, y_lo, 0, ks=range(0, 4), bank=0)
            dense(n, m, u, y_hi, y_lo, 0, ks=range(4, 8), bank=2).then_inc(mm_done, 1)
        steps(pe, N_MERGE, N_OUT, merge)
        pe.wait_ge(m_l, KT)
        steps(pe, N_OUT, N_FF, lambda n, m, u: dense(n, m, u, m_hi, m_lo, 0).then_inc(mm_done, 1))

        def rms(r, slot_tiles):
            for u in range(2):
                pe.wait_ge(evac[u], slot_tiles)
            pe.wait_ge(o_acc, r * KT)
            for t in range(NT):
                last = MM(ps[:, 7, t:t + 1], acc[:, t * P:(t + 1) * P], ones[:, 0:1], start=True, stop=True)
            last.then_inc(n_mm, 1)
            pe.wait_ge(n_dg, r)
            for b in range(2):
                last = MM(ps[:, 5 + b, :], ones[:], sqt[:, b * HALF:(b + 1) * HALF], start=True, stop=True)
            last.then_inc(n_bc, 1)
        rms(1, N_FF // 2)
        pe.wait_ge(xt_in, 16)
        for k in range(KT):
            if k >= 2:
                pe.wait_ge(x2_ok, k - 1)
            for t in range(NT):
                last = TR(banks(2 * (k % 2))[:, t * P:(t + 1) * P], xtok[:, t, k * P:(k + 1) * P], ident[:])
            last.then_inc(xt_ps, 1)
        rms(2, N_FF // 2)
        pe.wait_ge(f_l, KT)
        pe.wait_ge(x2_ok, KT)
        pe.wait_ge(n_rb, 2)
        n0, done = N_FF, 0
        for gi, sz in enumerate(FF_GROUPS):
            steps(pe, n0, n0 + 2 * sz, lambda n, m, u: dense(n, m, u, f_hi, f_lo, 0).then_inc(mm_done, 1))
            done += sz
            pe.wait_ge(u_l, done)
            n1 = n0 + 2 * sz
            steps(pe, n1, n1 + KT, lambda n, m, u: dense(n, m, u, u_hi, u_lo, 0, nk=sz).then_inc(mm_done, 1))
            n0 = n1 + KT
        rms(3, n0 // 2)
        pe.wait_ge(n_rb, 3)
        pe.wait_ge(x3_ok, KT)

        def out_T(t, m, u):
            if not (isinstance(t, int) and t < 2):
                pe.wait_ge(ot_ok, t - 1)
            for k in range(KT):
                last = TR(banks(2 * u)[:, k * P:(k + 1) * P], facc[:, k, t * P:(t + 1) * P], ident[:])
            last.then_inc(ot_ps, 1)
        for t in range(NT):
            out_T(t, t // 2, t % 2)

    block.__exit__(None, None, None)


_INS = ["x", "meta_tokens", "w_in", "b_in", "conv_w", "a_log", "dt_bias", "dn_norm_w", "att_sinks", "w_att_out",
        "w_dn_out", "w_out", "norm_mix_pre", "norm_mix_post", "norm_ffn_pre", "norm_ffn_post", "w_ffn_in", "w_ffn_out"]


def kernel(**inputs):
    import numpy as _np
    import concourse.bacc as _bacc
    from concourse import mybir as _mybir
    from concourse.bass_utils import run_bass_kernel_spmd as _run

    nc = _bacc.Bacc("TRN2", target_bir_lowering=False, num_devices=1)
    arrays, args = {}, []
    for name in _INS:
        a = _np.ascontiguousarray(inputs[name])
        if name != "meta_tokens":
            a = a[0]
        arrays[f"in_{name}"] = a
        args.append(nc.dram_tensor(f"in_{name}", a.shape, _mybir.dt.from_np(a.dtype), kind="ExternalInput").ap())
    result = nc.dram_tensor("out_0", (1, TOK, D), _mybir.dt.float32, kind="ExternalOutput").ap()
    build(nc, *args, result[0])
    r = _run(nc, [arrays], core_ids=[0])
    return r.results[0]["out_0"]
```

```python
import concourse.bass as bass
from concourse import mybir
import numpy as np

F32 = mybir.dt.float32
F32R = mybir.dt.float32r
ACT = mybir.ActivationFunctionType
ALU = mybir.AluOpType
AX = mybir.AxisListType

P = 128
D = 1024
KT = D // P
TOK = 1024
NT = TOK // P
META = 16
LW = META + TOK
HALF = 512
THIRD = 352
LAST = LW - 2 * THIRD
FF = 2816
EPS = 1e-6
NEG = -1.0e30
DH = 4
HD = 64
GRP = 4
Q0, K0, V0, DN0, DZ0, DAB0, G0 = 0, 512, 640, 768, 2304, 2816, 2824

N_KV, N_Q, N_DN, N_DZ, N_G, N_MERGE, N_OUT, N_FF = 0, 2, 6, 18, 22, 38, 46, 54
POOL_ADDS = 3
FF_GROUPS = [8, 8, 6]
R_BIAS, R_BG, R_PRE, R_POST, R_FPRE, R_FPOST, R_DNW, R_CONV = 0, 22, 38, 46, 54, 62, 70, 71
NROWS = R_CONV + 48

DELTA_OPS = [("KS", 0), ("P1", 1), ("DnT", 2), ("D2", 0), ("D2T", 1), ("VN", 2), ("D4", 0), ("D4T", 1), ("M2", 2),
             ("dS", 0), ("D8", 1), ("P2", 2), ("M3", 0), ("M4", 1), ("B", 2), ("BT", 0), ("gam", 1),
             ("B2", 2), ("B2T", 0), ("Ninv", 1), ("W2", 2), ("oT", 0), ("KK", 1), ("B4", 2), ("KQ", 0),
             ("W3", 2), ("vT", 0), ("TT", 2), ("kT", 0)]
SCAN = ["KS", "VN", "P1", "dS", "P2", "oT"]
FRONT = ["gam", "KK", "KQ", "vT", "kT"]
META_OPS = ["gam", "KK", "vT", "kT", "DnT", "D2", "D2T", "D4", "D4T", "M2", "D8", "M3", "M4", "VN", "dS"]
ATT_OPS = ["S00", "S01", "S10", "O0", "S11", "O1"]


def lane_of(op):
    return dict(DELTA_OPS)[op]


def ops_in(step, lane):
    every = [o for o, l in DELTA_OPS if l == lane]
    front = [o for o in every if o in FRONT]
    scan = [o for o in every if o in SCAN]
    if step == 0:
        return [(o, 0) for o in META_OPS if lane_of(o) == lane] + [(o, 1) for o in front]
    if step == NT + 1:
        return [(o, NT) for o in scan if o != "dS"]
    part = [o for o in every if (step > 1 or o not in scan) and (step < NT or o not in front)]
    return [(o, step + (o in front) - (o in scan)) for o in part]


def filled(op, c):
    lane = lane_of(op)
    if isinstance(c, int):
        order = [o for step in range(NT + 2) for o in ops_in(step, lane)]
        return order.index((op, c)) + 1
    step = c + (op in SCAN) - (op in FRONT)
    every = [o for o, l in DELTA_OPS if l == lane]
    done = len(ops_in(0, lane)) + len(ops_in(1, lane))
    return (step - 2) * len(every) + (done + every.index(op) + 1)


def att_filled(op, c):
    return (c - 1) * len(ATT_OPS) + (ATT_OPS.index(op) + 2)


def build(nc, x, meta, w_in, b_in, conv_w, a_log, dt_bias, dn_norm_w, att_sinks, w_att, w_dn, w_out,
          n_pre, n_post, f_pre, f_post, w_fi, w_fo, out):
    qkv_d = nc.dram_tensor("qkv_scratch", [12, P, LW], F32, kind="Internal").ap()
    gate_d = nc.dram_tensor("gate_scratch", [16, P, TOK], F32, kind="Internal").ap()
    x2_d = nc.dram_tensor("x2_scratch", [8, P, TOK], F32, kind="Internal").ap()

    top = [(nc.sbuf_base + 31) // 32 * 32]

    def at(name, shape, dt, offset):
        t = nc.alloc_sbuf_tensor_at(name, shape, dt, offset=offset)
        return t

    def keep(name, shape, dt=F32):
        size = 4 * int(np.prod(shape[1:]))
        t = at(name, shape, dt, top[0])
        top[0] += (size + 31) // 32 * 32
        return t

    def region(start, size):
        cur = [start]

        def take(name, shape, dt=F32):
            n = 4 * int(np.prod(shape[1:]))
            t = at(name, shape, dt, cur[0])
            cur[0] += (n + 31) // 32 * 32
            assert cur[0] <= start + size, (name, cur[0] - start, size)
            return t
        return take

    raw = keep("w_raw", [P, 2, KT, P])
    whi = keep("w_hi", [P, 2, KT, P], F32R)
    wlo = keep("w_lo", [P, 2, KT, P], F32R)
    ident = keep("ident", [P, P])
    upper = keep("upper_ones", [P, P])
    ones = keep("ones", [P, P])
    mask_up = keep("mask_up", [P, P])
    mask_low = keep("mask_low", [P, P])
    blocks16 = keep("blocks16", [P, P])
    band = keep("band", [P, META + 2 * P])
    band_now = keep("band_now", [P, META + 2 * P])
    params = keep("params", [P, P])
    wd_raw = keep("wd_raw", [P, KT, 8])
    wd_hi = keep("wd_hi", [P, KT, 8], F32R)
    wd_lo = keep("wd_lo", [P, KT, 8], F32R)
    dab_b = keep("dab_bias", [P, 8])
    dtb = keep("dt_bias_bc", [P, 4])
    alog = keep("a_log_bc", [P, 4])
    sink = keep("sink_bc", [P, 8])
    half = keep("minus_half", [P, 1])
    cols = keep("cols", [P, NT + 1, 44])
    fcols = keep("front_cols", [P, 2, 20])
    scols = keep("scan_cols", [P, 2, 20])
    rr = keep("inverse_norms", [P, NT + 1, 8])
    tiny = keep("tiny", [P, 96])
    small = keep("small", [P, 96])
    dabx = keep("dab", [P, NT + 1, 8])
    dabe = keep("dab_exp", [P, NT + 1, 8])
    R0 = top[0]
    R1 = R0 + 2 * KT * LW * 4
    R2 = R1 + 65536
    R3 = R2 + 32768
    end = nc.sbuf_usable_end
    assert end - R3 >= 12288, (end, R3, end - R3)

    take = region(R0, R1 - R0)
    h_hi = take("h_hi", [P, KT, LW], F32R)
    h_lo = take("h_lo", [P, KT, LW], F32R)
    take = region(R1, R2 - R1)
    aq = take("att_q", [P, GRP, TOK])
    ak = take("att_k", [P, P + TOK])
    av = take("att_v", [P, P + TOK])
    vtok = take("att_v_tokens", [P, NT + 1, P])
    gz = take("dn_gate", [P, DH, TOK])
    kwin = take("k_window", [P, 2, META + 2 * P])
    qblk = take("q_block", [P, 2, GRP, P])
    vwin = [take("v_window0", [P, 2, P])]
    vmeta = take("v_meta", [META, P])
    prob = take("prob", [P, 2, 2, META + 2 * P])
    pt = take("prob_T", [P, 3, GRP * P])
    dabT = pt[0:8].rearrange("p a b -> p (a b)")[:, 0:LW]
    take = region(R2, R3 - R2)
    xmeta = take("x_meta", [META, D])
    xn = take("x_norm", [P, 2, D])
    xw = take("x_weighted", [P, 2, D])
    prow = take("param_rows", [P, P])
    take = region(R3, end - R3)
    xsq = take("x_square", [P, 2, D])
    take = region(R2 - 4 * NT * D, 4 * NT * D)
    xin = take("x_in", [P, NT, D])
    take = region(R2, R3 - R2)
    rawc = take("conv_in", [P, 2, 3 + LW])
    cv = take("conv_sum", [P, 2, LW])
    cs = take("stored", [P, 2, LW])
    take = region(R3, end - R3)
    sqc = take("qk_squares", [P, 2, LW])
    take = region(R0, R1 - R0)
    qkv = take("qkv", [P, 2, 12, P])
    names = ["X1", "X2", "X3", "X4", "X5", "X6", "X7", "X8", "En", "Ninv", "TT0", "t1", "DT", "DL", "attT0",
             "vb0", "kd0", "Z", "vn", "o1", "osq", "S"]
    buf = {k: take("b_" + k, [P, DH, P]) for k in names}
    vwin.append(take("v_window1", [P, 2, P]))
    where = dict(Dn="X1", B="X1", DnT="X2", BT="X2", D2="X3", D8="X3", B2="X3", D2T="X4", B2T="X4", D4="X5",
                 B4="X5", D4T="X6", M1="X7", M3="X7", W1="X7", W3="X7", M2="X8", M4="X8", W2="X8")
    for k, v in where.items():
        buf[k] = buf[v]
    take = region(R3, end - R3)
    buf.update({k: take("b_" + k, [P, DH, P]) for k in ("TT1", "attT1", "vb1", "kd1", "op", "on")})
    take = region(R2, R3 - R2)
    ya = take("y_att", [P, GRP, TOK])
    yd = take("y_dn", [P, DH, TOK])
    take = region(R0, R1 - R0)
    y_hi = take("y_hi", [P, KT, TOK], F32R)
    y_lo = take("y_lo", [P, KT, TOK], F32R)
    take = region(R1, R2 - R1)
    m_hi = take("m_hi", [P, KT, TOK], F32R)
    m_lo = take("m_lo", [P, KT, TOK], F32R)
    take = region(R2, R3 - R2)
    gin = take("gates_in", [P, 2, 2, TOK])
    mt = take("merge_parts", [P, 2, TOK])
    take = region(R2, R3 - R2)
    oT = take("o_T", [P, KT, TOK])
    take = region(R3, end - R3)
    sqt = take("square", [P, 2, TOK])
    rb = take("rms_bc", [P, TOK])
    acc = at("square_sum", [P, TOK], F32, R0 + 4 * KT * TOK)
    take = region(R0, R1 - R0)
    xtok = take("x_tokens", [P, NT, D])
    take = region(R1, R2 - R1)
    f_hi = take("f_hi", [P, KT, TOK], F32R)
    f_lo = take("f_lo", [P, KT, TOK], F32R)
    take = region(R0, R1 - R0)
    u_hi = take("u_hi", [P, KT, TOK], F32R)
    u_lo = take("u_lo", [P, KT, TOK], F32R)
    take = region(R2, R3 - R2)
    facc = take("ffn_sum", [P, KT, TOK])
    take = region(R3, end - R3)
    sg = take("silu_gate", [P, TOK])
    up = take("hidden", [P, TOK])
    take = region(R1, R2 - R1)
    x2b = take("x2_back", [P, KT, TOK])
    otile = take("out_tile", [P, 4, D])

    ps = nc.alloc_psum_tensor("ps", [P, 8, HALF], F32)
    AS, APB = 0, 2

    def sem(name):
        return nc.alloc_semaphore(name)

    raw_in = [sem("raw_in0"), sem("raw_in1")]
    w_hi, w_lo = sem("w_hi"), sem("w_lo")
    mm_done = sem("mm_done")
    evac = [sem("evac0"), sem("evac1")]
    x_in = [sem("x_in0"), sem("x_in1")]
    x_sum, x_rs, x_nrm, x_tr, x_wt, x_hi, x_lo = (sem("x_sum"), sem("x_rs"), sem("x_nrm"), sem("x_tr"), sem("x_wt"),
                                                  sem("x_hi"), [sem("x_lo0"), sem("x_lo1")])
    par_in, par_tr, par_ok, wd_in, wd_h, wd_l = (sem("par_in"), sem("par_tr"), sem("par_ok"), sem("wd_in"),
                                                 sem("wd_h"), sem("wd_l"))
    consts, bc_in = sem("consts"), sem("bc_in")
    conv_in, conv_ok, silu_ok = sem("conv_in"), sem("conv_ok"), sem("silu_ok")
    dz_ok, gz_ok = sem("dz_ok"), sem("gz_ok")
    stored = [sem("stored0"), sem("stored1")]
    dab_cp, dab_tr = sem("dab_cp"), sem("dab_tr")
    dab_mm, dab_add, dab_act, dab_g, cum_mm, cols_ok = (sem("dab_mm"), sem("dab_add"), sem("dab_act"), sem("dab_g"),
                                                        sem("cum_mm"), sem("cols_ok"))
    full = [sem("lane0_full"), sem("lane1_full"), sem("lane2_full")]
    free = [sem("lane0_read"), sem("lane1_read"), sem("lane2_read")]
    s_full, s_free, p_full, p_free = sem("score_full"), sem("score_read"), sem("probT_full"), sem("probT_read")
    qkv_in = [sem("qkv_in0"), sem("qkv_in1")]
    qk_sq, qk_sum, norm_ok, col_ok = sem("qk_sq"), sem("qk_sum"), sem("norm_ok"), sem("col_ok")
    a1_ok, a2_ok, dt_ok, dl_ok, dn_ok, de_ok, m1_ok, w1_ok = (
        sem("a1_ok"), sem("a2_ok"), sem("dt_ok"), sem("dl_ok"), sem("dn_ok"), sem("de_ok"), sem("m1_ok"),
        sem("w1_ok"))
    ored_ok, on_ok = sem("ored_ok"), sem("on_ok")
    win_ok, nm_ok, ex_ok, rec_ok, pr_ok = sem("win_ok"), sem("nm_ok"), sem("ex_ok"), sem("rec_ok"), sem("pr_ok")
    y_h, y_l, gate_in = sem("y_h"), sem("y_l"), [sem("gate_in0"), sem("gate_in1")]
    mrg, m_h, m_l = sem("mrg"), sem("m_h"), sem("m_l")
    o_sq, o_sum, xt_in = sem("o_sq"), sem("o_sum"), sem("xt_in")
    n_bc, n_add, n_rb = sem("n_bc"), sem("n_add"), sem("n_rb")
    xt_ps, x2_ok, x2_st, f_h, f_l = sem("xt_ps"), sem("x2_ok"), sem("x2_st"), sem("f_h"), sem("f_l")
    gr_ok, sg_ok, up_ok, u_h, u_l = sem("gr_ok"), sem("sg_ok"), sem("up_ok"), sem("u_h"), sem("u_l")
    fa_ok, x2_back, x3_ok = sem("fa_ok"), sem("x2_back"), sem("x3_ok")
    o_sc, x3_pool = sem("o_sc"), sem("x3_pool")
    ot_ps, ot_ok = sem("ot_ps"), [sem(f"ot_ok{i}") for i in range(4)]
    out_st = [sem(f"out_st{i}") for i in range(4)]

    yd_ok = sem("yd_ok")
    Y_PARTS = [(ya, slice(0, TOK), slice(0, 4)), (yd, slice(0, TOK - P), slice(4, 8)),
               (yd, slice(TOK - P, TOK), slice(4, 8))]
    TR = nc.tensor.transpose
    MM = nc.tensor.matmul

    def wait(eng, s, value):
        if isinstance(value, int) and value <= 0:
            return
        eng.wait_ge(s, value)

    def settle(eng):
        eng.wait_ge(consts, 1)

    def steps(eng, first, last, body, peel=0):
        for n in range(first, first + peel):
            body(n, n // 2, n % 2)
        s = first + peel
        if s == last:
            return
        assert (last - s) % 2 == 0
        if last - s == 2:
            for n in (s, s + 1):
                body(n, n // 2, n % 2)
            return
        with eng.Fori(0, (last - s) // 2) as i:
            for u in (0, 1):
                body(i * 2 + (s + u), i + (s + u) // 2, (s + u) % 2)

    def mixer_steps(eng, step, scan):
        step(1, 0, 1, False, True)
        steps(eng, 2, NT, lambda c, m, u: step(c, m, u, True, True))
        step(NT, NT // 2, NT % 2, True, False)
        scan(NT, NT % 2)

    def delta_bank(op):
        return ps[:, 5 + lane_of(op), :].rearrange("p (h c) -> p h c", h=DH)

    def banks(b, n=2):
        return ps[:, b:b + n, :].rearrange("p a b -> p (a b)")

    def split_hi(n1, m1, u1):
        wait(nc.scalar, raw_in[u1], (m1 + 1) * 48)
        wait(nc.scalar, mm_done, n1 - 1)
        nc.scalar.activation(whi[:, u1], raw[:, u1], ACT.Copy).then_inc(w_hi, 1)

    def split_lo(n1, m1, u1):
        wait(nc.vector, w_hi, n1 + 1)
        nc.vector.tensor_tensor(wlo[:, u1], raw[:, u1], whi[:, u1].bitcast(F32), ALU.subtract).then_inc(w_lo, 1)

    def lo_part(engine, t, u, c, w=P):
        engine.tensor_tensor(h_lo[:, :, bass.ds(c, w)], xw[:, u, 0:KT * w].rearrange("p (k c) -> p k c", k=KT),
                             h_hi[:, :, bass.ds(c, w)].bitcast(F32), ALU.subtract).then_inc(x_lo[u], 1)

    def after(n, m, u):
        return (n + 1, m + u, 1 - u)

    def dense(n, m, u, hi, lo, c0, nk=KT, meta_cols=False, ks=None, bank=0, arrive=None,
              arrive_group=None):
        if ks is None:
            wait(nc.tensor, w_lo, n + 1)
            wait(nc.tensor, evac[u], m)
            ks = list(range(nk))
        groups = [(4 * u + bank + b, c0 + b * HALF, HALF) for b in range(2)]
        if meta_cols:
            groups = [(4 * u + b, b * THIRD, (THIRD, THIRD, LAST)[b]) for b in range(3)]

        def chunk(k, b, c, w):
            for i, (a, mv) in enumerate(((whi, hi), (whi, lo), (wlo, hi))):
                last = MM(ps[:, b, 0:w], a[:, u, k, :], mv[:, k, c:c + w],
                          start=(k == ks[0] and i == 0), stop=(k == ks[-1] and i == 2))
            return last
        if arrive_group:
            for b, c, w in groups:
                arrive_group(c + w)
                for k in ks:
                    last = chunk(k, b, c, w)
        elif arrive:
            for k in ks:
                arrive(k)
                for b, c, w in groups:
                    last = chunk(k, b, c, w)
        else:
            for b, c, w in groups:
                for k in ks:
                    last = chunk(k, b, c, w)
        return last

    block = nc.Block()
    block.__enter__()

    @block.sync
    def _(sp):
        sp.dma_start(xmeta[:], meta).then_inc(x_in[0], 16)
        sp.dma_start(xin[:, 0, :], x[0:P, :]).then_inc(x_in[1], 16)
        bq = b_in[Q0:Q0 + 512].rearrange("(g j c) -> g j c", g=2, c=HD)
        sp.dma_start(prow[0:GRP, 0:HD], bq[0]).then_inc(par_in, 16)
        sp.dma_start(prow[0:GRP, HD:P], bq[1]).then_inc(par_in, 16)
        for dst, cnt, src in ((GRP, 18, b_in[K0:DAB0]), (R_BG, 16, b_in[G0:G0 + 2048]), (R_PRE, 8, n_pre),
                              (R_POST, 8, n_post), (R_FPRE, 8, f_pre), (R_FPOST, 8, f_post), (R_DNW, 1, dn_norm_w),
                              (R_CONV, 48, conv_w.rearrange("k c -> (k c)"))):
            sp.dma_start(prow[dst:dst + cnt, :], src.rearrange("(t p) -> t p", p=P)).then_inc(par_in, 16)

        def load(n, m, u, pieces):
            wait(sp, w_lo, n - 1)
            for dst, src in pieces:
                sp.dma_start(dst, src).then_inc(raw_in[u], 48 // len(pieces))

        def w_cols(w, c):
            return w[:, bass.ds(c, P)].rearrange("(k p) c -> p k c", p=P)

        def kv_w(n, m, u):
            load(n, m, u, [(raw[:, u], w_cols(w_in, (n - N_KV) * P + K0))])

        def q_w2(n, m, u):
            j = n - N_Q
            wait(sp, w_lo, n - 1)
            for g in range(2):
                sp.dma_start(raw[:, u, :, g * HD:(g + 1) * HD],
                             w_in[:, bass.ds(j * HD + g * GRP * HD, HD)].rearrange("(k p) c -> p k c", p=P)
                             ).then_inc(raw_in[u], 16 + 16 * g)

        def dn_w(n, m, u):
            load(n, m, u, [(raw[:, u], w_cols(w_in, (n - N_DN) * P + DN0))])

        def g_w(n, m, u):
            load(n, m, u, [(raw[:, u], w_cols(w_in, (n - N_G) * P + G0))])

        def merge_w(n, m, u):
            wait(sp, w_lo, n - 1)
            c = (n - N_MERGE) * P
            for g in range(2):
                src = w_att[g * GRP * HD:(g + 1) * GRP * HD, bass.ds(c, P)].rearrange("(j p) c -> p j c", p=HD)
                sp.dma_start(raw[g * HD:(g + 1) * HD, u, 0:4, :], src).then_inc(raw_in[u], 16)
            sp.dma_start(raw[:, u, 4:8, :], w_dn[:, bass.ds(c, P)].rearrange("(k p) c -> p k c", p=P)
                         ).then_inc(raw_in[u], 16)

        def out_w(n, m, u):
            load(n, m, u, [(raw[:, u], w_cols(w_out, (n - N_OUT) * P))])

        def x_load(t, m, u):
            sp.wait_ge(x_in[u], m * 16)
            sp.dma_start(xin[:, bass.ds(t - 1, 1), :].rearrange("p a c -> p (a c)"),
                         x[bass.ds((t - 1) * P, P), :]).then_inc(x_in[u], 16)
        steps(sp, 2, NT + 1, x_load, peel=1)
        kv_w(0, 0, 0)
        kv_w(1, 0, 1)
        for dst, src in ((dab_b, b_in[DAB0:DAB0 + 8]), (dtb, dt_bias), (alog, a_log), (sink, att_sinks)):
            sp.dma_start(dst[:], src.rearrange("(a c) -> a c", a=1).to_broadcast([P, src.shape[0]])).then_inc(bc_in, 16)
        sp.dma_start(wd_raw[:], w_in[:, DAB0:DAB0 + 8].rearrange("(k p) c -> p k c", p=P)).then_inc(wd_in, 16)

        for n in range(N_Q, N_DN):
            q_w2(n, n // 2, n % 2)
        dn_w(N_DN, N_DN // 2, 0)
        dn_w(N_DN + 1, N_DN // 2, 1)

        def store_qkv(j, parity):
            sp.wait_ge(silu_ok, j + 1)
            sp.dma_start(qkv_d[bass.ds(j, 1)].rearrange("a p c -> p (a c)"), cs[:, parity, :]).then_inc(stored[parity], 16)

        def dn_step(n, m, u):
            dn_w(n, m, u)
            store_qkv(n - 2 - N_DN, u)
        steps(sp, N_DN + 2, N_DZ, dn_step)

        def dz_w(n, m, u):
            load(n, m, u, [(raw[:, u], w_cols(w_in, (n - N_DZ) * P + DZ0))])
            if n < N_DZ + 2:
                store_qkv(n - 2 - N_DN, u)
        for n in range(N_DZ, N_G):
            dz_w(n, n // 2, n % 2)
        g_w(N_G, N_G // 2, 0)
        g_w(N_G + 1, N_G // 2, 1)

        def g_step(n, m, u):
            if not (isinstance(n, int) and n >= N_MERGE):
                g_w(n, m, u)
            else:
                merge_w(n, m, u)
            sp.wait_ge(silu_ok, n - 2 - N_G + 13)
            sp.dma_start(gate_d[bass.ds(n - 2 - N_G, 1)].rearrange("a p c -> p (a c)"), cs[:, u, 0:TOK]
                         ).then_inc(stored[u], 16)
        steps(sp, N_G + 2, N_MERGE, g_step)
        g_step(N_MERGE, N_MERGE // 2, 0)
        g_step(N_MERGE + 1, N_MERGE // 2, 1)

        sp.wait_ge(mm_done, N_MERGE)
        for u in range(2):
            sp.wait_ge(stored[u], 16 * 14)
        sp.dma_start(qkv[:, 0, :, 0:META], qkv_d[:, :, 0:META].rearrange("t p c -> p t c")).then_inc(qkv_in[0], 16)

        def chunk_load(c, m, u):
            if isinstance(c, int) and c == 2:
                sp.wait_ge(full[lane_of("dS")], filled("dS", 0))
            elif not (isinstance(c, int) and c == 1):
                wait(sp, full[lane_of("P1")], filled("P1", c - 2))
            sp.dma_start(qkv[:, u], qkv_d[:, :, bass.ds((c - 1) * P + META, P)].rearrange("t p c -> p t c")
                         ).then_inc(qkv_in[u], 16)
        steps(sp, 1, NT + 1, chunk_load, peel=2)

        def gates_load(n, m, u):
            if isinstance(n, int) and n < N_MERGE + 2:
                sp.wait_ge(y_l, 3)
                sp.wait_ge(y_h, 3)
            else:
                sp.wait_ge(mrg, n - N_MERGE - 1)
            j = n - N_MERGE
            for g in range(2):
                sp.dma_start(gin[:, u, g, :], gate_d[bass.ds(j + 8 * g, 1)].rearrange("a p c -> p (a c)")
                             ).then_inc(gate_in[u], 16)
        gates_load(N_MERGE, N_MERGE // 2, 0)
        gates_load(N_MERGE + 1, N_MERGE // 2, 1)

        def merge_step(n, m, u):
            merge_w(n, m, u)
            gates_load(n, m, u)
        steps(sp, N_MERGE + 2, N_OUT, merge_step)
        out_w(N_OUT, N_OUT // 2, 0)
        out_w(N_OUT + 1, N_OUT // 2, 1)
        sp.wait_ge(mm_done, N_OUT)
        sp.dma_start(xtok[:], x.rearrange("(t p) d -> p t d", p=P)).then_inc(xt_in, 16)
        steps(sp, N_OUT + 2, N_FF, out_w)

        def ffn_weights(n0, s0, sz):
            def in_w(n, m, u):
                c = (m - n0 // 2 + s0) * P + u * FF
                load(n, m, u, [(raw[:, u], w_cols(w_fi, c))])

            def out_w2(n, m, u):
                load(n, m, u, [(raw[:, u, 0:sz, :],
                                w_fo[s0 * P:(s0 + sz) * P, bass.ds((n - n0 - 2 * sz) * P, P)]
                                .rearrange("(k p) c -> p k c", p=P))])
            return in_w, out_w2

        n0 = N_FF
        for gi, sz in enumerate(FF_GROUPS):
            in_w, out_w2 = ffn_weights(n0, sum(FF_GROUPS[:gi]), sz)
            if gi == 0:
                in_w(n0, n0 // 2, 0)
                in_w(n0 + 1, n0 // 2, 1)
                in_w(n0 + 2, n0 // 2 + 1, 0)
                in_w(n0 + 3, n0 // 2 + 1, 1)
                sp.wait_ge(x2_ok, KT)
                sp.dma_start(x2_d.rearrange("t p c -> p t c"), oT[:]).then_inc(x2_st, 16)
                steps(sp, n0 + 4, n0 + 2 * sz, in_w)
            else:
                steps(sp, n0, n0 + 2 * sz, in_w)
            steps(sp, n0 + 2 * sz, n0 + 2 * sz + KT, out_w2)
            n0 += 2 * sz + KT
        sp.wait_ge(x2_st, 16)
        sp.wait_ge(mm_done, n0 - KT)
        sp.dma_start(x2b[:], x2_d.rearrange("t p c -> p t c")).then_inc(x2_back, 16)

        for t in range(NT):
            sp.wait_ge(ot_ok[t % 4], t // 4 + 1)
            sp.dma_start(out[t * P:(t + 1) * P, :], otile[:, t % 4, :]).then_inc(out_st[t % 4], 16)
        for u in range(4):
            sp.wait_ge(out_st[u], 16 * (NT // 4))

    @block.gpsimd
    def _(pool):
        g = nc.gpsimd
        g.memset(ones[:], 1.0)
        g.memset(half[:], -0.5)
        g.memset(small[:, 4:5], 1.0 / D)
        g.memset(small[:, 5:6], EPS)
        g.memset(band[:], 0.0)
        g.memset(mask_up[:], 0.0)
        g.memset(mask_low[:], 0.0)
        g.memset(ident[:], 0.0)
        g.memset(upper[:], 1.0)
        g.memset(blocks16[:], 1.0)
        g.memset(ak[:, 0:P - META], 0.0)
        g.memset(av[:, 0:P - META], 0.0)
        g.memset(vtok[:, 0, :], 0.0)
        g.drain()
        g.affine_select(out=ident[:], in_=ident[:], compare_op=ALU.not_equal, fill=1.0, base=0,
                        pattern=[[-1, P]], channel_multiplier=1).then_inc(consts, 1)
        g.affine_select(out=upper[:], in_=upper[:], compare_op=ALU.is_ge, fill=0.0, base=0,
                        pattern=[[1, P]], channel_multiplier=-1)
        g.affine_select(out=mask_up[:], in_=mask_up[:], compare_op=ALU.is_ge, fill=NEG, base=0,
                        pattern=[[1, P]], channel_multiplier=-1)
        g.affine_select(out=mask_low[:], in_=mask_low[:], compare_op=ALU.is_gt, fill=NEG, base=0,
                        pattern=[[-1, P]], channel_multiplier=1)
        b3 = blocks16[:].rearrange("p (b c) -> p b c", c=16)
        g.affine_select(out=b3, in_=b3, compare_op=ALU.is_ge, fill=0.0, base=0,
                        pattern=[[-16, 8], [0, 16]], channel_multiplier=1)
        g.drain()
        g.affine_select(out=b3, in_=b3, compare_op=ALU.is_ge, fill=0.0, base=15,
                        pattern=[[16, 8], [0, 16]], channel_multiplier=-1)
        g.affine_select(out=band[:, META:META + P], in_=band[:, META:META + P], compare_op=ALU.is_gt, fill=NEG,
                        base=0, pattern=[[1, P]], channel_multiplier=-1)
        g.affine_select(out=band[:, META + P:], in_=band[:, META + P:], compare_op=ALU.is_ge, fill=NEG,
                        base=0, pattern=[[-1, P]], channel_multiplier=1)
        g.drain()
        g.tensor_copy(band_now[:], band[:])
        g.drain()
        g.memset(band_now[:, META:META + P], NEG).then_inc(consts, 1)

        def x_rsqrt(t, u, w=P):
            settle(pool)
            pool.wait_ge(x_sum, t + 1)
            if not (isinstance(t, int) and t < 2):
                pool.wait_ge(x_nrm, t - 1)
            g.tensor_tensor(small[0:w, 84 + u:85 + u], small[0:w, u:u + 1], small[0:w, 4:5], ALU.mult)
            g.drain()
            g.tensor_scalar(small[0:w, 84 + u:85 + u], small[0:w, 84 + u:85 + u], EPS, None, ALU.add)
            g.drain()
            g.tensor_tensor(small[0:w, 6 + u:7 + u], small[0:w, 84 + u:85 + u], half[0:w, :], ALU.pow).then_inc(x_rs, 1)

        def x_low(t, u, c, w=P):
            pool.wait_ge(x_hi, t + 1)
            lo_part(g, t, u, c, w)

        def x_step(t, m, u):
            x_rsqrt(t, u)
            if isinstance(t, int):
                x_low(0, 0, 0, META)
            elif u == 0:
                x_low(t - 2, u, (t - 3) * P + META)
        x_rsqrt(0, 0, META)
        x_rsqrt(1, 1)
        steps(pool, 2, NT + 1, x_step, peel=1)
        x_low(NT, 0, (NT - 1) * P + META)
        pool.wait_ge(x_lo[0], 5)
        pool.wait_ge(x_lo[1], 4)
        pool.wait_ge(par_tr, 1)
        g.memset(rawc[:, :, 0:3], 0.0).then_inc(consts, 1)

        def qk_square(j, m, u):
            pool.wait_ge(silu_ok, j + 1)
            if not (isinstance(j, int) and j < 2):
                pool.wait_ge(qk_sum, j - 1)
            g.tensor_tensor(sqc[:, u, :], cs[:, u, :], cs[:, u, :], ALU.mult).then_inc(qk_sq, 1)
        steps(pool, 0, 2 * DH, qk_square, peel=2)

        pool.wait_ge(dz_ok, DH)
        g.tensor_scalar(gz[:], gz[:], params[:, R_DNW:R_DNW + 1], None, ALU.mult).then_inc(gz_ok, 1)

        pool.wait_ge(norm_ok, 1)
        g.tensor_tensor(rr[:], rr[:], half[:].unsqueeze(2).to_broadcast([P, NT + 1, 8]), ALU.pow)
        g.drain()
        pool.wait_ge(cols_ok, 3)
        g.tensor_tensor(cols[:, :, 16:20], cols[:, :, 40:44], rr[:, :, 4:8], ALU.mult)
        g.tensor_scalar(cols[:, :, 32:36], rr[:, :, 0:4], float(P) ** -0.5, None, ALU.mult)
        g.drain()
        g.tensor_tensor(cols[:, :, 12:16], cols[:, :, 16:20], rr[:, :, 4:8], ALU.mult)
        g.tensor_tensor(cols[:, :, 36:40], cols[:, :, 32:36], cols[:, :, 32:36], ALU.mult)
        g.drain()
        g.tensor_scalar(cols[:, :, 12:16], cols[:, :, 12:16], -1.0, None, ALU.mult)
        g.drain()
        g.tensor_tensor(cols[:, :, 28:32], cols[:, :, 12:16], cols[:, :, 20:24], ALU.mult)
        g.drain()
        OF, OE = small[:, 44:48], small[:, 48:52]
        S2, S2S = ([scols[:, s, o:o + 4] for s in range(2)] for o in (12, 16))

        def front_cols(c, u):
            g.tensor_copy(fcols[:, u, :], cols[:, bass.ds(c, 1), 0:20].rearrange("p a c -> p (a c)")
                          ).then_inc(col_ok, 1)

        def scan_cols(c, u):
            g.tensor_copy(scols[:, u, :], cols[:, bass.ds(c, 1), 20:40].rearrange("p a c -> p (a c)"))

        def lower(c, L=P):
            pool.wait_ge(dn_ok, c + 1)
            g.tensor_tensor(buf["En"][0:L, :, 0:L], buf["t1"][0:L, :, 0:L], buf["Dn"][0:L, :, 0:L],
                            ALU.subtract).then_inc(de_ok, 1)

        def plus_one(dst, src, c, signal, L=P):
            pool.wait_ge(free[lane_of(src)], filled(src, c))
            g.tensor_tensor(buf[dst][0:L, :, 0:L], buf[src][0:L, :, 0:L],
                            ident[0:L, 0:L].unsqueeze(1).to_broadcast([L, DH, L]), ALU.add).then_inc(signal, 1)

        def out_norm(c, u):
            pool.wait_ge(ored_ok, c)
            g.tensor_tensor(OE, OE, S2S[u], ALU.mult)
            g.drain()
            g.tensor_scalar(OE, OE, 1.0 / P, EPS, ALU.mult, ALU.add)
            g.drain()
            g.tensor_tensor(OE, OE, half[:].to_broadcast([P, 4]), ALU.pow)
            g.drain()
            g.tensor_tensor(OF, OE, S2[u], ALU.mult)
            g.drain()
            g.tensor_tensor(buf["on"][:], buf["op"][:], OF.unsqueeze(2).to_broadcast([P, DH, P]),
                            ALU.mult).then_inc(on_ok, 1)

        def windows(c, u, first=False):
            if not first:
                pool.wait_ge(s_full, att_filled("O1", c - 2))
            g.tensor_copy(kwin[:, u, META:], ak[:, bass.ds((c - 1) * P, 2 * P)])
            g.tensor_copy(vwin[u][:], vtok[:, bass.ds(c - 1, 2), :])
            g.tensor_copy(qblk[:, u], aq[:, :, bass.ds((c - 1) * P, P)]).then_inc(win_ok, 1)

        def probs(c, i):
            pool.wait_ge(rec_ok, (c - 1) * 4 + (i + 1))
            pb = prob[:, i % 2]
            g.tensor_tensor(pb, pb, small[:, 56 + 2 * (i % 2):58 + 2 * (i % 2)].unsqueeze(2)
                            .to_broadcast([P, 2, META + 2 * P]), ALU.mult).then_inc(pr_ok, 1)

        def mixer(c, m, u, scan, front):
            plus_one("M1", "DnT", c, m1_ok)
            if front:
                front_cols(c + 1, 1 - u)
            scan_cols(c, u)
            probs(c, 0)
            if scan:
                out_norm(c - 1, 1 - u)
            probs(c, 1)
            plus_one("W1", "BT", c, w1_ok)
            if front:
                windows(c + 1, 1 - u)
            probs(c, 2)
            probs(c, 3)
            if front:
                lower(c + 1, P)

        def last_scan(c, u):
            out_norm(c, u)
        for c, L in ((0, META), (1, P)):
            front_cols(c, c)
            lower(c, L)
            if c == 0:
                plus_one("M1", "DnT", 0, m1_ok, META)
        pool.wait_ge(s_free, 1)
        pool.wait_ge(p_free, 1)
        for u in range(2):
            g.tensor_copy(kwin[:, u, 0:META], ak[:, P - META:P])
        windows(1, 1, True)
        mixer_steps(pool, mixer, last_scan)

        def merge_add(n, m, u):
            pool.wait_ge(evac[u], m + 1)
            wait(pool, m_l, n - N_MERGE)
            g.tensor_tensor(mt[:, 0, :], mt[:, 0, :], mt[:, 1, :], ALU.add).then_inc(mrg, 1)
        steps(pool, N_MERGE, N_OUT, merge_add, peel=2)

        def sum_squares(base, acc):
            pool.wait_ge(o_sq, base + 2)
            g.tensor_tensor(acc[:], sqt[:, 0, :], sqt[:, 1, :], ALU.add).then_inc(o_sum, 2)
            for k in range(2, KT - 1):
                g.drain()
                pool.wait_ge(o_sq, base + k + 1)
                g.tensor_tensor(acc[:], acc[:], sqt[:, k % 2, :], ALU.add).then_inc(o_sum, 1)
        sum_squares(0, acc)
        sum_squares(KT, acc)
        n0 = N_FF
        done = 0
        for sz in FF_GROUPS:
            def hidden_lo(j, m, u, done=done, n0=n0):
                pool.wait_ge(u_h, j + (done + 1))
                g.tensor_tensor(u_lo[:, bass.ds(j, 1), :].rearrange("p a c -> p (a c)"), up[:],
                                u_hi[:, bass.ds(j, 1), :].rearrange("p a c -> p (a c)").bitcast(F32),
                                ALU.subtract).then_inc(u_l, 1)
            steps(pool, 0, sz, hidden_lo)
            done += sz
            n0 += 2 * sz + KT
        sum_squares(2 * KT, rb)
        pool.wait_ge(x2_back, 16)
        for b in range(2):
            half_of = slice(b * HALF, (b + 1) * HALF)
            for k in range(POOL_ADDS):
                pool.wait_ge(o_sc, b * KT + k + 1)
                last = g.tensor_tensor(facc[:, k, half_of], facc[:, k, half_of], x2b[:, k, half_of], ALU.add)
            last.then_inc(x3_pool, 1)

    @block.scalar
    def _(act):
        a = nc.scalar

        def x_square(t, m, u):
            act.wait_ge(x_in[u], (m + 1) * 16)
            if not (isinstance(t, int) and t < 2):
                act.wait_ge(x_rs, t - 1)
            if isinstance(t, int) and t == 0:
                src, w = xmeta[:], META
            else:
                src, w = xin[:, bass.ds(t - 1, 1), :].rearrange("p a c -> p (a c)"), P
            settle(act)
            a.activation(xsq[0:w, u, :], src, ACT.Square, accum_out=small[0:w, u:u + 1]).then_inc(x_sum, 1)

        def x_high(t, u, c, w=P):
            act.wait_ge(x_wt, t + 1)
            settle(act)
            a.activation(h_hi[:, :, bass.ds(c, w)], xw[:, u, 0:KT * w].rearrange("p (k c) -> p k c", k=KT),
                         ACT.Copy).then_inc(x_hi, 1)

        def x_step(t, m, u):
            x_square(t, m, u)
            if isinstance(t, int):
                x_high(0, 0, 0, META)
            else:
                x_high(t - 2, u, (t - 3) * P + META)
        x_square(0, 0, 0)
        x_square(1, 0, 1)
        steps(act, 2, NT + 1, x_step, peel=1)
        split_hi(0, 0, 0)
        for t in (NT - 1, NT):
            x_high(t, t % 2, (t - 1) * P + META)
        act.wait_ge(wd_in, 16)
        a.activation(wd_hi[:], wd_raw[:], ACT.Copy).then_inc(wd_h, 1)

        def bias(base, j):
            return params[:, bass.ds(j + base, 1)]

        def kv_out(n, m, u):
            split_hi(*after(n, m, u))
            act.wait_ge(mm_done, n + 1)
            dst = (ak, av)[n]
            c = P - META
            a.activation(dst[:, c:c + 2 * THIRD].rearrange("p (b c) -> p b c", b=2), ps[:, 4 * u:4 * u + 2, 0:THIRD],
                         ACT.Identity, bias=params[:, GRP + n:GRP + n + 1])
            a.activation(dst[:, c + 2 * THIRD:], ps[:, 4 * u + 2, 0:LAST], ACT.Identity,
                         bias=params[:, GRP + n:GRP + n + 1]).then_inc(evac[u], 1)
        kv_out(0, 0, 0)
        kv_out(1, 0, 1)

        def q_out(n, m, u):
            split_hi(*after(n, m, u))
            act.wait_ge(mm_done, n + 1)
            settle(act)
            a.activation(aq[:, bass.ds(n - N_Q, 1), :].rearrange("p a c -> p (a c)"), banks(4 * u), ACT.Identity,
                         bias=bias(0, n - N_Q)).then_inc(evac[u], 1)
        steps(act, N_Q, N_DN, q_out)

        def silu_conv(j, parity, before):
            act.wait_ge(conv_ok, j + 1)
            wait(act, stored[parity], before * 16)
            if not isinstance(j, int) or 2 <= j < 10:
                act.wait_ge(qk_sq, j - 1)
            a.activation(cs[:, parity, :], cv[:, parity, :], ACT.Silu).then_inc(silu_ok, 1)

        def dn_out(n, m, u):
            split_hi(*after(n, m, u))
            j = n - N_DN
            if not (isinstance(n, int) and n == N_DN):
                silu_conv(j - 1, 1 - u, m - N_DN // 2 - (1 - u))
            act.wait_ge(mm_done, n + 1)
            b = bias(R_BIAS, n - N_DN + 6)
            settle(act)
            a.activation(rawc[:, u, 3:3 + 2 * THIRD].rearrange("p (b c) -> p b c", b=2),
                         ps[:, 4 * u:4 * u + 2, 0:THIRD], ACT.Identity, bias=b)
            a.activation(rawc[:, u, 3 + 2 * THIRD:], ps[:, 4 * u + 2, 0:LAST], ACT.Identity,
                         bias=b).then_inc(evac[u], 1)
        act.wait_ge(consts, 3)
        act.wait_ge(x_lo[0], 5)
        act.wait_ge(x_lo[1], 4)
        steps(act, N_DN, N_DN + 8, dn_out, peel=4)
        steps(act, N_DN + 8, N_DZ, dn_out, peel=4)

        def dz_out(n, m, u):
            split_hi(*after(n, m, u))
            if n == N_DZ:
                silu_conv(11, 1, 5)
            act.wait_ge(mm_done, n + 1)
            a.activation(gz[:, n - N_DZ, :], banks(4 * u), ACT.Silu, bias=bias(R_BIAS, n - N_DZ + 18)).then_inc(dz_ok, 1)
            a.drain().then_inc(evac[u], 1)
        act.wait_ge(dab_mm, 1)
        a.activation(dabT[:, 0:2 * THIRD].rearrange("p (b c) -> p b c", b=2), ps[0:8, 2:4, 0:THIRD], ACT.Copy)
        a.activation(dabT[:, 2 * THIRD:], ps[0:8, 7, P:P + LAST], ACT.Copy).then_inc(dab_cp, 1)
        for n in range(N_DZ, N_G):
            dz_out(n, n // 2, n % 2)

        def gate_out(n, m, u):
            split_hi(*after(n, m, u))
            act.wait_ge(mm_done, n + 1)
            act.wait_ge(stored[u], (m - N_G // 2 + 6) * 16)
            settle(act)
            a.activation(cs[:, u, 0:TOK], banks(4 * u), ACT.Sigmoid, bias=bias(R_BG, n - N_G)).then_inc(silu_ok, 1)
            a.drain().then_inc(evac[u], 1)
        act.wait_ge(bc_in, 64)
        ea = tiny[:, 48:52]
        a.activation(ea, alog[:], ACT.Exp)
        act.wait_ge(dab_add, 1)
        dx = dabx[:]
        a.activation(dabe[:, :, 4:8], dx[:, :, 4:8], ACT.Exp, scale=-1.0)
        a.activation(dabe[:, :, 0:4], dx[:, :, 0:4], ACT.Abs)
        a.drain()
        a.activation(dabe[:, :, 0:4], dabe[:, :, 0:4], ACT.Exp, scale=-1.0)
        a.drain()
        a.activation(dabe[:, :, 0:4], dabe[:, :, 0:4], ACT.Ln, bias=1.0).then_inc(dab_act, 1)
        for n in range(N_G, N_G + 2):
            gate_out(n, n // 2, n % 2)
        act.wait_ge(cols_ok, 1)
        a.activation(cols[:, :, 20:24], cols[:, :, 4:8], ACT.Exp)
        a.activation(cols[:, 1:, 8:12], cols[:, 1:, 8:12], ACT.Exp)
        a.activation(cols[0:META, 0, 8:12], cols[0:META, 0, 8:12], ACT.Exp)
        a.activation(cols[:, :, 24:28], cols[:, :, 24:28], ACT.Exp).then_inc(cols_ok, 2)
        steps(act, N_G + 2, N_MERGE, gate_out)

        def copy_of(op, c, L=P, dst=None):
            lane = lane_of(op)
            act.wait_ge(full[lane], filled(op, c))
            a.activation(buf[dst or op][0:L, :, 0:L], delta_bank(op)[0:L, :, 0:L], ACT.Copy).then_inc(free[lane], 1)

        def decays(c, L):
            act.wait_ge(a2_ok, c + 1)
            a.activation(buf["DL"][0:L, :, 0:L], buf["DL"][0:L, :, 0:L], ACT.Exp).then_inc(dl_ok, 1)
            act.wait_ge(a1_ok, c + 1)
            a.activation(buf["DT"][0:L, :, 0:L], buf["DT"][0:L, :, 0:L], ACT.Exp).then_inc(dt_ok, 1)

        def exps(c, i):
            act.wait_ge(nm_ok, (c - 1) * 4 + (i + 1))
            s = i % 2
            for h in range(2):
                a.activation(prob[:, s, h, :], prob[:, s, h, :], ACT.Exp, scale=HD ** -0.5,
                             bias=tiny[:, 56 + 4 * s + h:57 + 4 * s + h], accum_out=tiny[:, 64 + 4 * s + h:65 + 4 * s + h])
            a.activation(tiny[:, 66 + 4 * s:68 + 4 * s], tiny[:, 58 + 4 * s:60 + 4 * s], ACT.Exp).then_inc(ex_ok, 1)

        def probs_T(c, kv):
            act.wait_ge(p_full, (c - 1) * 2 + (kv + 2))
            a.activation(pt[0:META, 0, :], ps[0:META, APB, :], ACT.Copy)
            a.activation(pt[:, 1:3, :], ps[:, APB + 1:APB + 3, :], ACT.Copy).then_inc(p_free, 1)

        def att_out(c, kv):
            act.wait_ge(s_full, att_filled(f"O{kv}", c))
            settle(act)
            a.activation(ya[kv * HD:(kv + 1) * HD, :, bass.ds((c - 1) * P, P)],
                         ps[kv * HD:(kv + 1) * HD, AS, :].rearrange("p (j c) -> p j c", j=GRP),
                         ACT.Copy).then_inc(s_free, 1)

        decays(0, META)
        for op in ("DnT", "D2", "D2T", "D4", "D8"):
            copy_of(op, 0, META)
        act.wait_ge(full[lane_of("VN")], filled("VN", 0))
        a.activation(buf["vn"][0:META], delta_bank("VN")[0:META], ACT.Copy).then_inc(free[lane_of("VN")], 1)

        decays(1, P)

        def out_squares(c):
            act.wait_ge(free[lane_of("P2")], filled("P2", c))
            for h in range(DH):
                last = a.activation(buf["osq"][:, h, :], buf["op"][:, h, :], ACT.Square,
                                    accum_out=small[:, 48 + h:49 + h])
            last.then_inc(ored_ok, 1)

        def mixer(c, m, u, scan, front):
            for op in ("DnT", "D2", "D2T"):
                copy_of(op, c)
            if scan:
                copy_of("VN", c - 1, dst="vn")
            exps(c, 0)
            copy_of("D4", c)
            copy_of("D8", c)
            if scan:
                out_squares(c - 1)
            exps(c, 1)
            copy_of("B", c)
            copy_of("BT", c)
            copy_of("B2", c)
            if front:
                decays(c + 1, P)
            copy_of("Ninv", c)
            probs_T(c, 0)
            att_out(c, 0)
            copy_of("B4", c)
            exps(c, 2)
            exps(c, 3)
            copy_of("TT", c, dst=f"TT{u}")
            probs_T(c, 1)
            att_out(c, 1)

        def y_high(i):
            src, dst, k = Y_PARTS[i]
            a.activation(y_hi[:, k, dst], src[:, :, dst], ACT.Copy).then_inc(y_h, 1)

        def last_scan(c, u):
            copy_of("VN", c, dst="vn")
            act.wait_ge(s_free, att_filled("O1", NT))
            act.wait_ge(full[lane_of("P2")], filled("P2", c))
            y_high(0)
            out_squares(c)
            y_high(1)
            act.wait_ge(yd_ok, 1)
            y_high(2)
        mixer_steps(act, mixer, last_scan)

        def merge_hi(n, m, u):
            split_hi(*after(n, m, u))
            act.wait_ge(mrg, n - N_MERGE + 1)
            settle(act)
            a.activation(m_hi[:, bass.ds(n - N_MERGE, 1), :].rearrange("p a c -> p (a c)"), mt[:, 0, :],
                         ACT.Copy).then_inc(m_h, 1)
        steps(act, N_MERGE, N_OUT, merge_hi, peel=0)

        def square(src, idx, u):
            settle(act)
            wait(act, o_sum, idx - 1)
            a.activation(sqt[:, u, :], src, ACT.Square, scale=float(D) ** -0.5).then_inc(o_sq, 1)

        def root(r, cut=slice(0, TOK)):
            act.wait_ge(n_bc, r)
            a.activation(rb[:, cut], banks(6)[:, cut], ACT.Sqrt, bias=small[:, 5:6]).then_inc(n_add, 1)

        def out_evac(n, m, u):
            split_hi(*after(n, m, u))
            act.wait_ge(mm_done, n + 1)
            if isinstance(n, int) and n == N_OUT:
                act.wait_ge(m_l, KT)
            square(banks(4 * u), n - N_OUT, u)
            a.activation(oT[:, bass.ds(n - N_OUT, 1), :].rearrange("p a c -> p (a c)"), banks(4 * u),
                         ACT.Copy).then_inc(evac[u], 1)
        steps(act, N_OUT, N_FF, out_evac, peel=2)
        root(1)
        split_hi(*after(N_FF, N_FF // 2, 0))
        for k in range(KT):
            act.wait_ge(x2_ok, k + 1)
            a.activation(f_hi[:, k, :], oT[:, k, :], ACT.Copy, scale=params[:, R_FPRE + k:R_FPRE + k + 1]
                         ).then_inc(f_h, 1)
            square(oT[:, k, :], KT + k, k % 2)
        root(2)
        for n in (N_FF + 2, N_FF + 3):
            split_hi(n, n // 2, n % 2)
        n0, done = N_FF, 0
        for gi, sz in enumerate(FF_GROUPS):
            def gate(n, m, u, n0=n0, done=done):
                if not (isinstance(n, int) and n < N_FF + 3):
                    split_hi(*after(n, m, u))
                if u == 0:
                    act.wait_ge(gr_ok, m - n0 // 2 + (done + 1))
                    a.activation(sg[:], sg[:], ACT.Silu).then_inc(sg_ok, 1)
                else:
                    j = m - n0 // 2
                    act.wait_ge(up_ok, j + (done + 1))
                    settle(act)
                    a.activation(u_hi[:, bass.ds(j, 1), :].rearrange("p a c -> p (a c)"), up[:],
                                 ACT.Copy).then_inc(u_h, 1)
            steps(act, n0, n0 + 2 * sz, gate, peel=4)
            n1 = n0 + 2 * sz

            def only_split(n, m, u):
                split_hi(*after(n, m, u))

            def split_square(n, m, u, n1=n1):
                if not (isinstance(n, int) and n == n1 + KT - 1):
                    split_hi(*after(n, m, u))
                if not (isinstance(n, int) and n == n1):
                    k = n - n1 - 1
                    act.wait_ge(fa_ok, k + 1)
                    square(facc[:, bass.ds(k, 1), :].rearrange("p a c -> p (a c)"), k + 2 * KT, 1 - u)
            if gi < 2:
                steps(act, n1, n1 + KT, only_split)
            else:
                steps(act, n1, n1 + KT - 2, split_square, peel=2)
                for n in (n1 + KT - 2, n1 + KT - 1):
                    split_square(n, n // 2, n % 2)
                act.wait_ge(fa_ok, KT)
                square(facc[:, KT - 1, :], 3 * KT - 1, 1)
                for b in range(2):
                    root(3, slice(b * HALF, (b + 1) * HALF))
            done += sz
            n0 = n1 + KT
        for t in range(NT):
            if t >= NT // 2 and t % 2:
                continue
            act.wait_ge(ot_ps, t + 1)
            if t >= 4:
                act.wait_ge(out_st[t % 4], t // 4 * 16)
            a.activation(otile[:, t % 4, :], banks(2 * (t % 4)), ACT.Copy).then_inc(ot_ok[t % 4], 1)

    @block.vector
    def _(dve):
        v = nc.vector
        dve.wait_ge(par_tr, 1)
        v.tensor_copy(params[:, 0:NROWS], ps[:, 3, 0:NROWS]).then_inc(par_ok, 1)
        v.drain()

        def x_norm(t, u):
            dve.wait_ge(x_rs, t + 1)
            if isinstance(t, int) and t == 0:
                src, w = xmeta[:], META
            else:
                src, w = xin[:, bass.ds(t - 1, 1), :].rearrange("p a c -> p (a c)"), P
            v.tensor_scalar(xn[0:w, u, :], src, small[0:w, 6 + u:7 + u], None, ALU.mult).then_inc(x_nrm, 1)

        def x_weight(t, m, u, w=P):
            dve.wait_ge(x_tr, t + 1)
            if not (isinstance(t, int) and t < 2):
                dve.wait_ge(x_lo[u], m)
            v.tensor_tensor(xw[:, u, 0:KT * w].rearrange("p (k c) -> p k c", k=KT),
                            banks(4 + 2 * u)[:, 0:KT * w].rearrange("p (k c) -> p k c", k=KT),
                            params[:, R_PRE:R_PRE + KT].unsqueeze(2).to_broadcast([P, KT, w]),
                            ALU.mult).then_inc(x_wt, 1)

        def x_low(t, c):
            v.drain()
            dve.wait_ge(x_hi, t + 1)
            lo_part(v, t, 1, c)
        x_norm(0, 0)
        x_norm(1, 1)
        x_weight(0, 0, 0, META)
        x_norm(2, 0)
        x_weight(1, 0, 1)
        x_norm(3, 1)

        def x_step(t, m, u):
            x_weight(t - 2, m - 1, u)
            v.drain()
            x_norm(t, u)
            if u == 0:
                x_low(t - 3, (t - 4) * P + META)
        steps(dve, 4, NT, x_step)
        x_weight(NT - 2, NT // 2 - 1, 0)
        v.drain()
        x_norm(NT, 0)
        x_low(NT - 3, (NT - 4) * P + META)
        x_weight(NT - 1, NT // 2 - 1, 1)
        split_lo(0, 0, 0)
        x_weight(NT, NT // 2, 0)
        x_low(NT - 1, (NT - 2) * P + META)
        dve.wait_ge(wd_h, 1)
        v.tensor_tensor(wd_lo[:], wd_raw[:], wd_hi[:].bitcast(F32), ALU.subtract).then_inc(wd_l, 1)
        split_lo(1, 0, 1)
        steps(dve, 2, N_DN, lambda n, m, u: split_lo(n, m, u))
        split_lo(N_DN, N_DN // 2, 0)

        def conv(n, m, u):
            split_lo(*after(n, m, u))
            j = n - N_DN
            dve.wait_ge(evac[u], m + 1)
            if not (isinstance(n, int) and n < N_DN + 2):
                dve.wait_ge(silu_ok, j - 1)
            v.tensor_scalar(cv[:, u, :], rawc[:, u, 0:LW], params[:, bass.ds(j + R_CONV, 1)], None, ALU.mult)
            for k in range(1, 4):
                v.drain()
                last = v.scalar_tensor_tensor(cv[:, u, :], rawc[:, u, k:k + LW],
                                              params[:, bass.ds(j + (R_CONV + 12 * k), 1)], cv[:, u, :],
                                              ALU.mult, ALU.add)
            last.then_inc(conv_ok, 1)
        steps(dve, N_DN, N_DZ, conv, peel=2)
        split_lo(*after(N_DZ, N_DZ // 2, 0))
        dve.wait_ge(dab_tr, 1)
        dve.wait_ge(bc_in, 64)
        v.tensor_tensor(dab_b[:, 0:4], dab_b[:, 0:4], dtb[:], ALU.add)
        v.drain()
        v.tensor_tensor(dabx[:], ps[:, 3, 0:8 * (NT + 1)].rearrange("p (t c) -> p t c", c=8),
                        dab_b[:].unsqueeze(1).to_broadcast([P, NT + 1, 8]), ALU.add).then_inc(dab_add, 1)
        dve.wait_ge(qk_sum, 2 * DH)
        v.tensor_scalar(rr[:].rearrange("p t c -> p (t c)"), ps[:, 7, 0:8 * (NT + 1)], EPS, None,
                        ALU.add).then_inc(norm_ok, 1)
        for n in range(N_DZ + 1, N_G):
            split_lo(*after(n, n // 2, n % 2))

        dve.wait_ge(dab_act, 1)
        v.tensor_scalar(dabx[:, :, 0:4], dabx[:, :, 0:4], 0.0, None, ALU.max)
        v.tensor_scalar(dabe[:, :, 4:8], dabe[:, :, 4:8], 1.0, None, ALU.add)
        v.drain()
        v.tensor_tensor(dabx[:, :, 0:4], dabx[:, :, 0:4], dabe[:, :, 0:4], ALU.add)
        v.reciprocal(cols[:, :, 40:44], dabe[:, :, 4:8])
        v.tensor_scalar(tiny[:, 52:56], tiny[:, 48:52], -1.0, None, ALU.mult)
        v.drain()
        v.tensor_tensor(cols[:, :, 0:4], dabx[:, :, 0:4], tiny[:, 52:56].unsqueeze(1).to_broadcast([P, NT + 1, 4]),
                        ALU.mult).then_inc(dab_g, 1)
        for n in range(N_G, N_G + 2):
            split_lo(*after(n, n // 2, n % 2))
        dve.wait_ge(cum_mm, 1)
        c36 = [ps[:, 3, 128 * i:128 * i + 36].rearrange("p (t c) -> p t c", c=4) for i in range(2)]
        v.tensor_copy(cols[:, :, 4:8], c36[0])
        v.tensor_copy(cols[:, :, 24:28], c36[1])
        v.drain()
        v.tensor_tensor(cols[:, :, 8:12], cols[:, :, 24:28], cols[:, :, 4:8], ALU.subtract).then_inc(cols_ok, 1)
        steps(dve, N_G + 2, N_MERGE, lambda n, m, u: split_lo(*after(n, m, u)))

        dve.wait_ge(s_full, 1)
        v.tensor_copy(vtok[:, 1:, :], banks(AS).rearrange("p (t c) -> p t c", c=P)).then_inc(s_free, 1)
        dve.wait_ge(p_full, 1)
        v.tensor_copy(vmeta[:], ps[0:META, APB, 0:P]).then_inc(p_free, 1)


        def evac_of(op, c, make):
            lane = lane_of(op)
            dve.wait_ge(full[lane], filled(op, c))
            last = make(delta_bank(op))
            last.then_inc(free[lane], 1)

        def exponents(c, u, L=P):
            g_col = fcols[0:L, u, 4:8].unsqueeze(2).to_broadcast([L, DH, L])
            evac_of("gam", c, lambda b: v.tensor_tensor(buf["t1"][0:L, :, 0:L], b[0:L, :, 0:L], g_col, ALU.subtract))
            v.drain()
            v.scalar_tensor_tensor(buf["DL"][0:L, :, 0:L], buf["t1"][0:L, :, 0:L], -1.0,
                                   mask_low[0:L, 0:L].unsqueeze(1).to_broadcast([L, DH, L]),
                                   ALU.mult, ALU.add).then_inc(a2_ok, 1)
            v.tensor_tensor(buf["DT"][0:L, :, 0:L], buf["t1"][0:L, :, 0:L],
                            mask_up[0:L, 0:L].unsqueeze(1).to_broadcast([L, DH, L]), ALU.add).then_inc(a1_ok, 1)
            v.drain()

        def minus_a(c, u, L=P):
            lane = lane_of("KK")
            dve.wait_ge(dl_ok, c + 1)
            dve.wait_ge(full[lane], filled("KK", c))
            for h in range(DH):
                last = v.scalar_tensor_tensor(buf["t1"][0:L, h, 0:L], delta_bank("KK")[0:L, h, 0:L],
                                              fcols[0:L, u, 12 + h:13 + h], buf["DL"][0:L, h, 0:L],
                                              ALU.mult, ALU.mult)
            last.then_inc(free[lane], 1)

        def diagonal(c, L=P):
            v.tensor_tensor(buf["Dn"][0:L, :, 0:L], buf["t1"][0:L, :, 0:L],
                            blocks16[0:L, 0:L].unsqueeze(1).to_broadcast([L, DH, L]), ALU.mult).then_inc(dn_ok, 1)

        def att_T(c, u):
            dve.wait_ge(dt_ok, c + 1)
            evac_of("KQ", c, lambda b: v.tensor_tensor(buf[f"attT{u}"][:], b, buf["DT"][:], ALU.mult))

        def values(c, u, L=P):
            evac_of("vT", c, lambda b: v.tensor_tensor(
                buf[f"vb{u}"][0:L], b[0:L], fcols[0:L, u, 16:20].unsqueeze(2).to_broadcast([L, DH, P]), ALU.mult))

        def keys(c, u, L=P):
            evac_of("kT", c, lambda b: v.tensor_tensor(
                buf[f"kd{u}"][0:L], b[0:L], fcols[0:L, u, 8:12].unsqueeze(2).to_broadcast([L, DH, P]), ALU.mult))

        def copy_of(op, c, L=P):
            evac_of(op, c, lambda b: v.tensor_copy(buf[op][0:L, :, 0:L], b[0:L, :, 0:L]))

        def add_of(op, prev, c, L=P):
            evac_of(op, c, lambda b: v.tensor_tensor(buf[op][0:L, :, 0:L], b[0:L, :, 0:L], buf[prev][0:L, :, 0:L],
                                                     ALU.add))
            v.drain()

        exponents(0, 0, META)
        minus_a(0, 0, META)
        v.drain()
        diagonal(0, META)
        values(0, 0, META)
        keys(0, 0, META)
        copy_of("D4T", 0, META)
        dve.wait_ge(m1_ok, 1)
        add_of("M2", "M1", 0, META)
        add_of("M3", "M2", 0, META)
        add_of("M4", "M3", 0, META)
        evac_of("dS", 0, lambda b: v.tensor_copy(buf["S"][:], b))
        v.drain()
        dve.wait_ge(de_ok, 1)
        exponents(1, 1)
        minus_a(1, 1)
        v.drain()
        diagonal(1)
        att_T(1, 1)
        values(1, 1)
        keys(1, 1)

        def z_rows(c, u):
            lane = lane_of("KS")
            v.drain()
            dve.wait_ge(full[lane], filled("KS", c))
            for h in range(DH):
                last = v.scalar_tensor_tensor(buf["Z"][:, h, :], delta_bank("KS")[:, h, :], scols[:, u, 8 + h:9 + h],
                                              buf[f"vb{u}"][:, h, :], ALU.mult, ALU.add)
            last.then_inc(free[lane], 1)

        def state_out(c, u):
            evac_of("P1", c, lambda b: v.tensor_tensor(
                buf["o1"][:], b, scols[:, u, 0:4].unsqueeze(2).to_broadcast([P, DH, P]), ALU.mult))

        def state(c, u):
            lane = lane_of("dS")
            dve.wait_ge(full[lane], filled("dS", c))
            for h in range(DH):
                last = v.scalar_tensor_tensor(buf["S"][:, h, :], buf["S"][:, h, :], scols[:, u, 4 + h:5 + h],
                                              delta_bank("dS")[:, h, :], ALU.mult, ALU.add)
            last.then_inc(free[lane], 1)
            v.drain()

        def out_sum(c):
            evac_of("P2", c, lambda b: v.tensor_tensor(buf["op"][:], b, buf["o1"][:], ALU.add))

        def gated(c):
            evac_of("oT", c, lambda b: v.tensor_tensor(yd[:, :, bass.ds((c - 1) * P, P)], b,
                                                       gz[:, :, bass.ds((c - 1) * P, P)], ALU.mult))

        def scores(c, i):
            s = i % 2
            dve.wait_ge(s_full, att_filled(["S00", "S01", "S10", "S11"][i], c))
            dve.wait_ge(p_full, (c - 1) * 2 + (1 if i < 2 else 2))
            pb = prob[:, s]
            mask = band_now if isinstance(c, int) and c == 1 else band
            v.tensor_tensor(pb, ps[:, AS:AS + 2, 0:META + 2 * P],
                            mask[:].unsqueeze(1).to_broadcast([P, 2, META + 2 * P]), ALU.add).then_inc(s_free, 1)
            v.drain()
            v.tensor_reduce(tiny[:, 72 + 2 * s:74 + 2 * s], pb, axis=AX.X, op=ALU.max)
            v.drain()
            kh = 4 * (i // 2) + 2 * (i % 2)
            t0 = tiny[:, 72 + 2 * s:74 + 2 * s]
            v.scalar_tensor_tensor(t0, t0, HD ** -0.5, sink[:, kh:kh + 2], ALU.mult, ALU.max)
            v.drain()
            v.tensor_scalar(tiny[:, 56 + 4 * s:58 + 4 * s], t0, -1.0, None, ALU.mult)
            v.tensor_tensor(tiny[:, 58 + 4 * s:60 + 4 * s], sink[:, kh:kh + 2], t0, ALU.subtract).then_inc(nm_ok, 1)

        def denominators(c, i):
            s = i % 2
            dve.wait_ge(ex_ok, (c - 1) * 4 + (i + 1))
            v.tensor_tensor(tiny[:, 76 + 2 * s:78 + 2 * s], tiny[:, 64 + 4 * s:66 + 4 * s],
                            tiny[:, 66 + 4 * s:68 + 4 * s], ALU.add)
            v.drain()
            v.reciprocal(small[:, 56 + 2 * s:58 + 2 * s], tiny[:, 76 + 2 * s:78 + 2 * s]).then_inc(rec_ok, 1)

        def mixer(c, m, u, scan, front):
            w = 1 - u
            if scan:
                z_rows(c - 1, w)
                state_out(c - 1, w)
            scores(c, 0)
            copy_of("D4T", c)
            denominators(c, 0)
            dve.wait_ge(m1_ok, c + 1)
            add_of("M2", "M1", c)
            if scan:
                state(c - 1, w)
                out_sum(c - 1)
            add_of("M3", "M2", c)
            scores(c, 1)
            add_of("M4", "M3", c)
            denominators(c, 1)
            if front:
                exponents(c + 1, w)
            copy_of("B2T", c)
            scores(c, 2)
            dve.wait_ge(w1_ok, c)
            add_of("W2", "W1", c)
            if scan:
                gated(c - 1)
            if front:
                minus_a(c + 1, w)
            if front:
                att_T(c + 1, w)
            scores(c, 3)
            add_of("W3", "W2", c)
            if front:
                diagonal(c + 1)
            if front:
                values(c + 1, w)
            denominators(c, 2)
            if front:
                keys(c + 1, w)
            denominators(c, 3)

        def y_low(i):
            src, dst, k = Y_PARTS[i]
            dve.wait_ge(y_h, i + 1)
            v.tensor_tensor(y_lo[:, k, dst], src[:, :, dst], y_hi[:, k, dst].bitcast(F32),
                            ALU.subtract).then_inc(y_l, 1)

        def last_scan(c, u):
            z_rows(c, u)
            state_out(c, u)
            v.drain()
            out_sum(c)
            for i in range(3):
                if i == 2:
                    gated(c)
                    v.drain().then_inc(yd_ok, 1)
                y_low(i)
        dve.wait_ge(gz_ok, 1)
        mixer_steps(dve, mixer, last_scan)

        def merge_mul(n, m, u):
            split_lo(*after(n, m, u))
            v.drain()
            dve.wait_ge(mm_done, n + 1)
            dve.wait_ge(gate_in[u], (m - N_MERGE // 2 + 1) * 32)
            v.tensor_tensor(mt[:, 0, :], banks(4 * u), gin[:, u, 0, :], ALU.mult)
            v.tensor_tensor(mt[:, 1, :], banks(4 * u + 2), gin[:, u, 1, :], ALU.mult).then_inc(evac[u], 1)
            dve.wait_ge(m_h, n - N_MERGE + 1)
            v.tensor_tensor(m_lo[:, bass.ds(n - N_MERGE, 1), :].rearrange("p a c -> p (a c)"), mt[:, 0, :],
                            m_hi[:, bass.ds(n - N_MERGE, 1), :].rearrange("p a c -> p (a c)").bitcast(F32),
                            ALU.subtract).then_inc(m_l, 1)
        steps(dve, N_MERGE, N_OUT, merge_mul)
        steps(dve, N_OUT, N_FF, lambda n, m, u: split_lo(*after(n, m, u)))

        def rms(r):
            dve.wait_ge(n_add, r)
            v.reciprocal(rb[:], rb[:]).then_inc(n_rb, 1)
            v.drain()
        rms(1)

        def f_low(k):
            dve.wait_ge(f_h, k + 1)
            v.scalar_tensor_tensor(f_lo[:, k, :], oT[:, k, :], params[:, R_FPRE + k:R_FPRE + k + 1],
                                   f_hi[:, k, :].bitcast(F32), ALU.mult, ALU.subtract).then_inc(f_l, 1)

        def weighted(k):
            v.scalar_tensor_tensor(oT[:, k, :], oT[:, k, :], params[:, R_POST + k:R_POST + k + 1], rb[:],
                                   ALU.mult, ALU.mult)
        split_lo(*after(N_FF, N_FF // 2, 0))
        weighted(0)
        for k in range(KT):
            v.drain()
            dve.wait_ge(xt_ps, k + 1)
            v.tensor_tensor(oT[:, k, :], oT[:, k, :], banks(2), ALU.add).then_inc(x2_ok, 1)
            if k + 1 < KT:
                weighted(k + 1)
            v.drain()
            f_low(k)
        dve.wait_ge(n_bc, 2)
        for u, dst in enumerate((sg, up)):
            dve.wait_ge(mm_done, N_FF + 1 + u)
            v.tensor_copy(dst[:], banks(4 * u)).then_inc(evac[u], 1)
        for n in (N_FF + 2, N_FF + 3):
            split_lo(n, n // 2, n % 2)
        rms(2)
        v.tensor_tensor(sg[:], sg[:], rb[:], ALU.mult).then_inc(gr_ok, 1)
        v.tensor_tensor(up[:], up[:], rb[:], ALU.mult)
        v.drain()
        dve.wait_ge(sg_ok, 1)
        v.tensor_tensor(up[:], up[:], sg[:], ALU.mult).then_inc(up_ok, 1)
        n0, done = N_FF, 0
        for gi, sz in enumerate(FF_GROUPS):
            def prod(n, m, u, n0=n0, done=done):
                if isinstance(n, int) and n < N_FF + 2:
                    return
                if not (isinstance(n, int) and n == N_FF + 2):
                    split_lo(*after(n, m, u))
                v.drain()
                j = m - n0 // 2
                dve.wait_ge(mm_done, n + 1)
                if u == 0:
                    v.tensor_tensor(sg[:], banks(0), rb[:], ALU.mult).then_inc(gr_ok, 1)
                    v.drain().then_inc(evac[0], 1)
                else:
                    wait(dve, u_l, j + done)
                    v.tensor_tensor(up[:], banks(4), rb[:], ALU.mult).then_inc(evac[1], 1)
                    v.drain()
                    dve.wait_ge(sg_ok, j + (done + 1))
                    v.tensor_tensor(up[:], up[:], sg[:], ALU.mult).then_inc(up_ok, 1)
            steps(dve, n0, n0 + 2 * sz, prod, peel=4)
            n1 = n0 + 2 * sz

            def down(n, m, u, n1=n1, gi=gi, split=True):
                if split:
                    split_lo(*after(n, m, u))
                dve.wait_ge(mm_done, n + 1)
                dst = facc[:, bass.ds(n - n1, 1), :].rearrange("p a c -> p (a c)")
                if gi == 0:
                    if isinstance(n, int) and n == n1:
                        dve.wait_ge(x2_st, 16)
                    last = v.tensor_copy(dst, banks(4 * u))
                else:
                    last = v.tensor_tensor(dst, dst, banks(4 * u), ALU.add)
                last.then_inc(evac[u], 1)
                if gi == 2:
                    v.drain().then_inc(fa_ok, 1)
            if gi == 0:
                steps(dve, n1, n1 + KT, down, peel=2)
            elif gi == 1:
                v.drain()
                steps(dve, n1, n1 + KT, down)
            else:
                v.drain()
                steps(dve, n1, n1 + KT - 2, down)
                down(n1 + KT - 2, (n1 + KT - 2) // 2, 0)
                down(n1 + KT - 1, (n1 + KT - 1) // 2, 1, split=False)
            done += sz
            n0 = n1 + KT
        dve.wait_ge(x2_back, 16)
        for b in range(2):
            half_of = slice(b * HALF, (b + 1) * HALF)
            dve.wait_ge(n_add, 3 + b)
            v.reciprocal(rb[:, half_of], rb[:, half_of])
            v.drain()
            for k in range(KT):
                v.scalar_tensor_tensor(facc[:, k, half_of], facc[:, k, half_of],
                                       params[:, R_FPOST + k:R_FPOST + k + 1], rb[:, half_of],
                                       ALU.mult, ALU.mult).then_inc(o_sc, 1)
            v.drain()
            for k in range(POOL_ADDS, KT):
                last = v.tensor_tensor(facc[:, k, half_of], facc[:, k, half_of], x2b[:, k, half_of], ALU.add)
            last.then_inc(x3_ok, 1)
        for t in range(NT // 2 + 1, NT, 2):
            dve.wait_ge(ot_ps, t + 1)
            dve.wait_ge(out_st[t % 4], 16)
            v.tensor_copy(otile[:, t % 4, :], banks(2 * (t % 4))).then_inc(ot_ok[t % 4], 1)

    @block.tensor
    def _(pe):
        pe.wait_ge(consts, 1)
        pe.wait_ge(par_in, 160)
        TR(ps[:, 3, 0:NROWS], prow[0:NROWS, :], ident[0:NROWS, 0:NROWS]).then_inc(par_tr, 1)

        def x_tile(t, m, u, w=P):
            pe.wait_ge(x_nrm, t + 1)
            if not (isinstance(t, int) and t < 2):
                pe.wait_ge(x_wt, t - 1)
            for k in range(KT):
                last = TR(banks(4 + 2 * u)[:, k * w:(k + 1) * w], xn[0:w, u, k * P:(k + 1) * P], ident[0:w, 0:w])
            last.then_inc(x_tr, 1)
        x_tile(0, 0, 0, META)
        steps(pe, 1, NT + 1, x_tile, peel=2)

        def columns_there(c):
            t = -(-(c - META) // P)
            pe.wait_ge(x_lo[0], t // 2 + 1)
            pe.wait_ge(x_lo[1], (t + 1) // 2)
        for n in range(2):
            dense(n, 0, n, h_hi, h_lo, META, meta_cols=True,
                  arrive_group=columns_there if n == 0 else None).then_inc(mm_done, 1)
        steps(pe, N_Q, N_DN, lambda n, m, u: dense(n, m, u, h_hi, h_lo, META).then_inc(mm_done, 1))

        def conv_in_mm(n, m, u):
            dense(n, m, u, h_hi, h_lo, META, meta_cols=True).then_inc(mm_done, 1)

        def with_sums(n, m, u):
            conv_in_mm(n, m, u)
            j = n - N_DN - 2
            pe.wait_ge(qk_sq, j + 1)
            for t in range(NT + 1):
                c = max(0, META + (t - 1) * P)
                last = MM(ps[:, 7, bass.ds(j + 8 * t, 1)], sqc[:, u, c:c + P], ones[:, 0:1], start=True, stop=True)
            last.then_inc(qk_sum, 1)
        steps(pe, N_DN, N_DN + 2, conv_in_mm)
        steps(pe, N_DN + 2, N_DN + 10, with_sums)
        steps(pe, N_DN + 10, N_DZ, conv_in_mm)
        pe.wait_ge(wd_l, 1)
        pe.wait_ge(evac[0], N_DZ // 2)
        for out_cols, c, w in ((ps[0:8, 2, 0:THIRD], 0, THIRD), (ps[0:8, 3, 0:THIRD], THIRD, THIRD),
                               (ps[0:8, 7, P:P + LAST], 2 * THIRD, LAST)):
            for k in range(KT):
                for i, (a, mv) in enumerate(((wd_hi, h_hi), (wd_hi, h_lo), (wd_lo, h_hi))):
                    last = MM(out_cols, a[:, k, :], mv[:, k, c:c + w],
                              start=(k == 0 and i == 0), stop=(k == KT - 1 and i == 2))
        last.then_inc(dab_mm, 1)
        plain = lambda n, m, u: dense(n, m, u, h_hi, h_lo, META).then_inc(mm_done, 1)
        plain(N_DZ, N_DZ // 2, 0)
        pe.wait_ge(dab_cp, 1)
        for t in range(NT + 1):
            c = max(0, META + (t - 1) * P)
            last = TR(ps[:, 3, 8 * t:8 * t + 8], dabT[:, c:c + P], ident[0:8, 0:8])
        last.then_inc(dab_tr, 1)
        for n in range(N_DZ + 1, N_G + 2):
            plain(n, n // 2, n % 2)
        pe.wait_ge(consts, 2)
        pe.wait_ge(dab_g, 1)
        g_all = cols[:, :, 0:4]
        MM(ps[:, 3, 0:36].rearrange('p (t c) -> p t c', c=4), upper[:], g_all, start=True, stop=True)
        MM(ps[:, 3, 128 + 4:128 + 36].rearrange('p (t c) -> p t c', c=4), ones[:], cols[:, 1:, 0:4], start=True, stop=True)
        MM(ps[:, 3, 128:128 + 4], ones[0:META, :], cols[0:META, 0, 0:4], start=True, stop=True).then_inc(cum_mm, 1)
        steps(pe, N_G + 2, N_MERGE, plain)
        for u in range(2):
            pe.wait_ge(evac[u], N_MERGE // 2)
        for t in range(NT):
            last = TR(banks(AS)[:, t * P:(t + 1) * P], av[:, P + t * P:2 * P + t * P], ident[:])
        last.then_inc(s_full, 1)
        TR(ps[0:META, APB, 0:P], av[:, P - META:P], ident[:]).then_inc(p_full, 1)

        def fill(op, c, L, make, *waits):
            lane = lane_of(op)
            pe.wait_ge(free[lane], filled(op, c) - 1) if not (isinstance(c, int) and filled(op, c) == 1) else None
            for s, value in waits:
                if s is not free[lane]:
                    pe.wait_ge(s, value)
            for h in range(DH):
                last = make(h)
            last.then_inc(full[lane], 1)

        def ready(op, c):
            return free[lane_of(op)], filled(op, c)

        def own(op, c, u, L=P, *waits):
            q = lambda t: qkv[:, u, t, 0:L]
            X = lambda k, h: buf[k][0:L, h, 0:L]
            bank = lambda h: delta_bank(op)[0:L, h, 0:L]
            eye = ident[0:L, 0:L]
            pair = dict(D2=("DnT", "Dn"), D2T=("Dn", "DnT"), D4=("D2T", "D2"), D4T=("D2", "D2T"), M2=("D2", "M1"),
                        D8=("D4T", "D4"), M3=("D4", "M2"), M4=("D8", "M3"), B=("M4", "En"), BT=("En", "M4"),
                        B2=("BT", "B"), B2T=("B", "BT"), W2=("B2", "W1"), B4=("B2T", "B2"), W3=("B4", "W2"),
                        TT=("Ninv", "W3"))
            make = {"gam": lambda h: MM(bank(h), fcols[0:L, u, h:h + 1].to_broadcast([L, L]), upper[0:L, 0:L],
                                        start=True, stop=True),
                    "KK": lambda h: MM(bank(h), q(4 + h), q(4 + h), start=True, stop=True),
                    "KQ": lambda h: MM(bank(h), q(4 + h), q(h), start=True, stop=True),
                    "vT": lambda h: TR(delta_bank("vT")[0:L, h, :], q(8 + h), ident[:]),
                    "kT": lambda h: TR(delta_bank("kT")[0:L, h, :], q(4 + h), ident[:]),
                    "DnT": lambda h: TR(bank(h), X("Dn", h), eye),
                    "Ninv": lambda h: TR(bank(h), X("M4", h), eye)}
            if op in pair:
                lhsT, rhs = pair[op]
                fill(op, c, L, lambda h: MM(bank(h), X(lhsT, h), X(rhs, h), start=True, stop=True), *waits)
            else:
                fill(op, c, L, make[op], *waits)

        def scan_of(op, c, u, *waits):
            q = lambda t: qkv[:, u, t, :]
            X = lambda k, h: buf[k][:, h, :]
            pair = dict(KS=lambda h: (q(4 + h), X("S", h)), VN=lambda h: (X(f"TT{u}", h), X("Z", h)),
                        dS=lambda h: (X(f"kd{u}", h), X("vn", h)), P1=lambda h: (q(h), X("S", h)),
                        P2=lambda h: (X(f"attT{u}", h), X("vn", h)))
            if op == "oT":
                fill(op, c, P, lambda h: TR(delta_bank(op)[:, h, :], X("on", h), ident[:]), *waits)
            else:
                fill(op, c, P, lambda h: MM(delta_bank(op)[:, h, :], *pair[op](h), start=True, stop=True), *waits)

        def score(c, i, u):
            op = ["S00", "S01", "S10", "S11"][i]
            kv, j0 = i // 2, 2 * (i % 2)
            pe.wait_ge(s_free, att_filled(op, c) - 1)
            if i == 0:
                pe.wait_ge(win_ok, c)
            r = slice(kv * HD, (kv + 1) * HD)
            for j in range(2):
                last = MM(ps[:, AS + j, 0:META + 2 * P], qblk[r, u, j0 + j, :], kwin[r, u, :], start=True, stop=True)
            last.then_inc(s_full, 1)

        def prob_T(c, i):
            kv, j0 = i // 2, 2 * (i % 2)
            if i % 2 == 0:
                pe.wait_ge(p_free, (c - 1) * 2 + (kv + 1))
            pe.wait_ge(pr_ok, (c - 1) * 4 + (i + 1))
            for j in range(2):
                o = slice((j0 + j) * P, (j0 + j + 1) * P)
                TR(ps[0:META, APB, o], prob[:, i % 2, j, 0:META], ident[:])
                for b in range(2):
                    last = TR(ps[:, APB + 1 + b, o], prob[:, i % 2, j, META + b * P:META + (b + 1) * P], ident[:])
            if i % 2:
                last.then_inc(p_full, 1)

        def att_out(c, kv, u):
            op = f"O{kv}"
            pe.wait_ge(s_free, att_filled(op, c) - 1)
            pe.wait_ge(p_free, (c - 1) * 2 + (kv + 2))
            r = slice(kv * HD, (kv + 1) * HD)
            MM(ps[r, AS, :], vmeta[:, r], pt[0:META, 0, :], start=True, stop=False)
            MM(ps[r, AS, :], vwin[u][:, 0, r], pt[:, 1, :], start=False, stop=False)
            MM(ps[r, AS, :], vwin[u][:, 1, r], pt[:, 2, :], start=False, stop=True).then_inc(s_full, 1)

        pe.wait_ge(col_ok, 1)
        pe.wait_ge(qkv_in[0], 16)
        for op in ("gam", "KK", "vT", "kT"):
            own(op, 0, 0, META)
        own("DnT", 0, 0, META, (dn_ok, 1))
        own("D2", 0, 0, META, ready("DnT", 0))
        own("D2T", 0, 0, META)
        own("D4", 0, 0, META, ready("D2", 0), ready("D2T", 0))
        own("D4T", 0, 0, META)
        own("M2", 0, 0, META, (m1_ok, 1))
        own("D8", 0, 0, META, ready("D4", 0), ready("D4T", 0))
        own("M3", 0, 0, META, ready("M2", 0))
        own("M4", 0, 0, META, ready("D8", 0), ready("M3", 0))
        fill("VN", 0, META, lambda h: MM(delta_bank("VN")[0:META, h, :], buf["M4"][0:META, h, 0:META],
                                         buf["vb0"][0:META, h, :], start=True, stop=True), ready("M4", 0))
        fill("dS", 0, META, lambda h: MM(delta_bank("dS")[:, h, :], buf["kd0"][0:META, h, :],
                                         buf["vn"][0:META, h, :], start=True, stop=True), ready("VN", 0))
        pe.wait_ge(col_ok, 2)
        pe.wait_ge(qkv_in[1], 16)
        for op in ("gam", "KK", "KQ", "vT", "kT"):
            own(op, 1, 1)

        def mixer(c, m, u, scan, front):
            w = 1 - u
            if scan:
                scan_of("KS", c - 1, w, ready("TT", c - 1))
                scan_of("P1", c - 1, w)
            own("DnT", c, u, P, (dn_ok, c + 1))
            score(c, 0, u)
            own("D2", c, u, P, ready("DnT", c))
            own("D2T", c, u)
            if scan:
                scan_of("VN", c - 1, w, ready("KS", c - 1))
            own("D4", c, u, P, ready("D2", c), ready("D2T", c))
            own("D4T", c, u)
            own("M2", c, u, P, (m1_ok, c + 1))
            if scan:
                scan_of("dS", c - 1, w, ready("VN", c - 1))
            own("D8", c, u, P, ready("D4", c), ready("D4T", c))
            if scan:
                scan_of("P2", c - 1, w)
            own("M3", c, u, P, ready("M2", c))
            score(c, 1, u)
            own("M4", c, u, P, ready("D8", c), ready("M3", c))
            prob_T(c, 0)
            own("B", c, u, P, ready("M4", c), (de_ok, c + 1))
            own("BT", c, u)
            if front:
                own("gam", c + 1, w, P, (col_ok, c + 2))
            own("B2", c, u, P, ready("B", c), ready("BT", c))
            own("B2T", c, u)
            own("Ninv", c, u)
            prob_T(c, 1)
            score(c, 2, u)
            own("W2", c, u, P, ready("B2", c), (w1_ok, c))
            if scan:
                scan_of("oT", c - 1, w, (on_ok, c - 1))
            att_out(c, 0, u)
            if front:
                own("KK", c + 1, w, P, (qkv_in[w], (m + u + 1) * 16))
            own("B4", c, u, P, ready("B2T", c))
            if front:
                own("KQ", c + 1, w)
            score(c, 3, u)
            own("W3", c, u, P, ready("B4", c), ready("W2", c))
            if front:
                own("vT", c + 1, w)
            own("TT", c, u, P, ready("Ninv", c), ready("W3", c))
            prob_T(c, 2)
            if front:
                own("kT", c + 1, w)
            prob_T(c, 3)
            att_out(c, 1, u)

        def last_scan(c, u):
            scan_of("KS", c, u, ready("TT", c))
            scan_of("P1", c, u)
            scan_of("VN", c, u, ready("KS", c))
            scan_of("P2", c, u, ready("VN", c))
            pe.wait_ge(s_free, att_filled("O1", NT))
            pe.wait_ge(w_lo, N_MERGE + 1)
            pe.wait_ge(y_l, 1)
            dense(N_MERGE, N_MERGE // 2, 0, y_hi, y_lo, 0, ks=range(0, 4), bank=0)
            scan_of("oT", c, u, (on_ok, c))
        mixer_steps(pe, mixer, last_scan)

        pe.wait_ge(y_l, 3)

        def merge(n, m, u):
            wait(pe, w_lo, n + 1)
            wait(pe, evac[u], m)
            if not (isinstance(n, int) and n == N_MERGE):
                dense(n, m, u, y_hi, y_lo, 0, ks=range(0, 4), bank=0)
            dense(n, m, u, y_hi, y_lo, 0, ks=range(4, 8), bank=2).then_inc(mm_done, 1)
        steps(pe, N_MERGE, N_OUT, merge, peel=2)

        def rms(r):
            for src, s, value in ((acc if r < 3 else rb, o_sum, r * KT - 1), (sqt[:, 1, :], o_sq, r * KT)):
                pe.wait_ge(s, value)
                for b in range(2):
                    last = MM(ps[:, 6 + b, :], ones[:], src[:, b * HALF:(b + 1) * HALF],
                              start=(s is o_sum), stop=(s is o_sq))
            last.then_inc(n_bc, 1)
            pe.drain().then_inc(o_sum, 1)

        def out_tile(n, m, u):
            first = isinstance(n, int) and n == N_OUT
            arrive = (lambda k: pe.wait_ge(m_l, k + 1)) if first else None
            dense(n, m, u, m_hi, m_lo, 0, arrive=arrive).then_inc(mm_done, 1)
        steps(pe, N_OUT, N_FF, out_tile, peel=2)
        rms(1)

        def residual(k):
            if k:
                pe.wait_ge(x2_ok, k)
            for t in range(NT):
                last = TR(banks(2)[:, t * P:(t + 1) * P], xtok[:, t, k * P:(k + 1) * P], ident[:])
            last.then_inc(xt_ps, 1)
        pe.wait_ge(xt_in, 16)
        residual(0)
        for u in range(2):
            pe.wait_ge(evac[u], N_FF // 2)
        for u in range(2):
            pe.wait_ge(w_lo, N_FF + 1 + u)
        pe.wait_ge(n_rb, 1)
        for k in range(KT):
            if k + 1 < KT:
                residual(k + 1)
            if k == KT - 1:
                rms(2)
            pe.wait_ge(f_l, k + 1)
            for u in range(2):
                for b in range(2):
                    for i, (a, mv) in enumerate(((whi, f_hi), (whi, f_lo), (wlo, f_hi))):
                        last = MM(ps[:, 4 * u + b, :], a[:, u, k, :], mv[:, k, b * HALF:(b + 1) * HALF],
                                  start=(k == 0 and i == 0), stop=(k == KT - 1 and i == 2))
                if k == KT - 1:
                    last.then_inc(mm_done, 1)
        n0, done = N_FF, 0
        for gi, sz in enumerate(FF_GROUPS):
            steps(pe, n0 + 2 * (gi == 0), n0 + 2 * sz,
                  lambda n, m, u: dense(n, m, u, f_hi, f_lo, 0).then_inc(mm_done, 1))
            n1 = n0 + 2 * sz

            def down(n, m, u, n1=n1, gi=gi, sz=sz, done=done):
                arrive = (lambda k: pe.wait_ge(u_l, done + k + 1)) if isinstance(n, int) and n == n1 else None
                dense(n, m, u, u_hi, u_lo, 0, nk=sz, arrive=arrive).then_inc(mm_done, 1)
            steps(pe, n1, n1 + KT, down, peel=2)
            done += sz
            n0 = n1 + KT
        rms(3)
        for t in range(NT):
            if t % (NT // 2) == 0:
                pe.wait_ge(x3_ok, 1 + t // (NT // 2))
                pe.wait_ge(x3_pool, 1 + t // (NT // 2))
            if t == 3:
                pe.wait_ge(n_add, 4)
            if t >= 4:
                pe.wait_ge(ot_ok[t % 4], 1)
            for k in range(KT):
                last = TR(banks(2 * (t % 4))[:, k * P:(k + 1) * P], facc[:, k, t * P:(t + 1) * P], ident[:])
            last.then_inc(ot_ps, 1)

    block.__exit__(None, None, None)


_INS = ["x", "meta_tokens", "w_in", "b_in", "conv_w", "a_log", "dt_bias", "dn_norm_w", "att_sinks", "w_att_out",
        "w_dn_out", "w_out", "norm_mix_pre", "norm_mix_post", "norm_ffn_pre", "norm_ffn_post", "w_ffn_in", "w_ffn_out"]


def kernel(**inputs):
    import numpy as _np
    import concourse.bacc as _bacc
    from concourse import mybir as _mybir
    from concourse.bass_utils import run_bass_kernel_spmd as _run

    nc = _bacc.Bacc("TRN2", target_bir_lowering=False, num_devices=1)
    arrays, args = {}, []
    for name in _INS:
        a = _np.ascontiguousarray(inputs[name])
        if name != "meta_tokens":
            a = a[0]
        arrays[f"in_{name}"] = a
        args.append(nc.dram_tensor(f"in_{name}", a.shape, _mybir.dt.from_np(a.dtype), kind="ExternalInput").ap())
    result = nc.dram_tensor("out_0", (1, TOK, D), _mybir.dt.float32, kind="ExternalOutput").ap()
    build(nc, *args, result[0])
    r = _run(nc, [arrays], core_ids=[0])
    return r.results[0]["out_0"]
```
